# Optimizing a Trainium2 kernel written in Bass

```python
import math
import jax, jax.numpy as jnp
from jax import lax
import numpy as np

D_MODEL = 1024
BATCH = 1
SEQ = 512
DEPTH = 2

N_EVEN = (DEPTH + 1) // 2
N_ODD = DEPTH // 2
EPS = 1e-6
NEG = -1e30
BIG = 1e30

MLA_HEADS = 8
MLA_Q_RANK = 384
MLA_KV_RANK = 256
MLA_NOPE = 64
MLA_ROPE = 32
MLA_V = 64
ROPE_BASE = 10000.0
MLA_Q_BLOCK = 128

GDN_HEADS = 4
GDN_DK = 128
GDN_DV = 128
GDN_CONV = 4
GDN_CHUNK = 64

NSA_HEADS = 16
NSA_GROUPS = 4
NSA_HPG = NSA_HEADS // NSA_GROUPS
NSA_DIM = 64
CMP_BLOCK = 32
CMP_STRIDE = 16
CMP_HIDDEN = 256
SEL_BLOCK = 64
SEL_TOPN = 16
WINDOW = 512
NSA_Q_BLOCK = 64

FFN_HIDDEN = ((8 * D_MODEL + 3 * 256 - 1) // (3 * 256)) * 256

GDN_QK = GDN_HEADS * GDN_DK
GDN_VW = GDN_HEADS * GDN_DV
EVEN_SPLITS = (MLA_Q_RANK, MLA_KV_RANK, MLA_ROPE, GDN_QK, GDN_QK, GDN_VW, GDN_VW, GDN_HEADS, GDN_HEADS)
EVEN_IN = sum(EVEN_SPLITS)
EVEN_MIX = MLA_HEADS * MLA_V + GDN_VW
NSA_QW = NSA_HEADS * NSA_DIM
NSA_KVW = NSA_GROUPS * NSA_DIM
ODD_SPLITS = (NSA_QW,) + (NSA_KVW,) * 6 + (3 * NSA_HEADS,)
ODD_IN = sum(ODD_SPLITS)
ODD_MIX = NSA_QW

kernel_name = 'hybrid_mla_gdn_nsa_trunk'

def _split(z, sizes):
    cuts = np.cumsum(sizes)[:-1].tolist()
    return jnp.split(z, cuts, axis=-1)

def rmsnorm(x, g):
    xf = x.astype(jnp.float32)
    y = xf * lax.rsqrt(jnp.mean(xf * xf, axis=-1, keepdims=True) + EPS)
    return (y * g.astype(jnp.float32)).astype(x.dtype)

def l2norm(x):
    xf = x.astype(jnp.float32)
    return xf * lax.rsqrt(jnp.sum(xf * xf, axis=-1, keepdims=True) + EPS)

def alibi_slopes(n):
    return 2.0 ** (-8.0 * jnp.arange(1, n + 1, dtype=jnp.float32) / n)

def apply_rope(x, pos):
    half = x.shape[-1] // 2
    inv = ROPE_BASE ** (-jnp.arange(half, dtype=jnp.float32) / half)
    ang = pos.astype(jnp.float32)[:, None] * inv[None, :]
    cos = jnp.cos(ang)[None, :, None, :]
    sin = jnp.sin(ang)[None, :, None, :]
    xf = x.astype(jnp.float32)
    x1, x2 = xf[..., :half], xf[..., half:]
    return jnp.concatenate([x1 * cos - x2 * sin, x2 * cos + x1 * sin], axis=-1).astype(x.dtype)

def causal_attention_blocked(q, k, v, scale):
    B, S, H, DQ = q.shape
    DVh = v.shape[-1]
    nb = S // MLA_Q_BLOCK
    q_blocks = q.reshape(B, nb, MLA_Q_BLOCK, H, DQ).swapaxes(0, 1)
    kpos = jnp.arange(S)
    vf = v.astype(jnp.float32)

    def one(args):
        qi, i = args
        qpos = i * MLA_Q_BLOCK + jnp.arange(MLA_Q_BLOCK)
        s = jnp.einsum('bqhd,bkhd->bhqk', qi, k, preferred_element_type=jnp.float32) * scale
        s = jnp.where(kpos[None, :] <= qpos[:, None], s, NEG)
        p = jax.nn.softmax(s, axis=-1)
        return jnp.einsum('bhqk,bkhd->bqhd', p, vf)

    o = lax.map(one, (q_blocks, jnp.arange(nb)))
    return o.swapaxes(0, 1).reshape(B, S, H, DVh)

def mla_attention(c_q, c_kv, k_r, q_norm, kv_norm, w_uq, w_ukv, pos):
    B, S, _ = c_q.shape
    q = (rmsnorm(c_q, q_norm) @ w_uq).reshape(B, S, MLA_HEADS, MLA_NOPE + MLA_ROPE)
    kv = (rmsnorm(c_kv, kv_norm) @ w_ukv).reshape(B, S, MLA_HEADS, MLA_NOPE + MLA_V)
    q_rot = apply_rope(q[..., MLA_NOPE:], pos)
    k_rot = apply_rope(k_r[:, :, None, :], pos)
    q = jnp.concatenate([q[..., :MLA_NOPE], q_rot], axis=-1)
    k = jnp.concatenate([kv[..., :MLA_NOPE], jnp.broadcast_to(k_rot, (B, S, MLA_HEADS, MLA_ROPE))], axis=-1)
    v = kv[..., MLA_NOPE:]
    o = causal_attention_blocked(q, k, v, (MLA_NOPE + MLA_ROPE) ** -0.5)
    return o.reshape(B, S, MLA_HEADS * MLA_V).astype(c_q.dtype)

def causal_depthwise_conv(x, w):
    K, C = w.shape
    return lax.conv_general_dilated(x, w[:, None, :].astype(x.dtype), window_strides=(1,),
                                    padding=[(K - 1, 0)], dimension_numbers=('NWC', 'WIO', 'NWC'),
                                    feature_group_count=C)

def chunk_gated_delta_rule(q, k, v, beta, g):
    B, S, H, DK = q.shape
    DV = v.shape[-1]
    C = GDN_CHUNK
    N = S // C
    f32 = jnp.float32

    def chunks(t):
        t = t.astype(f32).reshape((B, N, C, H) + t.shape[3:])
        return jnp.moveaxis(t, 3, 2).swapaxes(0, 1)

    qc, kc, vc, bc, gc = [chunks(t) for t in (q, k, v, beta, g)]
    gc = jnp.cumsum(gc, axis=-1)
    lower = jnp.tril(jnp.ones((C, C), dtype=bool))
    strict = jnp.tril(jnp.ones((C, C), dtype=bool), -1)
    decay = jnp.exp(jnp.where(lower, gc[..., :, None] - gc[..., None, :], -jnp.inf))
    kb = kc * bc[..., None]
    a = jnp.where(strict, jnp.einsum('nbhid,nbhjd->nbhij', kb, kc) * decay, 0.0)
    eye = jnp.eye(C, dtype=f32)
    t_inv = lax.linalg.triangular_solve(a + eye, jnp.broadcast_to(eye, a.shape), left_side=True, lower=True)
    u = jnp.einsum('nbhij,nbhjd->nbhid', t_inv, vc * bc[..., None])
    w = jnp.einsum('nbhij,nbhjd->nbhid', t_inv, kb * jnp.exp(gc)[..., None])
    intra = jnp.einsum('nbhid,nbhjd->nbhij', qc, kc) * decay
    q_dec = qc * jnp.exp(gc)[..., None]
    k_dec = kc * jnp.exp(gc[..., -1:] - gc)[..., None]
    g_last = jnp.exp(gc[..., -1])

    def step(state, xs):
        u_i, w_i, qd_i, kd_i, a_i, gl_i = xs
        v_new = u_i - jnp.einsum('bhcd,bhde->bhce', w_i, state)
        o_i = jnp.einsum('bhcd,bhde->bhce', qd_i, state) + jnp.einsum('bhij,bhje->bhie', a_i, v_new)
        state = state * gl_i[..., None, None] + jnp.einsum('bhcd,bhce->bhde', kd_i, v_new)
        return state, o_i

    state0 = jnp.zeros((B, H, DK, DV), f32)
    _, o = lax.scan(step, state0, (u, w, q_dec, k_dec, intra, g_last))
    return o.swapaxes(0, 1).swapaxes(2, 3).reshape(B, S, H, DV)

def gated_deltanet(z_q, z_k, z_v, z_g, z_b, z_a, conv_w, a_log, dt_bias, out_norm):
    B, S, _ = z_q.shape
    f32 = jnp.float32
    qkv = jax.nn.silu(causal_depthwise_conv(jnp.concatenate([z_q, z_k, z_v], axis=-1), conv_w))
    q, k, v = _split(qkv, (GDN_QK, GDN_QK, GDN_VW))
    q = l2norm(q.reshape(B, S, GDN_HEADS, GDN_DK)) * (GDN_DK ** -0.5)
    k = l2norm(k.reshape(B, S, GDN_HEADS, GDN_DK))
    v = v.reshape(B, S, GDN_HEADS, GDN_DV)
    beta = jax.nn.sigmoid(z_b.astype(f32))
    g = -jnp.exp(a_log.astype(f32)) * jax.nn.softplus(z_a.astype(f32) + dt_bias.astype(f32))
    o = chunk_gated_delta_rule(q, k, v, beta, g)
    o = rmsnorm(o, out_norm) * jax.nn.silu(z_g.astype(f32).reshape(B, S, GDN_HEADS, GDN_DV))
    return o.reshape(B, S, GDN_VW).astype(z_q.dtype)

def compress_blocks(x, starts, pe, w1, w2):
    B, _, G, D = x.shape
    n = starts.shape[0]
    idx = starts[:, None] + jnp.arange(CMP_BLOCK)[None, :]
    blk = x[:, idx] + pe[None, None, :, None, :].astype(x.dtype)
    flat = blk.transpose(0, 1, 3, 2, 4).reshape(B, n, G, CMP_BLOCK * D)
    return jax.nn.gelu(flat @ w1) @ w2

def nsa_attention(z_q, z_kc, z_vc, z_ks, z_vs, z_kw, z_vw, z_g, pe_k, w1_k, w2_k, pe_v, w1_v, w2_v):
    B, S, _ = z_q.shape
    G, R, D = NSA_GROUPS, NSA_HPG, NSA_DIM
    f32 = jnp.float32
    Tq = NSA_Q_BLOCK
    q = z_q.reshape(B, S, G, R, D)
    kc, vc, ks, vs, kw, vw = [t.reshape(B, S, G, D) for t in (z_kc, z_vc, z_ks, z_vs, z_kw, z_vw)]
    gates = jax.nn.sigmoid(z_g.astype(f32)).reshape(B, S, G, R, 3)
    scale = D ** -0.5
    slopes = alibi_slopes(NSA_HEADS).reshape(G, R)

    n_cmp = (S - CMP_BLOCK) // CMP_STRIDE + 1
    cmp_start = jnp.arange(n_cmp) * CMP_STRIDE
    cmp_end = cmp_start + CMP_BLOCK - 1
    cmp_center = cmp_start.astype(f32) + 0.5 * (CMP_BLOCK - 1)
    k_cmp = compress_blocks(kc, cmp_start, pe_k, w1_k, w2_k)
    v_cmp = compress_blocks(vc, cmp_start, pe_v, w1_v, w2_v).astype(f32)

    n_sel = S // SEL_BLOCK
    top_n = min(SEL_TOPN, n_sel)
    sel_start = jnp.arange(n_sel) * SEL_BLOCK
    overlap = ((cmp_start[:, None] <= sel_start[None, :] + SEL_BLOCK - 1)
               & (cmp_end[:, None] >= sel_start[None, :])).astype(f32)
    ks_blk = ks.reshape(B, n_sel, SEL_BLOCK, G, D).transpose(0, 3, 1, 2, 4)
    vs_blk = vs.reshape(B, n_sel, SEL_BLOCK, G, D).transpose(0, 3, 1, 2, 4)
    gather = jax.vmap(jax.vmap(lambda blocks, idx: blocks[idx]))

    kw_pad = jnp.pad(kw, ((0, 0), (WINDOW, 0), (0, 0), (0, 0)))
    vw_pad = jnp.pad(vw, ((0, 0), (WINDOW, 0), (0, 0), (0, 0)))
    jsel = jnp.arange(n_sel)

    def one(i):
        t0 = i * Tq
        qi = lax.dynamic_slice_in_dim(q, t0, Tq, axis=1)
        gi = lax.dynamic_slice_in_dim(gates, t0, Tq, axis=1)
        qpos = t0 + jnp.arange(Tq)
        qpos_f = qpos.astype(f32)

        s = jnp.einsum('bqgrd,bngd->bgrqn', qi, k_cmp, preferred_element_type=f32) * scale
        s = s - slopes[:, :, None, None] * (qpos_f[:, None] - cmp_center[None, :])
        valid = cmp_end[None, :] <= qpos[:, None]
        p_cmp = jax.nn.softmax(jnp.where(valid, s, NEG), axis=-1) * jnp.any(valid, axis=-1)[:, None].astype(f32)
        o_cmp = jnp.einsum('bgrqn,bngd->bqgrd', p_cmp, v_cmp)

        imp = jnp.einsum('bgrqn,nj->bgqj', p_cmp, overlap)
        q_blk = qpos // SEL_BLOCK
        forced = (jsel[None, :] == 0) | (jsel[None, :] == q_blk[:, None]) | (jsel[None, :] == q_blk[:, None] - 1)
        causal_blk = jsel[None, :] <= q_blk[:, None]
        imp = jnp.where(forced, BIG, jnp.where(causal_blk, imp, NEG))
        _, sel = lax.top_k(imp, top_n)
        k_g = gather(ks_blk, sel)
        v_g = gather(vs_blk, sel).astype(f32)
        s_pos = sel[..., None] * SEL_BLOCK + jnp.arange(SEL_BLOCK)
        dist = (qpos[None, None, :, None, None] - s_pos).astype(f32)[:, :, None]
        s = jnp.einsum('bqgrd,bgqnsd->bgrqns', qi, k_g, preferred_element_type=f32) * scale
        s = jnp.where(dist >= 0, s - slopes[None, :, :, None, None, None] * dist, NEG)
        p = jax.nn.softmax(s.reshape(B, G, R, Tq, top_n * SEL_BLOCK), axis=-1).reshape(s.shape)
        o_sel = jnp.einsum('bgrqns,bgqnsd->bqgrd', p, v_g)

        k_win = lax.dynamic_slice_in_dim(kw_pad, t0, Tq + WINDOW, axis=1)
        v_win = lax.dynamic_slice_in_dim(vw_pad, t0, Tq + WINDOW, axis=1).astype(f32)
        kpos = t0 - WINDOW + jnp.arange(Tq + WINDOW)
        dw = qpos[:, None] - kpos[None, :]
        wvalid = (dw >= 0) & (dw < WINDOW) & (kpos[None, :] >= 0)
        s = jnp.einsum('bqgrd,bkgd->bgrqk', qi, k_win, preferred_element_type=f32) * scale
        s = s - slopes[:, :, None, None] * dw.astype(f32)
        p = jax.nn.softmax(jnp.where(wvalid, s, NEG), axis=-1)
        o_win = jnp.einsum('bgrqk,bkgd->bqgrd', p, v_win)

        o = gi[..., 0:1] * o_cmp + gi[..., 1:2] * o_sel + gi[..., 2:3] * o_win
        return o.reshape(B, Tq, G * R * D).astype(z_q.dtype)

    out = lax.map(one, jnp.arange(S // Tq))
    return out.swapaxes(0, 1).reshape(B, S, G * R * D)

def even_mixer(xn, w_in, q_norm, kv_norm, w_uq, w_ukv, conv_w, a_log, dt_bias, gdn_norm, w_out, pos):
    z = xn @ w_in
    c_q, c_kv, k_r, z_q, z_k, z_v, z_g, z_b, z_a = _split(z, EVEN_SPLITS)
    o_mla = mla_attention(c_q, c_kv, k_r, q_norm, kv_norm, w_uq, w_ukv, pos)
    o_gdn = gated_deltanet(z_q, z_k, z_v, z_g, z_b, z_a, conv_w, a_log, dt_bias, gdn_norm)
    return jnp.concatenate([o_mla, o_gdn], axis=-1) @ w_out

def odd_mixer(xn, w_in, pe_k, w1_k, w2_k, pe_v, w1_v, w2_v, w_out):
    z = xn @ w_in
    z_q, z_kc, z_vc, z_ks, z_vs, z_kw, z_vw, z_g = _split(z, ODD_SPLITS)
    o = nsa_attention(z_q, z_kc, z_vc, z_ks, z_vs, z_kw, z_vw, z_g, pe_k, w1_k, w2_k, pe_v, w1_v, w2_v)
    return o @ w_out

def swiglu(x, w_gate, w_up, w_down):
    return (jax.nn.silu(x @ w_gate) * (x @ w_up)) @ w_down

def setup_inputs(seed: int = 0) -> dict:
    key = jax.random.key(seed)
    keys = iter(jax.random.split(key, 32))
    f32 = jnp.float32
    NE, NO, D = N_EVEN, N_ODD, D_MODEL

    def dense(shape, fan_in):
        return jax.random.normal(next(keys), shape, f32) * (fan_in ** -0.5)

    def gain(shape):
        return 1.0 + 0.02 * jax.random.normal(next(keys), shape, f32)

    def small(shape):
        return 0.02 * jax.random.normal(next(keys), shape, f32)

    conv_ch = 2 * GDN_QK + GDN_VW
    a_init = jax.random.uniform(next(keys), (NE, GDN_HEADS), f32, 1.0, 16.0)
    dt = jnp.exp(jax.random.uniform(next(keys), (NE, GDN_HEADS), f32, math.log(1e-3), math.log(1e-1)))
    flat_cmp = CMP_BLOCK * NSA_DIM
    return {
        'x': jax.random.normal(next(keys), (BATCH, SEQ, D), f32),
        'ev_attn_norm': gain((NE, D)),
        'ev_w_in': dense((NE, D, EVEN_IN), D),
        'ev_q_norm': gain((NE, MLA_Q_RANK)),
        'ev_kv_norm': gain((NE, MLA_KV_RANK)),
        'ev_w_uq': dense((NE, MLA_Q_RANK, MLA_HEADS * (MLA_NOPE + MLA_ROPE)), MLA_Q_RANK),
        'ev_w_ukv': dense((NE, MLA_KV_RANK, MLA_HEADS * (MLA_NOPE + MLA_V)), MLA_KV_RANK),
        'ev_conv_w': dense((NE, GDN_CONV, conv_ch), GDN_CONV),
        'ev_a_log': jnp.log(a_init),
        'ev_dt_bias': dt + jnp.log(-jnp.expm1(-dt)),
        'ev_gdn_norm': gain((NE, GDN_DV)),
        'ev_w_out': dense((NE, EVEN_MIX, D), EVEN_MIX),
        'od_attn_norm': gain((NO, D)),
        'od_w_in': dense((NO, D, ODD_IN), D),
        'od_pe_k': small((NO, CMP_BLOCK, NSA_DIM)),
        'od_w1_k': dense((NO, flat_cmp, CMP_HIDDEN), flat_cmp),
        'od_w2_k': dense((NO, CMP_HIDDEN, NSA_DIM), CMP_HIDDEN),
        'od_pe_v': small((NO, CMP_BLOCK, NSA_DIM)),
        'od_w1_v': dense((NO, flat_cmp, CMP_HIDDEN), flat_cmp),
        'od_w2_v': dense((NO, CMP_HIDDEN, NSA_DIM), CMP_HIDDEN),
        'od_w_out': dense((NO, ODD_MIX, D), ODD_MIX),
        'ffn_norm': gain((DEPTH, D)),
        'ffn_w_gate': dense((DEPTH, D, FFN_HIDDEN), D),
        'ffn_w_up': dense((DEPTH, D, FFN_HIDDEN), D),
        'ffn_w_down': dense((DEPTH, FFN_HIDDEN, D), FFN_HIDDEN),
        'final_norm': gain((D,)),
    }

def reference(x, ev_attn_norm, ev_w_in, ev_q_norm, ev_kv_norm, ev_w_uq, ev_w_ukv, ev_conv_w,
              ev_a_log, ev_dt_bias, ev_gdn_norm, ev_w_out, od_attn_norm, od_w_in, od_pe_k, od_w1_k,
              od_w2_k, od_pe_v, od_w1_v, od_w2_v, od_w_out, ffn_norm, ffn_w_gate, ffn_w_up,
              ffn_w_down, final_norm):
    S = x.shape[1]
    pos = jnp.arange(S, dtype=jnp.int32)
    h = x
    for layer in range(DEPTH):
        i = layer // 2
        if layer % 2 == 0:
            mix = even_mixer(rmsnorm(h, ev_attn_norm[i]), ev_w_in[i], ev_q_norm[i], ev_kv_norm[i],
                             ev_w_uq[i], ev_w_ukv[i], ev_conv_w[i], ev_a_log[i], ev_dt_bias[i],
                             ev_gdn_norm[i], ev_w_out[i], pos)
        else:
            mix = odd_mixer(rmsnorm(h, od_attn_norm[i]), od_w_in[i], od_pe_k[i], od_w1_k[i], od_w2_k[i],
                            od_pe_v[i], od_w1_v[i], od_w2_v[i], od_w_out[i])
        h = h + mix.astype(h.dtype)
        h = h + swiglu(rmsnorm(h, ffn_norm[layer]), ffn_w_gate[layer], ffn_w_up[layer], ffn_w_down[layer]).astype(h.dtype)
    return rmsnorm(h, final_norm)


_drawn_inputs = setup_inputs


def setup_inputs(seed=0):
    import zlib

    import numpy as np

    out = dict(_drawn_inputs(seed))
    spreads = {}
    factors = {'ev_attn_norm': 3.586,
     'ev_q_norm': 8.0,
     'ev_kv_norm': 8.0,
     'ev_gdn_norm': 5.02,
     'od_attn_norm': 6.978,
     'od_pe_k': 35.02,
     'od_pe_v': 64.0,
     'ffn_norm': 2.82,
     'final_norm': 7.863}
    for name, (base, spread) in spreads.items():
        noise = np.random.default_rng([zlib.crc32(name.encode()), seed]).standard_normal(out[name].shape)
        drawn = base * np.exp(spread * noise) if base else spread * noise
        out[name] = __import__('jax').numpy.asarray(drawn.astype(out[name].dtype))
    for name, factor in factors.items():
        out[name] = (out[name] * factor).astype(out[name].dtype)
    return out
```

```python
import math
from contextlib import ExitStack

import numpy as np

import concourse.bass as bass
from concourse import mybir

D_MODEL, SEQ, EPS = 1024, 512, 1e-6
MLA_HEADS, Q_RANK, KV_RANK, NOPE, ROPE, MLA_V = 8, 384, 256, 64, 32, 64
GDN_HEADS, GDN_D, GDN_CONV = 4, 128, 4
NSA_HEADS, NSA_GROUPS, NSA_DIM = 16, 4, 64
NSA_HPG = NSA_HEADS // NSA_GROUPS
CMP_BLOCK, CMP_STRIDE, CMP_HIDDEN = 32, 16, 256
FFN_HIDDEN = ((8 * D_MODEL + 3 * 256 - 1) // (3 * 256)) * 256
P = 128
KT = D_MODEL // P
NQT = SEQ // P
FT = FFN_HIDDEN // P
UK, UM = 8, 2
NCMP = 32
NEG = -1e30
BIG = 3.0e38

UNITS = {}
_at = 0
for _name, _n in (("ev_in", 11), ("mla", 3), ("ev_out", 4), ("gu0", FT), ("down0", 12), ("od_in", 10),
                  ("cmp", 4), ("od_out", 4), ("gu1", FT), ("down1", 12)):
    UNITS[_name] = (_at, _at + _n)
    _at += _n
N_UNITS = _at

COLS = {}
_at = 0
for _name, _n in (("ident", P), ("utri", P), ("ones", P), ("level", 7 * P), ("rope", SEQ),
                  ("rel", SEQ), ("causal", SEQ), ("any_valid", NQT),
                  ("g_ev", KT), ("g_od", KT), ("g_ffn0", KT), ("g_ffn1", KT), ("g_final", KT),
                  ("g_q", 3), ("g_kv", 2), ("g_gdn", 1), ("conv", 12 * GDN_CONV), ("a_log", GDN_HEADS),
                  ("dt_bias", GDN_HEADS), ("eps", 1), ("slope", NSA_HEADS), ("pe_k", 16), ("pe_v", 16), ("w_gate", KT * 48)):
    COLS[_name] = (_at, _at + _n)
    _at += _n
N_COLS = _at


def build_program(nc, x_t, stream, consts, cmp_bias_in, w2_in, out_t, dbg=None):
    F32, F32R = mybir.dt.float32, mybir.dt.float32r
    ACT, ALU, AX = mybir.ActivationFunctionType, mybir.AluOpType, mybir.AxisListType
    whole = ExitStack()

    def sb(ctx, name, shape, dt=F32, side=None):
        return ctx.enter_context(nc.sbuf_tensor(name, shape, dt, side=side))

    def banks(ctx, tag):
        return [ctx.enter_context(nc.psum_tensor(f"ps_{tag}{i}", [P, 512], F32)) for i in range(8)]

    sem_of = {}

    def sem(name):
        sem_of[name] = whole.enter_context(nc.semaphore(name))
        return sem_of[name]

    cst = sb(whole, "cst", [P, N_COLS])
    h = sb(whole, "h", [P, KT, SEQ])
    raw = sb(whole, "raw", [P, 2, UK * UM * P])
    whi = sb(whole, "whi", [P, 2, UK * UM * P], F32R)
    wlo = sb(whole, "wlo", [P, 2, UK * UM * P], F32R)

    def const(name, rows=slice(0, P)):
        a, b = COLS[name]
        return cst[rows, a:b]

    ident, utri, ones = const("ident"), const("utri"), const("ones")
    eps = const("eps")

    unit_landed = [sem("unit_landed0"), sem("unit_landed1")]
    hi_ready, lo_ready, tiles_done = sem("hi_ready"), sem("lo_ready"), sem("tiles_done")

    def load_unit(sp, u, slot, landed):
        sp.wait_ge(lo_ready, u - 1)
        sp.dma_start(raw[:, slot, :], stream[u]).then_inc(landed, 16)

    def load_units(sp, name):
        a, b = UNITS[name][0] + 2, min(UNITS[name][1] + 2, N_UNITS)
        pairs = (b - a) // 2
        if pairs == 1:
            load_unit(sp, a, a % 2, unit_landed[a % 2])
            load_unit(sp, a + 1, (a + 1) % 2, unit_landed[(a + 1) % 2])
        elif pairs:
            with sp.Fori(0, pairs) as i:
                for s in range(2):
                    load_unit(sp, a + s + 2 * i, (a + s) % 2, unit_landed[(a + s) % 2])
        if (b - a) % 2:
            load_unit(sp, b - 1, (b - 1) % 2, unit_landed[(b - 1) % 2])

    def split_hi(act, base, i):
        s = base % 2
        act.wait_ge(unit_landed[s], 16 * (base // 2 + 1) + 16 * i)
        if not (isinstance(i, int) and base + 2 * i < 2):
            act.wait_ge(tiles_done, 2 * (base - 1) + 4 * i)
        nc.scalar.activation(whi[:, s, :], raw[:, s, :], ACT.Copy).then_inc(hi_ready, 1)

    def split_lo(pool, base, i):
        s = base % 2
        pool.wait_ge(hi_ready, base + 1 + 2 * i)
        nc.gpsimd.tensor_tensor(wlo[:, s, :], raw[:, s, :], whi[:, s, :].bitcast(F32),
                                ALU.subtract).then_inc(lo_ready, 1)

    def split_los(pool, name):
        a, b = UNITS[name][0] + 1, min(UNITS[name][1] + 1, N_UNITS)
        if (b - a) // 2 == 1:
            split_lo(pool, a, 0)
            split_lo(pool, a + 1, 0)
        elif (b - a) // 2:
            with pool.Fori(0, (b - a) // 2) as i:
                split_lo(pool, a, i)
                split_lo(pool, a + 1, i)
        if (b - a) % 2:
            split_lo(pool, b - 1, 0)

    def three_passes(acc, lhs_hi, lhs_lo, rhs_hi, rhs_lo, start, stop):
        nc.tensor.matmul(acc, lhs_hi, rhs_hi, start=start, stop=False)
        nc.tensor.matmul(acc, lhs_hi, rhs_lo, start=False, stop=False)
        return nc.tensor.matmul(acc, lhs_lo, rhs_hi, start=False, stop=stop)

    def unit_block(s, k, m):
        c = (k * UM + m) * P
        return whi[:, s, c:c + P], wlo[:, s, c:c + P]

    def column_tile(acc, s, m, x_hi, x_lo, k0=0, nk=UK, first=True, last=True):
        for k in range(nk):
            w_hi, w_lo = unit_block(s, k, m)
            mm = three_passes(acc, w_hi, w_lo, x_hi[:, k0 + k, :], x_lo[:, k0 + k, :],
                              first and k == 0, last and k == nk - 1)
        return mm

    norm_sems = {n: sem("norm_" + n) for n in ("sq", "ms", "ln", "rstd", "scaled", "xh", "xl")}
    norms = [0]

    def norm_parts(sq, rstd, ms, gain, xh=None, xl=None):
        n = norms[0]
        norms[0] += 1
        nk = KT * n
        s = norm_sems

        def on_act(act):
            for k in range(KT):
                nc.scalar.activation(sq[:, k, :], h[:, k, :], ACT.Square).then_inc(s["sq"], 1)
            act.wait_ge(s["ms"], n + 1)
            nc.scalar.activation(rstd[:], ms[:], ACT.Ln, bias=eps, scale=1.0 / D_MODEL).then_inc(s["ln"], 1)
            act.wait_ge(s["ln"], n + 1)
            nc.scalar.activation(rstd[:], rstd[:], ACT.Exp, scale=-0.5).then_inc(s["rstd"], 1)
            if xh is not None:
                for k in range(KT):
                    act.wait_ge(s["scaled"], nk + k + 1)
                    nc.scalar.activation(xh[:, k, :], sq[:, k, :], ACT.Copy,
                                         scale=gain[:, k:k + 1]).then_inc(s["xh"], 1)

        def on_pe(pe):
            for k in range(KT):
                pe.wait_ge(s["sq"], nk + k + 1)
                mm = nc.tensor.matmul(ms[:], ones, sq[:, k, :], start=(k == 0), stop=(k == KT - 1))
            mm.then_inc(s["ms"], 1)

        def on_dve(dve):
            dve.wait_ge(s["rstd"], n + 1)
            for k in range(KT):
                nc.vector.tensor_tensor(sq[:, k, :], h[:, k, :], rstd[:], ALU.mult).then_inc(s["scaled"], 1)
            for k in range(KT):
                dve.wait_ge(s["xh"], nk + k + 1)
                nc.vector.scalar_tensor_tensor(out=xl[:, k, :], in0=sq[:, k, :], scalar=gain[:, k:k + 1],
                                               in1=xh[:, k, :].bitcast(F32), op0=ALU.mult,
                                               op1=ALU.subtract).then_inc(s["xl"], 1)

        return on_act, on_pe, on_dve, nk + KT, n + 1

    def attention(tag, n_groups, per_group, c, s_banks, t_banks, o_banks, prob, prob_t, neg_max, row_sum,
                  query, keys, values, bias, take):
        n_heads = n_groups * per_group
        n_items = NQT * n_heads
        scores_done, biased = sem(f"scores_{tag}"), sem(f"biased_{tag}")
        probs_ready, turned = sem(f"probs_{tag}"), sem(f"turned_{tag}")
        copied = [sem(f"copied_even_{tag}"), sem(f"copied_odd_{tag}")]
        pv_done, o_taken = sem(f"pv_{tag}"), sem(f"o_taken_{tag}")

        def width(qt):
            return (qt + 1) * P

        def copy(engine, do, a, qt):
            engine.wait_ge(turned, NQT * a + qt + 1)
            if not (isinstance(a, int) and NQT * a + qt < 2):
                engine.wait_ge(pv_done, NQT * a + qt - 1)
            do(prob_t[:, qt % 2, 0:width(qt)], t_banks[qt % 2][:, 0:width(qt)]).then_inc(copied[qt % 2], 1)

        def act_copy(out, in_):
            return nc.scalar.activation(out, in_, ACT.Copy)

        def on_act(act):
            def group(g, first):
                for br in range(per_group):
                    a = per_group * g + br
                    for qt in range(NQT):
                        act.wait_ge(biased, NQT * a + qt + 1)
                        nc.scalar.activation(prob[:, qt, 0:width(qt)], prob[:, qt, 0:width(qt)], ACT.Exp,
                                             bias=neg_max[:, qt:qt + 1], scale=-1.0,
                                             accum_out=row_sum(g, br)[:, qt:qt + 1]).then_inc(probs_ready, 1)
                        if qt == 0 and not (first and br == 0):
                            copy(act, act_copy, a - 1, 2)
                        if qt == 2:
                            copy(act, act_copy, a, 0)
            group(0, True)
            with act.Fori(1, n_groups) as g:
                group(g, False)
            copy(act, act_copy, n_heads - 1, 2)

        def on_dve(dve):
            def group(g, first):
                for br in range(per_group):
                    a = per_group * g + br
                    for qt in range(NQT):
                        dve.wait_ge(scores_done, NQT * a + qt + 1)
                        if not (first and br == 0):
                            dve.wait_ge(turned, NQT * a + qt - 3)
                        nc.vector.tensor_tensor_reduce(
                            out=prob[:, qt, 0:width(qt)], in0=s_banks[qt][:, 0:width(qt)], in1=bias(g, qt),
                            scale=-c, scalar=BIG, op0=ALU.add, op1=ALU.min,
                            accum_out=neg_max[:, qt:qt + 1]).then_inc(biased, 1)
                        if qt == 1 and not (first and br == 0):
                            copy(dve, nc.vector.tensor_copy, a - 1, 3)
                        if qt == 3:
                            copy(dve, nc.vector.tensor_copy, a, 1)
                            if not (first and br == 0):
                                dve.wait_ge(pv_done, NQT * a)
                                gb = (g, br - 1) if br else (g - 1, per_group - 1)
                                take(dve, *gb, o_banks[gb[1]]).then_inc(o_taken, 1)
            for g in range(n_groups):
                group(g, g == 0)
            copy(dve, nc.vector.tensor_copy, n_heads - 1, 3)
            dve.wait_ge(pv_done, n_items)
            take(dve, n_groups - 1, per_group - 1, o_banks[per_group - 1]).then_inc(o_taken, 1)

        def on_pe(pe):
            for t in range(n_items + 3):
                if t < n_items:
                    a, qt = divmod(t, NQT)
                    if t >= 4:
                        pe.wait_ge(biased, t - 3)
                    nc.tensor.matmul(s_banks[qt][:, 0:width(qt)], query(a, qt), keys(a, width(qt)),
                                     start=True, stop=True).then_inc(scores_done, 1)
                if 2 <= t < n_items + 2:
                    a, qt = divmod(t - 2, NQT)
                    pe.wait_ge(probs_ready, t - 1)
                    if t >= 4:
                        pe.wait_ge(copied[qt % 2], (t - 4) // 2 + 1)
                    for kt in range(qt + 1):
                        tr = nc.tensor.transpose(t_banks[qt % 2][:, kt * P:(kt + 1) * P],
                                                 prob[:, qt, kt * P:(kt + 1) * P], ident)
                    tr.then_inc(turned, 1)
                if t >= 3:
                    a, qt = divmod(t - 3, NQT)
                    pe.wait_ge(copied[qt % 2], (t - 3) // 2 + 1)
                    if qt == 0 and a >= 2:
                        pe.wait_ge(o_taken, a - 1)
                    for kt in range(qt + 1):
                        pv = nc.tensor.matmul(o_banks[a % 2][:, qt * 64:(qt + 1) * 64],
                                              prob_t[:, qt % 2, kt * P:(kt + 1) * P], values(a, kt),
                                              start=(kt == 0), stop=(kt == qt))
                    pv.then_inc(pv_done, 1)
        return on_act, on_dve, on_pe

    even, even_in = ExitStack(), ExitStack()
    zg = sb(even, "zg", [P, GDN_HEADS, SEQ])
    misc = sb(even, "misc", [P, SEQ])
    qkv = sb(even, "qkv", [P, 12, SEQ])
    z = sb(even_in, "z", [P, 12, SEQ + 4])
    lat = sb(even_in, "lat", [P, 5, SEQ])

    in_landed = sem("in_landed")
    with ExitStack() as ph:
        xh, xl = sb(ph, "xh_ev", [P, KT, SEQ], F32R), sb(ph, "xl_ev", [P, KT, SEQ], F32R)
        sq, rstd = sb(ph, "sq_ev", [P, KT, SEQ]), sb(ph, "rstd_ev", [P, SEQ])
        ps = banks(ph, "evin")
        n_act, n_pe, n_dve, x_ready, _ = norm_parts(sq, rstd, ps[4], const("g_ev"), xh, xl)
        out_a, out_v = sem("evin_out_act"), sem("evin_out_dve")
        with nc.Block() as block:
            @block.sync
            def _(sp):
                sp.dma_start(cst[:], consts).then_inc(in_landed, 16)
                sp.dma_start(h[:], x_t).then_inc(in_landed, 16)
                sp.dma_start(raw[:, 0, :], stream[0]).then_inc(unit_landed[0], 16)
                sp.dma_start(raw[:, 1, :], stream[1]).then_inc(unit_landed[1], 16)
                load_units(sp, "ev_in")

            @block.gpsimd
            def _(pool):
                nc.gpsimd.memset(z[:, :, 0:3], 0.0)
                split_lo(pool, 0, 0)
                split_los(pool, "ev_in")

            def out_of(t):
                return lat[:, t, :] if t < 5 else misc[:]

            @block.scalar
            def _(act):
                act.preload_act_table_set("natural_log_exp_and_others")
                act.wait_ge(in_landed, 32)
                n_act(act)
                split_hi(act, 0, 0)
                for u in range(3):
                    split_hi(act, u + 1, 0)
                    act.wait_ge(tiles_done, 2 * u + 1)
                    nc.scalar.activation(out_of(2 * u), ps[2 * u % 4][:], ACT.Copy).then_inc(out_a, 1)

                def z_unit(i, s, out):
                    split_hi(act, 4 + s, i)
                    act.wait_ge(tiles_done, 6 + 2 * s + 1 + 4 * i)
                    nc.scalar.activation(out, ps[(2 + 2 * s) % 4][:], ACT.Copy).then_inc(out_a, 1)
                with act.Fori(0, 3) as i:
                    for s in range(2):
                        z_unit(i, s, z[:, 4 * i + 2 * s, 3:3 + SEQ])
                for s in range(2):
                    z_unit(3, s, zg[:, 2 * s, :])

            @block.vector
            def _(dve):
                dve.wait_ge(in_landed, 32)
                n_dve(dve)
                for u in range(3):
                    dve.wait_ge(tiles_done, 2 * u + 2)
                    nc.vector.tensor_copy(out_of(2 * u + 1), ps[(2 * u + 1) % 4][:]).then_inc(out_v, 1)

                def z_unit(i, s, out):
                    dve.wait_ge(tiles_done, 6 + 2 * s + 2 + 4 * i)
                    nc.vector.tensor_copy(out, ps[(3 + 2 * s) % 4][:]).then_inc(out_v, 1)
                with dve.Fori(0, 3) as i:
                    for s in range(2):
                        z_unit(i, s, z[:, 4 * i + 2 * s + 1, 3:3 + SEQ])
                for s in range(2):
                    z_unit(3, s, zg[:, 2 * s + 1, :])

            @block.tensor
            def _(pe):
                pe.wait_ge(in_landed, 32)
                n_pe(pe)
                pe.wait_ge(norm_sems["xl"], x_ready)

                def unit(u, i):
                    pe.wait_ge(lo_ready, u + 1 + 2 * i)
                    b = 2 * (u % 2)
                    if not (isinstance(i, int) and u < 2):
                        pe.wait_ge(out_a, u - 1 + 2 * i)
                        pe.wait_ge(out_v, u - 1 + 2 * i)
                    column_tile(ps[b][:], u % 2, 0, xh, xl).then_inc(tiles_done, 1)
                    column_tile(ps[b + 1][:], u % 2, 1, xh, xl).then_inc(tiles_done, 1)

                for u in range(3):
                    unit(u, 0)
                with pe.Fori(0, 4) as i:
                    unit(3, i)
                    unit(4, i)

    mla = ExitStack()
    q_all = sb(mla, "q_all", [96, MLA_HEADS, SEQ], side="right")
    k_all = sb(mla, "k_all", [96, MLA_HEADS, SEQ], side="right")
    v_all = sb(mla, "v_all", [P, NQT, MLA_HEADS * MLA_V], side="right")
    with ExitStack() as ph:
        lat_hi, lat_lo = sb(ph, "lat_hi", [P, 5, SEQ], F32R), sb(ph, "lat_lo", [P, 5, SEQ], F32R)
        sq, rstd = sb(ph, "sq_lat", [P, 5, SEQ]), sb(ph, "rstd_lat", [P, 2, SEQ])
        rot_a, rot_b = qkv[:, 8:10, :], qkv[:, 10:12, :]
        ps = banks(ph, "lat")
        g_lat = cst[:, COLS["g_q"][0]:COLS["g_kv"][1]]
        rope = const("rope")
        conv_w = const("conv")
        lat_sq, lat_ms, lat_ln, lat_rstd = sem("lat_sq"), sem("lat_ms"), sem("lat_ln"), sem("lat_rstd")
        lat_scaled, lat_hi_ready, lat_ready = sem("lat_scaled"), sem("lat_hi_ready"), sem("lat_ready")
        head_done, nope_out, rot_done, rope_out = sem("head_done"), sem("nope_out"), sem("rot_done"), sem("rope_out")
        kr_mul, kr_ready, kr_out = sem("kr_mul"), sem("kr_ready"), sem("kr_out")
        kv_done, kv_out_a, kv_out_v = sem("kv_done"), sem("kv_out_act"), sem("kv_out_dve")
        conv_step, conv_ready, silu_out = sem("conv_step"), sem("conv_ready"), sem("silu_out")
        U = UNITS["mla"][0]
        PARTS = ((0, 3, Q_RANK), (3, 5, KV_RANK))

        def wait_head(e, hd):
            if hd == 4:
                e.wait_ge(tiles_done, 2 * (U + 1))
            elif hd == 7:
                e.wait_ge(tiles_done, 2 * (U + 2))
            else:
                e.wait_ge(head_done, hd + 1 - (hd > 4))

        with nc.Block() as block:
            @block.sync
            def _(sp):
                load_units(sp, "mla")

            @block.gpsimd
            def _(pool):
                split_los(pool, "mla")
                pool.wait_ge(lo_ready, UNITS["mla"][1] + 1)
                pool.wait_ge(kr_mul, 2)
                for hd in range(MLA_HEADS):
                    nc.gpsimd.tensor_tensor(k_all[64:96, hd, :], rot_a[64:96, 1, :], rot_b[64:96, 1, :],
                                            ALU.add).then_inc(kr_out, 1)

            @block.scalar
            def _(act):
                for t in range(5):
                    nc.scalar.activation(sq[:, t, :], lat[:, t, :], ACT.Square).then_inc(lat_sq, 1)
                split_hi(act, U + 1, 0)
                for n, (a, b, rank) in enumerate(PARTS):
                    act.wait_ge(lat_ms, n + 1)
                    nc.scalar.activation(rstd[:, n, :], ps[n][:], ACT.Ln, bias=eps,
                                         scale=1.0 / rank).then_inc(lat_ln, 1)
                act.wait_ge(lat_ln, 2)
                for n in range(2):
                    nc.scalar.activation(rstd[:, n, :], rstd[:, n, :], ACT.Exp, scale=-0.5).then_inc(lat_rstd, 1)
                for t in range(5):
                    act.wait_ge(lat_scaled, t + 1)
                    nc.scalar.activation(lat_hi[:, t, :], sq[:, t, :], ACT.Copy,
                                         scale=g_lat[:, t:t + 1]).then_inc(lat_hi_ready, 1)
                for hd in range(MLA_HEADS):
                    wait_head(act, hd)
                    nc.scalar.activation(q_all[0:64, hd, :], ps[2 + hd % 2][0:64, :], ACT.Copy).then_inc(nope_out, 1)
                    if hd == 4:
                        split_hi(act, U + 2, 0)
                    if hd == 7:
                        split_hi(act, U + 3, 0)
                for j in range(4):
                    act.wait_ge(kv_done, j + 1)
                    nc.scalar.activation(k_all[0:64, 2 * j, :], ps[4 + j % 2][0:64, :], ACT.Copy).then_inc(kv_out_a, 1)
                for tt in range(0, NQT, 2):
                    act.wait_ge(kv_done, 4 + tt + 1)
                    nc.scalar.activation(v_all[:, tt, :], ps[4 + tt % 2][:], ACT.Copy).then_inc(kv_out_a, 1)
                for t in range(12):
                    act.wait_ge(conv_ready, t + 1)
                    nc.scalar.activation(qkv[:, t, :], qkv[:, t, :], ACT.Silu).then_inc(silu_out, 1)
                nc.scalar.activation(zg[:], zg[:], ACT.Silu)

            @block.vector
            def _(dve):
                nc.vector.tensor_tensor(rot_a[64:96, 1, :], misc[64:96, :], rope[64:96, :], ALU.mult).then_inc(kr_mul, 1)
                nc.vector.tensor_tensor(rot_b[64:96, 1, :], misc[96:128, :], rope[96:128, :], ALU.mult).then_inc(kr_mul, 1)
                for n, (a, b, rank) in enumerate(PARTS):
                    dve.wait_ge(lat_rstd, n + 1)
                    for t in range(a, b):
                        nc.vector.tensor_tensor(sq[:, t, :], lat[:, t, :], rstd[:, n, :], ALU.mult).then_inc(lat_scaled, 1)
                for t in range(5):
                    dve.wait_ge(lat_hi_ready, t + 1)
                    nc.vector.scalar_tensor_tensor(out=lat_lo[:, t, :], in0=sq[:, t, :], scalar=g_lat[:, t:t + 1],
                                                   in1=lat_hi[:, t, :].bitcast(F32), op0=ALU.mult,
                                                   op1=ALU.subtract).then_inc(lat_ready, 1)
                for hd in range(MLA_HEADS):
                    wait_head(dve, hd)
                    if hd:
                        dve.wait_ge(rope_out, hd)
                    b = ps[2 + hd % 2]
                    nc.vector.tensor_tensor(rot_a[64:96, 0, :], b[64:96, :], rope[64:96, :], ALU.mult).then_inc(rot_done, 1)
                    nc.vector.tensor_tensor(rot_b[64:96, 0, :], b[96:128, :], rope[96:128, :], ALU.mult).then_inc(rot_done, 1)
                    dve.wait_ge(rot_done, 2 * hd + 2)
                    nc.vector.tensor_tensor(q_all[64:96, hd, :], rot_a[64:96, 0, :], rot_b[64:96, 0, :],
                                            ALU.add).then_inc(rope_out, 1)
                for j in range(4):
                    dve.wait_ge(kv_done, j + 1)
                    nc.vector.tensor_copy(k_all[0:64, 2 * j + 1, :], ps[4 + j % 2][64:128, :]).then_inc(kv_out_v, 1)
                for tt in range(1, NQT, 2):
                    if tt == 3:
                        dve.wait_ge(tiles_done, 2 * (U + 3))
                    else:
                        dve.wait_ge(kv_done, 4 + tt + 1)
                    nc.vector.tensor_copy(v_all[:, tt, :], ps[4 + tt % 2][:]).then_inc(kv_out_v, 1)
                dve.wait_ge(rope_out, MLA_HEADS)
                for t in range(12):
                    if t == 8:
                        dve.wait_ge(kr_out, MLA_HEADS)
                    w = conv_w[:, t * GDN_CONV:(t + 1) * GDN_CONV]
                    nc.vector.tensor_scalar(qkv[:, t, :], z[:, t, 0:SEQ], w[:, 0:1], None, ALU.mult).then_inc(conv_step, 1)
                    for j in range(1, GDN_CONV):
                        dve.wait_ge(conv_step, 3 * t + j)
                        nc.vector.scalar_tensor_tensor(out=qkv[:, t, :], in0=z[:, t, j:j + SEQ], scalar=w[:, j:j + 1],
                                                       in1=qkv[:, t, :], op0=ALU.mult, op1=ALU.add
                                                       ).then_inc(conv_step if j < GDN_CONV - 1 else conv_ready, 1)

            @block.tensor
            def _(pe):
                for n, (a, b, rank) in enumerate(PARTS):
                    for t in range(a, b):
                        pe.wait_ge(lat_sq, t + 1)
                        mm = nc.tensor.matmul(ps[n][:], ones, sq[:, t, :], start=(t == a), stop=(t == b - 1))
                    mm.then_inc(lat_ms, 1)
                pe.wait_ge(lat_ready, 5)
                for hd in range(MLA_HEADS):
                    s = (U + (hd > 4)) % 2
                    pe.wait_ge(lo_ready, U + (hd > 4) + 1)
                    if hd >= 2:
                        pe.wait_ge(nope_out, hd - 1)
                        pe.wait_ge(rope_out, hd - 1)
                    for k in range(3):
                        c = (3 * (hd - 5 * (hd > 4)) + k) * P
                        mm = three_passes(ps[2 + hd % 2][:], whi[:, s, c:c + P], wlo[:, s, c:c + P],
                                          lat_hi[:, k, :], lat_lo[:, k, :], k == 0, k == 2)
                    if hd in (4, 7):
                        mm.then_inc(tiles_done, 2)
                    else:
                        mm.then_inc(head_done, 1)
                s = (U + 2) % 2
                pe.wait_ge(lo_ready, U + 3)
                for j in range(4):
                    if j >= 2:
                        pe.wait_ge(kv_out_a, j - 1)
                        pe.wait_ge(kv_out_v, j - 1)
                    for k in range(2):
                        c = (2 * j + k) * P
                        mm = three_passes(ps[4 + j % 2][:], whi[:, s, c:c + P], wlo[:, s, c:c + P],
                                          lat_hi[:, 3 + k, :], lat_lo[:, 3 + k, :], k == 0, k == 1)
                    mm.then_inc(kv_done, 1)
                for tt in range(NQT):
                    if tt < 2:
                        pe.wait_ge(kv_out_a, 3 + tt)
                        pe.wait_ge(kv_out_v, 3 + tt)
                    elif tt == 2:
                        pe.wait_ge(kv_out_a, 5)
                    else:
                        pe.wait_ge(kv_out_v, 5)
                    tok = slice(tt * P, (tt + 1) * P)
                    for k in range(2):
                        c = (8 + 4 * k) * P
                        mm = three_passes(ps[4 + tt % 2][:], lat_hi[:, 3 + k, tok], lat_lo[:, 3 + k, tok],
                                          whi[:, s, c:c + 512], wlo[:, s, c:c + 512], k == 0, k == 1)
                    if tt == 3:
                        mm.then_inc(tiles_done, 2)
                    else:
                        mm.then_inc(kv_done, 1)
    even_in.close()

    mix_hi = sb(even, "mix_hi", [P, KT, SEQ], F32R)
    mix_lo = sb(even, "mix_lo", [P, KT, SEQ], F32R)
    with ExitStack() as ph:
        prob, prob_t = sb(ph, "prob_m", [P, NQT, SEQ]), sb(ph, "prob_t_m", [P, 2, SEQ])
        neg_max, row_sum = sb(ph, "neg_max_m", [P, NQT]), sb(ph, "row_sum_m", [P, MLA_HEADS, NQT])
        inv = sb(ph, "inv_m", [P, NQT])
        o_nat = sb(ph, "o_nat", [P, NQT, MLA_HEADS * MLA_V])
        ps = banks(ph, "mla")
        causal = const("causal")
        inv_ready, o_scaled, mix_turned, mix_hi_out, mix_lo_out = (
            sem("m_inv"), sem("m_scaled"), sem("m_turned"), sem("m_hi_out"), sem("m_lo_out"))

        def take(dve, g, br, bank):
            a = 2 * g + br
            nc.vector.reciprocal(inv[:], row_sum[:, a, :]).then_inc(inv_ready, 1)
            dve.wait_ge(inv_ready, a + 1)
            return nc.vector.tensor_tensor(o_nat[:, :, bass.ts(a, MLA_V)],
                                           bank[:, 0:NQT * MLA_V].rearrange("p (t d) -> p t d", t=NQT),
                                           inv[:, :, None].to_broadcast([P, NQT, MLA_V]), ALU.mult)

        with nc.Block() as block:
            on_act, on_dve, on_pe = attention(
                "mla", MLA_HEADS // 2, 2, float((NOPE + ROPE) ** -0.5), ps[0:4], ps[4:6], ps[6:8], prob, prob_t,
                neg_max, lambda g, br: row_sum[:, 2 * g + br, :],
                query=lambda a, qt: q_all[:, a, qt * P:(qt + 1) * P],
                keys=lambda a, w: k_all[:, a, 0:w],
                values=lambda a, kt: v_all[:, kt, a * MLA_V:(a + 1) * MLA_V],
                bias=lambda g, qt: causal[:, (NQT - 1 - qt) * P:SEQ], take=take)

            @block.scalar
            def _(act):
                on_act(act)
                for f in range(4):
                    act.wait_ge(mix_turned, f + 1)
                    nc.scalar.activation(mix_hi[:, f, :], ps[f][:], ACT.Copy).then_inc(mix_hi_out, 1)

            @block.vector
            def _(dve):
                on_dve(dve)
                for f in range(4):
                    dve.wait_ge(mix_hi_out, f + 1)
                    nc.vector.tensor_tensor(mix_lo[:, f, :], ps[f][:], mix_hi[:, f, :].bitcast(F32),
                                            ALU.subtract).then_inc(mix_lo_out, 1)

            @block.tensor
            def _(pe):
                on_pe(pe)
                pe.wait_ge(sem_of["o_taken_mla"], MLA_HEADS)
                for f in range(4):
                    for qt in range(NQT):
                        tr = nc.tensor.transpose(ps[f][:, qt * P:(qt + 1) * P], o_nat[:, qt, f * P:(f + 1) * P], ident)
                    tr.then_inc(mix_turned, 1)
    mla.close()

    NC, HD, C = NQT, GDN_HEADS, P
    with ExitStack() as ph:
        def tile(name, *shape):
            return sb(ph, name, [P, *shape])
        ba = tile("g_ba", NC, 8)
        col = {n: tile("g_" + n, NC, HD) for n in ("beta", "soft", "tmp", "g", "gc", "egc", "bg", "last", "kd", "elast", "ea", "nbeta")}
        norm = tile("g_norm", 2, 512)
        kbg, kdec, vb = (tile("g_" + n, NC, HD * C) for n in ("kbg", "kdec", "vb"))
        nat, intra = tile("g_nat", NC, HD * C), tile("g_intra", NC, HD * C)
        t_, tt_ = tile("g_t", NC, HD * C), tile("g_tt", NC, HD * C)
        dec = tile("g_dec", 2, HD * C)
        xb = tile("g_x", 2, HD * C)
        off = tile("g_off", 2, HD * C)
        state = tile("g_state", HD * C)
        vn = tile("g_vn", HD * C)
        ps = banks(ph, "gdn")
        vrows = const("level")

        def heads(ap):
            return ap.rearrange("p (h c) -> p h c", h=HD)

        def over(c4):
            return c4[:, :, None].to_broadcast([P, HD, C])

        def per_head(mat):
            return mat[:, None, :].to_broadcast([P, HD, C])

        def chained(engine, s):
            n = [0]

            def step(ins):
                ins.then_inc(s, 1)
                n[0] += 1
                engine.wait_ge(s, n[0])
            return step
        E_SEMS = {n: sem("gdn_" + n) for n in (
            "sq", "ms", "ln", "rs", "normed", "ba_turned", "ba_out", "act_col", "dve_col", "g_ready", "gc_done", "gc_out",
            "rows_done", "diff", "dec", "dec_masked", "decb", "pairs_done", "nat_out", "intra_out", "qd_row", "qd_out",
            "k_turned", "k_out", "v_turned", "v_out", "off_ready", "x_done", "x_out", "u_done", "t_out", "tt_out",
            "w_done", "w_out", "vn_done", "vn_out", "o_done", "o_out", "s_done", "s_out", "o_sq", "o_ms", "o_ln", "o_rs",
            "y1", "y2", "y_hi", "y_lo", "id_out")}
        S_ = E_SEMS
        with nc.Block() as block:
            @block.scalar
            def _(act):
                for n in range(10):
                    if n < 8:
                        if n >= 2:
                            act.wait_ge(S_["ms"], n - 1)
                        nc.scalar.activation(xb[:, n % 2, :], qkv[:, n, :], ACT.Square).then_inc(S_["sq"], 1)
                    if n < 2:
                        continue
                    t = n - 2
                    act.wait_ge(S_["ms"], t + 1)
                    if t >= 2:
                        act.wait_ge(S_["normed"], t - 1)
                    nc.scalar.activation(norm[:, t % 2, :], ps[t % 4][:], ACT.Ln, bias=eps).then_inc(S_["ln"], 1)
                    act.wait_ge(S_["ln"], t + 1)
                    nc.scalar.activation(norm[:, t % 2, :], norm[:, t % 2, :], ACT.Exp, scale=-0.5).then_inc(S_["rs"], 1)
                step = chained(act, S_["act_col"])
                act.wait_ge(S_["ba_out"], 1)
                nc.scalar.activation(col["beta"][:], ba[:, :, 0:4], ACT.Exp, scale=-1.0).then_inc(S_["dec"], 1)
                act.wait_ge(S_["dve_col"], 1)
                step(nc.scalar.activation(col["tmp"][:], col["soft"][:], ACT.Abs))
                step(nc.scalar.activation(col["tmp"][:], col["tmp"][:], ACT.Exp, scale=-1.0))
                step(nc.scalar.activation(col["tmp"][:], col["tmp"][:], ACT.Ln, bias=1.0))
                step(nc.scalar.activation(col["ea"][:, 0, :], const("a_log"), ACT.Exp))
                act.wait_ge(S_["gc_done"], 1)
                nc.scalar.activation(col["gc"][:], ps[4][:, 0:NC * HD], ACT.Copy).then_inc(S_["gc_out"], 1)
                nc.scalar.activation(col["egc"][:], ps[4][:, 0:NC * HD], ACT.Exp).then_inc(S_["gc_out"], 1)
                nc.scalar.activation(col["elast"][:], ps[4][:, 64:64 + NC * HD], ACT.Exp).then_inc(S_["gc_out"], 1)
                nc.scalar.activation(col["last"][:], ps[4][:, 64:64 + NC * HD], ACT.Copy).then_inc(S_["gc_out"], 1)
                act.wait_ge(S_["diff"], 1)
                nc.scalar.activation(col["kd"][:], col["kd"][:], ACT.Exp).then_inc(S_["gc_out"], 1)

            @block.tensor
            def _(pe):
                for c in range(NC):
                    tr = nc.tensor.transpose(ps[5][:, 8 * c:8 * c + 8], misc[0:8, c * P:(c + 1) * P], ident[0:8, 0:8])
                tr.then_inc(S_["ba_turned"], 1)
                for t in range(8):
                    pe.wait_ge(S_["sq"], t + 1)
                    if t >= 4:
                        pe.wait_ge(S_["ln"], t - 3)
                    nc.tensor.matmul(ps[t % 4][:], ones, xb[:, t % 2, :], start=True, stop=True).then_inc(S_["ms"], 1)
                pe.wait_ge(S_["g_ready"], 1)
                nc.tensor.matmul(ps[4][:, 0:NC * HD], utri, col["g"][:].rearrange("p c h -> p (c h)"), start=True, stop=True)
                nc.tensor.matmul(ps[4][:, 64:64 + NC * HD], ones, col["g"][:].rearrange("p c h -> p (c h)"),
                                 start=True, stop=True).then_inc(S_["gc_done"], 1)

            @block.vector
            def _(dve):
                dve.wait_ge(S_["ba_turned"], 1)
                nc.vector.tensor_copy(ba[:].rearrange("p c h -> p (c h)"), ps[5][:, 0:8 * NC]).then_inc(S_["ba_out"], 1)
                dve.wait_ge(S_["ba_out"], 1)
                dtb = const("dt_bias")[:, None, :].to_broadcast([P, NC, HD])
                nc.vector.tensor_tensor(col["soft"][:], ba[:, :, 4:8], dtb, ALU.add).then_inc(S_["dve_col"], 1)
                for t in range(8):
                    dve.wait_ge(S_["rs"], t + 1)
                    nc.vector.scalar_tensor_tensor(out=qkv[:, t, :], in0=qkv[:, t, :],
                                                   scalar=float(GDN_D ** -0.5) if t < 4 else 1.0,
                                                   in1=norm[:, t % 2, :], op0=ALU.mult, op1=ALU.mult
                                                   ).then_inc(S_["normed"], 1)
                step = chained(dve, S_["decb"])
                dve.wait_ge(S_["dec"], 1)
                step(nc.vector.tensor_scalar(col["beta"][:], col["beta"][:], 1.0, None, ALU.add))
                step(nc.vector.reciprocal(col["beta"][:], col["beta"][:]))
                step(nc.vector.tensor_scalar(col["nbeta"][:], col["beta"][:], -1.0, None, ALU.mult))
                dve.wait_ge(S_["act_col"], 4)
                step(nc.vector.scalar_tensor_tensor(out=col["soft"][:], in0=col["soft"][:], scalar=0.0,
                                                    in1=col["tmp"][:], op0=ALU.max, op1=ALU.add))
                eab = col["ea"][:, 0:1, :].to_broadcast([P, NC, HD])
                nc.vector.scalar_tensor_tensor(out=col["g"][:], in0=col["soft"][:], scalar=-1.0, in1=eab,
                                               op0=ALU.mult, op1=ALU.mult).then_inc(S_["g_ready"], 1)
                dve.wait_ge(S_["gc_out"], 4)
                nc.vector.tensor_tensor(col["kd"][:], col["last"][:], col["gc"][:], ALU.subtract).then_inc(S_["diff"], 1)
                nc.vector.tensor_tensor(col["bg"][:], col["beta"][:], col["egc"][:], ALU.mult)

        with nc.Block() as block:
            def k_tile(hd, c):
                return qkv[:, 4 + hd, c * C:(c + 1) * C]

            def q_tile(hd, c):
                return qkv[:, hd, c * C:(c + 1) * C]

            def q_chunk(c):
                return qkv[:, 0:4, c * C:(c + 1) * C]

            @block.tensor
            def _(pe):
                for c in range(NC):
                    if c:
                        pe.wait_ge(S_["diff"], 1 + c)
                        pe.wait_ge(S_["qd_row"], c)
                        pe.wait_ge(S_["dec_masked"], c)
                    for hd in range(HD):
                        nc.tensor.matmul(ps[0][:, hd * C:(hd + 1) * C], col["g"][:, c, hd:hd + 1].to_broadcast([P, C]),
                                         utri, start=True, stop=True)
                        mm = nc.tensor.matmul(ps[1][:, hd * C:(hd + 1) * C], col["nbeta"][:, c, hd:hd + 1].to_broadcast([P, C]),
                                              ident, start=True, stop=True)
                    mm.then_inc(S_["rows_done"], 1)
                    if c:
                        pe.wait_ge(S_["nat_out"], c)
                        pe.wait_ge(S_["intra_out"], c)
                    for hd in range(HD):
                        nc.tensor.matmul(ps[2][:, hd * C:(hd + 1) * C], k_tile(hd, c), k_tile(hd, c), start=True, stop=True)
                        mm = nc.tensor.matmul(ps[3][:, hd * C:(hd + 1) * C], k_tile(hd, c), q_tile(hd, c), start=True, stop=True)
                    mm.then_inc(S_["pairs_done"], 1)
                    if c:
                        pe.wait_ge(S_["k_out"], 2 * c)
                    for hd in range(HD):
                        tr = nc.tensor.transpose(ps[4][:, hd * C:(hd + 1) * C], k_tile(hd, c), ident)
                    tr.then_inc(S_["k_turned"], 1)
                    if c:
                        pe.wait_ge(S_["v_out"], c)
                    for hd in range(HD):
                        tr = nc.tensor.transpose(ps[5][:, hd * C:(hd + 1) * C], qkv[:, 8 + hd, c * C:(c + 1) * C], ident)
                    tr.then_inc(S_["v_turned"], 1)

            @block.vector
            def _(dve):
                for c in range(NC):
                    dve.wait_ge(S_["rows_done"], c + 1)
                    if c:
                        dve.wait_ge(S_["nat_out"], c)
                        dve.wait_ge(S_["intra_out"], c)
                    nc.vector.tensor_tensor(heads(dec[:, 0, :]), heads(ps[0][:]), over(col["gc"][:, c, :]),
                                            ALU.subtract).then_inc(S_["diff"], 1)
                    dve.wait_ge(S_["diff"], 2 + c)
                    nc.vector.tensor_scalar(dec[:, 0, :], dec[:, 0, :], 0.0, None, ALU.min).then_inc(S_["y1"], 1)
                    dve.wait_ge(S_["k_turned"], c + 1)
                    nc.vector.tensor_tensor(heads(kbg[:, c, :]), heads(ps[4][:]), over(col["bg"][:, c, :]), ALU.mult).then_inc(S_["k_out"], 1)
                    nc.vector.tensor_tensor(heads(kdec[:, c, :]), heads(ps[4][:]), over(col["kd"][:, c, :]), ALU.mult).then_inc(S_["k_out"], 1)
                    dve.wait_ge(S_["v_turned"], c + 1)
                    nc.vector.tensor_tensor(heads(vb[:, c, :]), heads(ps[5][:]), over(col["beta"][:, c, :]), ALU.mult).then_inc(S_["v_out"], 1)
                    dve.wait_ge(S_["dec"], 2 + c)
                    nc.vector.tensor_tensor(heads(dec[:, 1, :]), heads(dec[:, 0, :]), per_head(utri), ALU.mult).then_inc(S_["y2"], 1)
                    dve.wait_ge(S_["y2"], c + 1)
                    nc.vector.tensor_tensor(dec[:, 0, :], dec[:, 1, :], ps[1][:], ALU.mult).then_inc(S_["dec_masked"], 1)
                    dve.wait_ge(S_["dec_masked"], c + 1)
                    dve.wait_ge(S_["pairs_done"], c + 1)
                    nc.vector.tensor_tensor(nat[:, c, :], ps[2][:], dec[:, 0, :], ALU.mult).then_inc(S_["nat_out"], 1)
                    nc.vector.tensor_tensor(intra[:, c, :], ps[3][:], dec[:, 1, :], ALU.mult).then_inc(S_["intra_out"], 1)
                    dve.wait_ge(S_["qd_row"], c + 1)
                    nc.vector.tensor_tensor(q_chunk(c), q_chunk(c), heads(norm[:, c % 2, :]), ALU.mult).then_inc(S_["qd_out"], 1)

            @block.scalar
            def _(act):
                for c in range(NC):
                    act.wait_ge(S_["diff"], 2 + c)
                    if c >= 2:
                        act.wait_ge(S_["qd_out"], c - 1)
                    nc.scalar.activation(norm[:, c % 2, :], ps[0][:], ACT.Exp).then_inc(S_["qd_row"], 1)
                    act.wait_ge(S_["y1"], c + 1)
                    nc.scalar.activation(dec[:, 0, :], dec[:, 0, :], ACT.Exp).then_inc(S_["dec"], 1)

        LEVELS = 7
        with nc.Block() as block:
            def level(l):
                return vrows[:, l * P:(l + 1) * P]

            @block.gpsimd
            def _(pool):
                for l in range(LEVELS):
                    for c in range(NC):
                        n = l * NC + c
                        if n >= 2:
                            pool.wait_ge(S_["x_done"], n - 1)
                            if n < NC + 2:
                                pool.wait_ge(S_["tt_out"], n - 1)
                        nc.gpsimd.tensor_tensor(heads(off[:, n % 2, :]), heads(nat[:, c, :]), per_head(level(l)),
                                                ALU.mult).then_inc(S_["off_ready"], 1)

            @block.tensor
            def _(pe):
                for l in range(LEVELS):
                    for c in range(NC):
                        n = l * NC + c
                        pe.wait_ge(S_["off_ready"], n + 1)
                        if n >= 2:
                            pe.wait_ge(S_["x_out"], n - 1)
                        if l:
                            pe.wait_ge(S_["t_out"], n - NC + 1)
                        for hd in range(HD):
                            r = slice(hd * C, (hd + 1) * C)
                            mm = nc.tensor.matmul(ps[n % 2][:, r], off[:, n % 2, r], t_[:, c, r] if l else ident,
                                                  start=True, stop=True)
                        mm.then_inc(S_["x_done"], 1)
                        if l:
                            m = n - NC
                            pe.wait_ge(S_["x_out"], n + 1)
                            pe.wait_ge(S_["tt_out"], n - NC + 1)
                            if l < LEVELS - 1:
                                if m >= 2:
                                    pe.wait_ge(S_["t_out"], n - 1)
                                for hd in range(HD):
                                    r = slice(hd * C, (hd + 1) * C)
                                    nc.tensor.matmul(ps[2 + n % 2][:, r], tt_[:, c, r], xb[:, n % 2, r], start=True, stop=True)
                            if m >= 2:
                                pe.wait_ge(S_["tt_out"], n - 1)
                            for hd in range(HD):
                                r = slice(hd * C, (hd + 1) * C)
                                mm = nc.tensor.matmul(ps[4 + n % 2][:, r], xb[:, n % 2, r], tt_[:, c, r], start=True, stop=True)
                            mm.then_inc(S_["u_done"], 1)

            @block.scalar
            def _(act):
                for n in range(LEVELS * NC):
                    act.wait_ge(S_["x_done"], n + 1)
                    if n >= NC + 2:
                        act.wait_ge(S_["u_done"], n - NC - 1)
                    elif n >= 2:
                        act.wait_ge(S_["t_out"], n - 1)
                    nc.scalar.activation(xb[:, n % 2, :], ps[n % 2][:], ACT.Copy).then_inc(S_["x_out"], 1)

            @block.vector
            def _(dve):
                for l in range(LEVELS):
                    for c in range(NC):
                        n = l * NC + c
                        if l == 0:
                            dve.wait_ge(S_["x_out"], n + 1)
                            nc.vector.tensor_tensor(heads(t_[:, c, :]), heads(xb[:, n % 2, :]), per_head(ident), ALU.add).then_inc(S_["t_out"], 1)
                            nc.vector.tensor_tensor(heads(tt_[:, c, :]), heads(off[:, n % 2, :]), per_head(ident), ALU.add).then_inc(S_["tt_out"], 1)
                        else:
                            dve.wait_ge(S_["u_done"], n - NC + 1)
                            if l < LEVELS - 1:
                                nc.vector.tensor_tensor(t_[:, c, :], t_[:, c, :], ps[2 + n % 2][:], ALU.add).then_inc(S_["t_out"], 1)
                            nc.vector.tensor_tensor(tt_[:, c, :], tt_[:, c, :], ps[4 + n % 2][:], ALU.add).then_inc(S_["tt_out"], 1)

        nw = t_
        o_t = nat
        with nc.Block() as block:
            def o_chunk(c):
                return o_t[:, :, c * C:(c + 1) * C]

            @block.tensor
            def _(pe):
                for c in range(NC):
                    if c >= 2:
                        pe.wait_ge(S_["w_out"], c - 1)
                    for hd in range(HD):
                        r = slice(hd * C, (hd + 1) * C)
                        mm = nc.tensor.matmul(ps[c % 2][:, r], kbg[:, c, r], tt_[:, c, r], start=True, stop=True)
                    mm.then_inc(S_["w_done"], 1)
                for c in range(NC):
                    if c:
                        pe.wait_ge(S_["w_out"], c + 1)
                        pe.wait_ge(S_["s_out"], c)
                        pe.wait_ge(S_["vn_out"], c)
                    for hd in range(HD):
                        r = slice(hd * C, (hd + 1) * C)
                        mm = nc.tensor.matmul(ps[2][:, r], tt_[:, c, r], vb[:, c, r], start=True, stop=c == 0)
                        if c:
                            mm = nc.tensor.matmul(ps[2][:, r], nw[:, c, r], state[:, r], start=False, stop=True)
                    mm.then_inc(S_["vn_done"], 1)
                    pe.wait_ge(S_["vn_out"], c + 1)
                    if c:
                        pe.wait_ge(S_["s_out"], c)
                    for hd in range(HD):
                        r = slice(hd * C, (hd + 1) * C)
                        if c < NC - 1:
                            mm = nc.tensor.matmul(ps[3][:, r], kdec[:, c, r], vn[:, r], start=True, stop=True)
                    if c < NC - 1:
                        mm.then_inc(S_["s_done"], 1)
                    if c:
                        pe.wait_ge(S_["o_out"], c)
                    for hd in range(HD):
                        r = slice(hd * C, (hd + 1) * C)
                        if c:
                            nc.tensor.matmul(ps[4][:, r], state[:, r], q_tile(hd, c), start=True, stop=False)
                        mm = nc.tensor.matmul(ps[4][:, r], vn[:, r], intra[:, c, r], start=c == 0, stop=True)
                    mm.then_inc(S_["o_done"], 1)
                for hd in range(HD):
                    pe.wait_ge(S_["o_sq"], hd + 1)
                    nc.tensor.matmul(ps[hd][:], ones, xb[:, hd % 2, :], start=True, stop=True).then_inc(S_["o_ms"], 1)

            @block.scalar
            def _(act):
                for c in range(NC):
                    act.wait_ge(S_["w_done"], c + 1)
                    nc.scalar.activation(nw[:, c, :], ps[c % 2][:], ACT.Copy, scale=-1.0).then_inc(S_["w_out"], 1)
                for c in range(NC):
                    act.wait_ge(S_["vn_done"], c + 1)
                    if c:
                        act.wait_ge(S_["o_done"], c)
                    nc.scalar.activation(vn[:], ps[2][:], ACT.Copy).then_inc(S_["vn_out"], 1)
                act.wait_ge(S_["o_out"], NC)
                for hd in range(HD):
                    if hd >= 2:
                        act.wait_ge(S_["o_ms"], hd - 1)
                    nc.scalar.activation(xb[:, hd % 2, :], o_t[:, hd, :], ACT.Square).then_inc(S_["o_sq"], 1)
                for hd in range(HD):
                    act.wait_ge(S_["o_ms"], hd + 1)
                    if hd >= 2:
                        act.wait_ge(S_["y_lo"], hd - 1)
                    nc.scalar.activation(norm[:, hd % 2, :], ps[hd][:], ACT.Ln, bias=eps, scale=1.0 / GDN_D).then_inc(S_["o_ln"], 1)
                    act.wait_ge(S_["o_ln"], hd + 1)
                    nc.scalar.activation(norm[:, hd % 2, :], norm[:, hd % 2, :], ACT.Exp, scale=-0.5).then_inc(S_["o_rs"], 1)
                for hd in range(HD):
                    act.wait_ge(S_["id_out"], hd + 1)
                    nc.scalar.activation(mix_hi[:, 4 + hd, :], o_t[:, hd, :], ACT.Copy).then_inc(S_["y_hi"], 1)

            @block.vector
            def _(dve):
                for c in range(NC):
                    if c < NC - 1:
                        dve.wait_ge(S_["s_done"], c + 1)
                        if c == 0:
                            nc.vector.tensor_copy(state[:], ps[3][:]).then_inc(S_["s_out"], 1)
                    dve.wait_ge(S_["o_done"], c + 1)
                    if 0 < c < NC - 1:
                        nc.vector.tensor_tensor(heads(state[:]), heads(state[:]), over(col["elast"][:, c, :]), ALU.mult).then_inc(S_["v_turned"], 1)
                        dve.wait_ge(S_["v_turned"], NC + c)
                        nc.vector.tensor_tensor(state[:], state[:], ps[3][:], ALU.add).then_inc(S_["s_out"], 1)
                    nc.vector.tensor_copy(o_chunk(c), heads(ps[4][:])).then_inc(S_["o_out"], 1)
                for hd in range(HD):
                    dve.wait_ge(S_["o_sq"], hd + 1)
                    dve.wait_ge(S_["o_rs"], hd + 1)
                    nc.vector.scalar_tensor_tensor(out=o_t[:, hd, :], in0=o_t[:, hd, :], scalar=const("g_gdn"), in1=norm[:, hd % 2, :],
                                                   op0=ALU.mult, op1=ALU.mult).then_inc(S_["y_lo"], 1)
                    dve.wait_ge(S_["y_lo"], hd + 1)
                    nc.vector.tensor_tensor(o_t[:, hd, :], o_t[:, hd, :], zg[:, hd, :], ALU.mult).then_inc(S_["id_out"], 1)
                for hd in range(HD):
                    dve.wait_ge(S_["y_hi"], hd + 1)
                    nc.vector.tensor_tensor(mix_lo[:, 4 + hd, :], o_t[:, hd, :], mix_hi[:, 4 + hd, :].bitcast(F32), ALU.subtract)

    def project_residual(name, x_hi, x_lo):
        U = UNITS[name][0]
        added = sem(f"added_{name}")
        with ExitStack() as ph:
            ps = banks(ph, name)
            with nc.Block() as block:
                @block.sync
                def _(sp):
                    load_units(sp, name)

                @block.gpsimd
                def _(pool):
                    split_los(pool, name)

                @block.scalar
                def _(act):
                    with act.Fori(0, 2) as i:
                        split_hi(act, U + 1, i)
                        split_hi(act, U + 2, i)

                @block.vector
                def _(dve):
                    with dve.Fori(0, 2) as i:
                        for t in range(4):
                            dve.wait_ge(tiles_done, 2 * U + t + 1 + 4 * i)
                            nc.vector.tensor_tensor(h[:, 4 * i + t, :], h[:, 4 * i + t, :], ps[t][:],
                                                    ALU.add).then_inc(added, 1)

                @block.tensor
                def _(pe):
                    with pe.Fori(0, 2) as i:
                        for j in range(2):
                            pe.wait_ge(lo_ready, U + j + 1 + 2 * i)
                            for m in range(2):
                                pe.wait_ge(added, 4 * i)
                                column_tile(ps[2 * j + m][:], (U + j) % 2, m, x_hi, x_lo).then_inc(tiles_done, 1)

    project_residual("ev_out", mix_hi, mix_lo)
    even.close()

    def ffn(n):
        gu, down = f"gu{n}", f"down{n}"
        with ExitStack() as ph:
            hid_hi, hid_lo = sb(ph, f"hid_hi{n}", [P, FT, SEQ], F32R), sb(ph, f"hid_lo{n}", [P, FT, SEQ], F32R)
            ps = banks(ph, f"ffn{n}")
            with ExitStack() as up:
                xh, xl = sb(up, f"xh_f{n}", [P, KT, SEQ], F32R), sb(up, f"xl_f{n}", [P, KT, SEQ], F32R)
                sq, rstd = sb(up, f"sq_f{n}", [P, KT, SEQ]), sb(up, f"rstd_f{n}", [P, SEQ])
                n_act, n_pe, n_dve, x_ready, _ = norm_parts(sq, rstd, ps[4], const(f"g_ffn{n}"), xh, xl)
                silu, prod = sq[:, 0:2, :], sq[:, 2:4, :]
                silu_done, prod_done, hi_done, lo_done = (sem(f"silu{n}"), sem(f"prod{n}"), sem(f"hid_hi_out{n}"),
                                                          sem(f"hid_lo_out{n}"))
                U = UNITS[gu][0]
                with nc.Block() as block:
                    @block.sync
                    def _(sp):
                        load_units(sp, gu)

                    @block.gpsimd
                    def _(pool):
                        split_los(pool, gu)

                    @block.scalar
                    def _(act):
                        n_act(act)
                        act.wait_ge(norm_sems["xl"], x_ready)
                        with act.Fori(0, FT // 2) as i:
                            split_hi(act, U + 1, i)
                            for m in range(2):
                                act.wait_ge(tiles_done, 2 * U + m + 1 + 4 * i)
                                nc.scalar.activation(silu[:, m, :], ps[m][:], ACT.Silu).then_inc(silu_done, 1)
                            split_hi(act, U + 2, i)
                            for m in range(2):
                                act.wait_ge(prod_done, m + 1 + 2 * i)
                                nc.scalar.activation(hid_hi[:, 2 * i + m, :], prod[:, m, :], ACT.Copy).then_inc(hi_done, 1)

                    @block.vector
                    def _(dve):
                        n_dve(dve)
                        with dve.Fori(0, FT // 2) as i:
                            dve.wait_ge(lo_done, 2 * i)
                            for m in range(2):
                                dve.wait_ge(tiles_done, 2 * U + m + 3 + 4 * i)
                                dve.wait_ge(silu_done, m + 1 + 2 * i)
                                nc.vector.tensor_tensor(prod[:, m, :], silu[:, m, :], ps[2 + m][:],
                                                        ALU.mult).then_inc(prod_done, 1)
                            for m in range(2):
                                dve.wait_ge(hi_done, m + 1 + 2 * i)
                                nc.vector.tensor_tensor(hid_lo[:, 2 * i + m, :], prod[:, m, :],
                                                        hid_hi[:, 2 * i + m, :].bitcast(F32),
                                                        ALU.subtract).then_inc(lo_done, 1)

                    @block.tensor
                    def _(pe):
                        n_pe(pe)
                        pe.wait_ge(norm_sems["xl"], x_ready)
                        with pe.Fori(0, FT // 2) as i:
                            for j in range(2):
                                pe.wait_ge(lo_ready, U + j + 1 + 2 * i)
                                pe.wait_ge(prod_done if j else silu_done, 2 * i)
                                for m in range(2):
                                    column_tile(ps[2 * j + m][:], (U + j) % 2, m, xh, xl).then_inc(tiles_done, 1)
            U = UNITS[down][0]
            added = sem(f"added_{down}")
            with nc.Block() as block:
                @block.sync
                def _(sp):
                    load_units(sp, down)

                @block.gpsimd
                def _(pool):
                    split_los(pool, down)

                @block.scalar
                def _(act):
                    a, b = U + 1, min(UNITS[down][1] + 1, N_UNITS)
                    with act.Fori(0, (b - a) // 2) as i:
                        split_hi(act, a, i)
                        split_hi(act, a + 1, i)
                    if (b - a) % 2:
                        split_hi(act, b - 1, 0)

                @block.vector
                def _(dve):
                    with dve.Fori(0, KT // 4) as i:
                        for t in range(4):
                            dve.wait_ge(tiles_done, 2 * (U + 3 * (t // 2) + 2) + t % 2 + 1 + 12 * i)
                            nc.vector.tensor_tensor(h[:, 4 * i + t, :], h[:, 4 * i + t, :], ps[4 + t][:],
                                                    ALU.add).then_inc(added, 1)

                @block.tensor
                def _(pe):
                    with pe.Fori(0, KT // 4) as i:
                        for j in range(6):
                            pe.wait_ge(lo_ready, U + j + 1 + 6 * i)
                            if j % 3 == 0:
                                pe.wait_ge(added, 4 * i)
                            r = j % 3
                            for m in range(2):
                                column_tile(ps[4 + 2 * (j // 3) + m][:], (U + j) % 2, m, hid_hi, hid_lo, k0=UK * r,
                                            nk=min(UK, FT - UK * r), first=r == 0, last=r == 2).then_inc(tiles_done, 1)

    ffn(0)

    odd, cmp_in = ExitStack(), ExitStack()
    G, CW = NSA_GROUPS, SEQ + CMP_STRIDE
    q_n = sb(odd, "q_n", [P, NSA_HEADS // 2, SEQ])
    k_two = [sb(odd, f"k_{n}", [P, G, SEQ]) for n in ("sel", "win")]
    v_two = [sb(odd, f"v_{n}", [P, NQT, G * NSA_DIM]) for n in ("sel", "win")]
    gates = sb(odd, "gates", [P, NQT, 3 * NSA_HEADS])
    k_cmp = sb(odd, "k_cmp", [P, G * NCMP])
    v_cmp = sb(odd, "v_cmp", [P, G * NSA_DIM])
    seq_hi = [sb(cmp_in, f"seq_hi_{n}", [P, G + 1, CW], F32R) for n in "kv"]
    seq_lo = [sb(cmp_in, f"seq_lo_{n}", [P, G + 1, CW], F32R) for n in "kv"]
    with ExitStack() as ph:
        xh, xl = sb(ph, "xh_od", [P, KT, SEQ], F32R), sb(ph, "xl_od", [P, KT, SEQ], F32R)
        sq, rstd = sb(ph, "sq_od", [P, KT, SEQ]), sb(ph, "rstd_od", [P, SEQ])
        ps = banks(ph, "odin")
        n_act, n_pe, n_dve, x_ready, _ = norm_parts(sq, rstd, ps[4], const("g_od"), xh, xl)
        out_a, out_v, padded, piece_hi = sem("odin_out_act"), sem("odin_out_dve"), sem("od_padded"), sem("od_piece_hi")
        piece_lo = sem("od_piece_lo")
        gate_done, gate_exp, gate_step = sem("gate_done"), sem("gate_exp"), sem("gate_step")
        U = UNITS["od_in"][0]
        w_gate = const("w_gate")
        HALF = NSA_DIM

        def half(t):
            return slice(t * HALF, (t + 1) * HALF)

        with nc.Block() as block:
            @block.sync
            def _(sp):
                load_units(sp, "od_in")

            @block.gpsimd
            def _(pool):
                for t in seq_hi + seq_lo:
                    nc.gpsimd.memset(t[:].bitcast(F32), 0.0).then_inc(padded, 1)
                split_los(pool, "od_in")

            @block.scalar
            def _(act):
                n_act(act)
                with act.Fori(0, 2) as i:
                    for j in range(2):
                        split_hi(act, U + 1 + j, i)
                        act.wait_ge(tiles_done, 2 * (U + j) + 1 + 4 * i)
                        nc.scalar.activation(q_n[:, 4 * i + 2 * j, :], ps[2 * j][:], ACT.Copy).then_inc(out_a, 1)
                act.wait_ge(padded, 4)
                for v in range(2):
                    nc.scalar.activation(seq_hi[v][:, G, 0:CMP_BLOCK:2], const("pe_v" if v else "pe_k"),
                                         ACT.Copy).then_inc(piece_hi, 1)
                    split_hi(act, U + 5 + v, 0)
                    for m in range(2):
                        act.wait_ge(tiles_done, 2 * (U + 4 + v) + m + 1)
                        for g in range(2):
                            src = ps[2 * v + m][half(g), :]
                            nc.scalar.activation(seq_hi[v][0:64, 2 * m + g, 0:SEQ], src, ACT.Copy).then_inc(piece_hi, 1)
                            nc.scalar.activation(seq_hi[v][64:128, 2 * m + g, 0:SEQ - 1], src[:, 1:SEQ],
                                                 ACT.Copy).then_inc(piece_hi, 1)
                for v in range(2):
                    split_hi(act, U + 7 + v, 0)
                    for m in range(2):
                        act.wait_ge(tiles_done, 2 * (U + 6 + v) + m + 1)
                        for r in range(2):
                            nc.scalar.activation(k_two[v][half(r), 2 * m, :], ps[2 * v + m][half(0), :],
                                                 ACT.Copy).then_inc(out_a, 1)
                for v in range(2):
                    split_hi(act, U + 9 + v, 0)
                    act.wait_ge(tiles_done, 2 * (U + 8 + v) + 1)
                    nc.scalar.activation(v_two[v][:, 0:2, :], ps[2 * v][:], ACT.Copy).then_inc(out_a, 1)
                act.wait_ge(gate_done, 1)
                nc.scalar.activation(gates[:], ps[5][:, 0:NQT * 48], ACT.Exp, scale=-1.0).then_inc(gate_exp, 1)

            @block.vector
            def _(dve):
                n_dve(dve)
                with dve.Fori(0, 2) as i:
                    for j in range(2):
                        dve.wait_ge(tiles_done, 2 * (U + j) + 2 + 4 * i)
                        nc.vector.tensor_copy(q_n[:, 4 * i + 2 * j + 1, :], ps[2 * j + 1][:]).then_inc(out_v, 1)
                dve.wait_ge(padded, 4)
                for v in range(2):
                    dve.wait_ge(piece_hi, 9 * v + 1)
                    nc.vector.tensor_tensor(seq_lo[v][:, G, 0:CMP_BLOCK:2], const("pe_v" if v else "pe_k"),
                                            seq_hi[v][:, G, 0:CMP_BLOCK:2].bitcast(F32), ALU.subtract)
                    for m in range(2):
                        dve.wait_ge(piece_hi, 9 * v + 4 * m + 5)
                        for g in range(2):
                            src = ps[2 * v + m][half(g), :]
                            nc.vector.tensor_tensor(seq_lo[v][0:64, 2 * m + g, 0:SEQ], src,
                                                    seq_hi[v][0:64, 2 * m + g, 0:SEQ].bitcast(F32),
                                                    ALU.subtract).then_inc(piece_lo, 1)
                            nc.vector.tensor_tensor(seq_lo[v][64:128, 2 * m + g, 0:SEQ - 1], src[:, 1:SEQ],
                                                    seq_hi[v][64:128, 2 * m + g, 0:SEQ - 1].bitcast(F32),
                                                    ALU.subtract).then_inc(piece_lo, 1)
                for v in range(2):
                    for m in range(2):
                        dve.wait_ge(tiles_done, 2 * (U + 6 + v) + m + 1)
                        for r in range(2):
                            nc.vector.tensor_copy(k_two[v][half(r), 2 * m + 1, :], ps[2 * v + m][half(1), :]).then_inc(out_v, 1)
                for v in range(2):
                    dve.wait_ge(tiles_done, 2 * (U + 8 + v) + 2)
                    nc.vector.tensor_copy(v_two[v][:, 2:4, :], ps[2 * v + 1][:]).then_inc(out_v, 1)
                dve.wait_ge(gate_exp, 1)
                nc.vector.tensor_scalar(gates[:], gates[:], 1.0, None, ALU.add).then_inc(gate_step, 1)
                dve.wait_ge(gate_step, 1)
                nc.vector.reciprocal(gates[:], gates[:])

            @block.tensor
            def _(pe):
                n_pe(pe)
                pe.wait_ge(norm_sems["xl"], x_ready)

                def unit(u, i, *free):
                    pe.wait_ge(lo_ready, U + u + 1 + 2 * i)
                    for s, v in free:
                        pe.wait_ge(s, v)
                    for m in range(2):
                        column_tile(ps[2 * (u % 2) + m][:], (U + u) % 2, m, xh, xl).then_inc(tiles_done, 1)
                with pe.Fori(0, 2) as i:
                    unit(0, i, (out_a, 2 * i), (out_v, 2 * i))
                    unit(1, i, (out_a, 2 * i), (out_v, 2 * i))
                unit(4, 0, (out_a, 3), (out_v, 3))
                unit(5, 0, (out_a, 4), (out_v, 4))
                unit(6, 0, (piece_lo, 8))
                unit(7, 0, (piece_lo, 16))
                for v in range(2):
                    u = 8 + v
                    pe.wait_ge(lo_ready, U + u + 1)
                    pe.wait_ge(out_a, 4 + 4 * (v + 1))
                    pe.wait_ge(out_v, 4 + 4 * (v + 1))
                    for tt in range(NQT):
                        tok = slice(tt * P, (tt + 1) * P)
                        acc = ps[2 * v + tt // 2][:, (tt % 2) * 256:(tt % 2) * 256 + 256]
                        for k in range(KT):
                            c = slice(k * 256, (k + 1) * 256)
                            s = (U + u) % 2
                            mm = three_passes(acc, xh[:, k, tok], xl[:, k, tok], whi[:, s, c], wlo[:, s, c],
                                              k == 0, k == KT - 1)
                        if tt % 2:
                            mm.then_inc(tiles_done, 1)
                for tt in range(NQT):
                    tok = slice(tt * P, (tt + 1) * P)
                    for part, x in enumerate((xh, xl)):
                        for k in range(KT):
                            mm = nc.tensor.matmul(ps[5][:, tt * 48:(tt + 1) * 48], x[:, k, tok].bitcast(F32),
                                                  w_gate[:, k * 48:(k + 1) * 48],
                                                  start=part == 0 and k == 0, stop=part == 1 and k == KT - 1)
                mm.then_inc(gate_done, 1)

    w2_landed = sem("w2_landed")
    with ExitStack() as ph:
        w2 = sb(ph, "w2_sb", [P, 4 * NSA_DIM])
        first = sb(ph, "cmp_first", [P, 2])
        hidden = sb(ph, "cmp_hidden", [P, 4, G * NCMP])
        ps = banks(ph, "cmp")
        bias_out, hidden_out, cmp_done, k_out, zeroed = (sem("cmp_bias_out"), sem("cmp_hidden_out"), sem("cmp_done"),
                                                 sem("cmp_k_out"), sem("cmp_zeroed"))
        U, N = UNITS["cmp"][0], G * NCMP
        with nc.Block() as block:
            @block.sync
            def _(sp):
                sp.dma_start(w2[:], w2_in).then_inc(w2_landed, 16)
                load_units(sp, "cmp")

            @block.gpsimd
            def _(pool):
                nc.gpsimd.memset(v_cmp[:], 0.0).then_inc(zeroed, 1)
                split_los(pool, "cmp")

            @block.tensor
            def _(pe):
                for v in range(2):
                    for r in range(2):
                        u = 2 * v + r
                        pe.wait_ge(lo_ready, U + u + 1)
                        for m in range(2):
                            for k in range(UK):
                                w_hi, w_lo = unit_block((U + u) % 2, k, m)
                                t0 = 2 * (UK * r + k)
                                cols = slice(t0, t0 + CMP_STRIDE * (NCMP - 1) + 1, CMP_STRIDE)
                                mm = three_passes(ps[2 * v + m][:, 0:N + NCMP], w_hi, w_lo, seq_hi[v][:, :, cols],
                                                  seq_lo[v][:, :, cols], r == 0 and k == 0, r == 1 and k == UK - 1)
                            mm.then_inc(tiles_done, 1)
                pe.wait_ge(w2_landed, 16)
                for v in range(2):
                    pe.wait_ge(hidden_out, 2 * v + 2)
                    for m in range(2):
                        w = w2[:, (2 * v + m) * NSA_DIM:(2 * v + m + 1) * NSA_DIM]
                        if v == 0:
                            mm = nc.tensor.matmul(ps[4][0:64, 0:N], w, hidden[:, m, :], start=m == 0, stop=m == 1)
                        else:
                            mm = nc.tensor.matmul(ps[5][:, 0:NSA_DIM], hidden[:, 2 + m, :], w, start=m == 0, stop=m == 1)
                    mm.then_inc(cmp_done, 1)

            @block.scalar
            def _(act):
                for u in range(4):
                    split_hi(act, U + u + 1, 0)
                for v in range(2):
                    for m in range(2):
                        act.wait_ge(tiles_done, 2 * (U + 2 * v + 1) + m + 1)
                        nc.scalar.activation(first[:, m:m + 1], ps[2 * v + m][:, N:N + 1], ACT.Copy).then_inc(bias_out, 1)
                        act.wait_ge(bias_out, 2 * v + m + 1)
                        nc.scalar.activation(hidden[:, 2 * v + m, :], ps[2 * v + m][:, 0:N], ACT.Gelu_apprx_tanh,
                                             bias=first[:, m:m + 1]).then_inc(hidden_out, 1)
                act.wait_ge(cmp_done, 1)
                nc.scalar.activation(k_cmp[0:64, :], ps[4][0:64, 0:N], ACT.Copy)
                nc.scalar.activation(k_cmp[64:128, :], ps[4][0:64, 0:N], ACT.Copy)

            @block.vector
            def _(dve):
                dve.wait_ge(zeroed, 1)
                dve.wait_ge(cmp_done, 2)
                for g in range(G):
                    r = slice(g * NCMP, (g + 1) * NCMP)
                    nc.vector.tensor_copy(v_cmp[r, g * NSA_DIM:(g + 1) * NSA_DIM], ps[5][r, 0:NSA_DIM])
    cmp_in.close()

    att = ExitStack()
    o_acc = sb(att, "o_acc", [P, NQT, NSA_HEADS * NSA_DIM])
    with ExitStack() as ph:
        cmp_bias = sb(ph, "cmp_bias_sb", [P, NQT, NSA_HEADS * NCMP])
        probs = sb(ph, "c_probs", [P, 2, NSA_HEADS * NCMP])
        stat = sb(ph, "c_stat", [P, 2, 3, NSA_HEADS])
        turned_sb = sb(ph, "c_turned", [P, 2, SEQ])
        tmp = sb(ph, "c_tmp", [P, 2, 2, 2])
        ps = banks(ph, "natt")
        bias_landed = sem("cmp_bias_landed")
        names = ("s", "biased", "max", "sub", "exp", "sum", "inv", "gate", "valid", "turned", "copied", "o", "o_out")
        cs = {n: sem("c_" + n) for n in names}
        with nc.Block() as block:
            @block.sync
            def _(sp):
                sp.dma_start(cmp_bias[:], cmp_bias_in.rearrange("p (t n) -> p t n", t=NQT)).then_inc(bias_landed, 16)

            def keys3(ap):
                return ap.rearrange("p (h n) -> p h n", n=NCMP)

            @block.tensor
            def _(pe):
                def outputs(qt):
                    pe.wait_ge(cs["exp"], qt + 1)
                    if qt:
                        pe.wait_ge(cs["copied"], qt)
                    for r in range(NSA_HPG):
                        tr = nc.tensor.transpose(ps[4][:, r * P:(r + 1) * P], probs[:, qt % 2, r * P:(r + 1) * P], ident)
                    tr.then_inc(cs["turned"], 1)
                    pe.wait_ge(cs["copied"], qt + 1)
                    if qt:
                        pe.wait_ge(cs["o_out"], 2 * qt)
                    for r in range(NSA_HPG):
                        mm = nc.tensor.matmul(ps[5 + r // 2][:, (r % 2) * 256:(r % 2) * 256 + 256],
                                              turned_sb[:, qt % 2, r * P:(r + 1) * P], v_cmp[:], start=True, stop=True)
                    mm.then_inc(cs["o"], 1)
                for qt in range(NQT):
                    if qt >= 2:
                        pe.wait_ge(cs["biased"], 2 * (qt - 1))
                    for hd in range(NSA_HEADS):
                        rows = slice((hd % 2) * 64, (hd % 2) * 64 + 64)
                        mm = nc.tensor.matmul(ps[2 * (qt % 2) + hd % 2][:, (hd // 2) * NCMP:(hd // 2 + 1) * NCMP],
                                              q_n[rows, hd // 2, qt * P:(qt + 1) * P],
                                              k_cmp[rows, (hd // NSA_HPG) * NCMP:(hd // NSA_HPG + 1) * NCMP],
                                              start=True, stop=True)
                    mm.then_inc(cs["s"], 1)
                    if qt:
                        outputs(qt - 1)
                outputs(NQT - 1)

            @block.scalar
            def _(act):
                for qt in range(NQT):
                    act.wait_ge(cs["sub"], qt + 1)
                    nc.scalar.activation(probs[:, qt % 2, :], probs[:, qt % 2, :], ACT.Exp,
                                         scale=float(NSA_DIM ** -0.5)).then_inc(cs["exp"], 1)
                    act.wait_ge(cs["turned"], qt + 1)
                    if qt >= 2:
                        act.wait_ge(cs["o"], qt - 1)
                    nc.scalar.activation(turned_sb[:, qt % 2, :], ps[4][:], ACT.Copy).then_inc(cs["copied"], 1)

            @block.vector
            def _(dve):
                dve.wait_ge(bias_landed, 16)

                def flat(qt):
                    return keys3(probs[:, qt % 2, :])

                def finish(qt):
                    st = stat[:, qt % 2]
                    dve.wait_ge(cs["exp"], qt + 1)
                    nc.vector.tensor_reduce(st[:, 1, :], flat(qt), AX.X, ALU.add).then_inc(cs["sum"], 1)
                    dve.wait_ge(cs["sum"], qt + 1)
                    nc.vector.reciprocal(st[:, 1, :], st[:, 1, :]).then_inc(cs["inv"], 1)
                    dve.wait_ge(cs["inv"], qt + 1)
                    g0 = gates[:, qt, :].rearrange("p (g r t) -> p r g t", g=G, t=3)[:, :, :, 0]
                    nc.vector.tensor_tensor(st[:, 2, :].rearrange("p (r g) -> p r g", g=G),
                                            st[:, 1, :].rearrange("p (r g) -> p r g", g=G), g0, ALU.mult).then_inc(cs["gate"], 1)
                    dve.wait_ge(cs["gate"], qt + 1)
                    nc.vector.tensor_scalar(st[:, 2, :], st[:, 2, :], const("any_valid")[:, qt:qt + 1], None,
                                            ALU.mult).then_inc(cs["valid"], 1)
                    dve.wait_ge(cs["valid"], qt + 1)
                    dve.wait_ge(cs["o"], qt + 1)
                    for b in range(2):
                        src = ps[5 + b][:].rearrange("p (r g d) -> p r g d", r=2, g=G)
                        dst = o_acc[:, qt, :].rearrange("p (g r d) -> p r g d", g=G, r=NSA_HPG)[:, 2 * b:2 * b + 2]
                        co = st[:, 2, :].rearrange("p (b r g) -> p b r g", r=2, g=G)[:, b]
                        nc.vector.tensor_tensor(dst, src, co[:, :, :, None].to_broadcast([P, 2, G, NSA_DIM]),
                                                ALU.mult).then_inc(cs["o_out"], 1)

                for qt in range(NQT):
                    dve.wait_ge(cs["s"], qt + 1)
                    if qt >= 2:
                        dve.wait_ge(cs["turned"], qt - 1)
                        dve.wait_ge(cs["sum"], qt - 1)
                    bq = cmp_bias[:, qt, :].rearrange("p (g b a n) -> p a g b n", g=G, a=2, n=NCMP)
                    dst = probs[:, qt % 2, :].rearrange("p (b a g n) -> p a g b n", g=G, a=2, n=NCMP)
                    for a in range(2):
                        src = ps[2 * (qt % 2) + a][:, 0:8 * NCMP].rearrange("p (g b n) -> p g b n", g=G, n=NCMP)
                        nc.vector.tensor_tensor(dst[:, a], src, bq[:, a], ALU.add).then_inc(cs["biased"], 1)
                    dve.wait_ge(cs["biased"], 2 * qt + 2)
                    nc.vector.tensor_reduce(stat[:, qt % 2, 0, :], flat(qt), AX.X, ALU.max).then_inc(cs["max"], 1)
                    dve.wait_ge(cs["max"], qt + 1)
                    nc.vector.tensor_tensor(flat(qt), flat(qt),
                                            stat[:, qt % 2, 0, :, None].to_broadcast([P, NSA_HEADS, NCMP]),
                                            ALU.subtract).then_inc(cs["sub"], 1)
                    if qt:
                        finish(qt - 1)
                finish(NQT - 1)

    with ExitStack() as ph:
        dist = sb(ph, "dist", [P, NSA_HEADS, SEQ])
        prob, prob_t = sb(ph, "prob_n", [P, NQT, SEQ]), sb(ph, "prob_t_n", [P, 2, SEQ])
        neg_max, row_sum = sb(ph, "neg_max_n", [P, NQT]), sb(ph, "row_sum_n", [P, 2 * NSA_HEADS, NQT])
        inv, part = sb(ph, "inv_n", [P, NQT]), sb(ph, "part_n", [P, NQT, NSA_DIM])
        ps = banks(ph, "nat2")
        inv_ready, coef_ready, part_ready, dist_ready = sem("n_inv"), sem("n_coef"), sem("n_part"), sem("n_dist")
        rel, slope = const("rel"), const("slope")

        def take(dve, g, br, bank):
            n = 2 * g + br
            if n:
                dve.wait_ge(sem_of["o_taken_nsa"], n)
            nc.vector.reciprocal(inv[:], row_sum[:, n, :]).then_inc(inv_ready, 1)
            dve.wait_ge(inv_ready, n + 1)
            nc.vector.tensor_tensor(inv[:], inv[:], gates[:, :, 3 * g + 1 + br], ALU.mult).then_inc(coef_ready, 1)
            dve.wait_ge(coef_ready, n + 1)
            ins = nc.vector.tensor_tensor(part[:], bank[:, 0:NQT * NSA_DIM].rearrange("p (t d) -> p t d", t=NQT),
                                          inv[:, :, None].to_broadcast([P, NQT, NSA_DIM]), ALU.mult)
            ins.then_inc(part_ready, 1)
            dve.wait_ge(part_ready, n + 1)
            cols = slice(g * NSA_DIM, (g + 1) * NSA_DIM)
            return nc.vector.tensor_tensor(o_acc[:, :, cols], o_acc[:, :, cols], part[:], ALU.add)

        on_act, on_dve, on_pe = attention(
            "nsa", NSA_HEADS, 2, float(NSA_DIM ** -0.5), ps[0:4], ps[4:6], ps[6:8], prob, prob_t, neg_max,
            lambda g, br: row_sum[:, 2 * g + br, :],
            query=lambda a, qt: q_n[(a // 2 % 2) * 64:(a // 2 % 2) * 64 + 64, a // 4, qt * P:(qt + 1) * P],
            keys=lambda a, w: k_two[a % 2][(a // 2 % 2) * 64:(a // 2 % 2) * 64 + 64, a // 8, 0:w],
            values=lambda a, kt: v_two[a % 2][:, kt, (a // 8) * NSA_DIM:(a // 8 + 1) * NSA_DIM],
            bias=lambda g, qt: dist[:, g, (NQT - 1 - qt) * P:SEQ], take=take)
        with nc.Block() as block:
            @block.gpsimd
            def _(pool):
                for hd in range(NSA_HEADS):
                    nc.gpsimd.tensor_scalar(dist[:, hd, :], rel, slope[:, hd:hd + 1], None, ALU.mult).then_inc(dist_ready, 1)

            @block.scalar
            def _(act):
                on_act(act)

            @block.vector
            def _(dve):
                dve.wait_ge(dist_ready, NSA_HEADS)
                on_dve(dve)

            @block.tensor
            def _(pe):
                on_pe(pe)

    with ExitStack() as tail:
        mix_hi = sb(tail, "mix_hi_od", [P, KT, SEQ], F32R)
        mix_lo = sb(tail, "mix_lo_od", [P, KT, SEQ], F32R)
        turned, hi_out = sem("od_turned"), sem("od_hi_out")
        with ExitStack() as ph:
            ps = banks(ph, "odmix")
            with nc.Block() as block:
                @block.tensor
                def _(pe):
                    for f in range(KT):
                        for qt in range(NQT):
                            tr = nc.tensor.transpose(ps[f][:, qt * P:(qt + 1) * P], o_acc[:, qt, f * P:(f + 1) * P], ident)
                        tr.then_inc(turned, 1)

                @block.scalar
                def _(act):
                    for f in range(KT):
                        act.wait_ge(turned, f + 1)
                        nc.scalar.activation(mix_hi[:, f, :], ps[f][:], ACT.Copy).then_inc(hi_out, 1)

                @block.vector
                def _(dve):
                    for f in range(KT):
                        dve.wait_ge(hi_out, f + 1)
                        nc.vector.tensor_tensor(mix_lo[:, f, :], ps[f][:], mix_hi[:, f, :].bitcast(F32), ALU.subtract)
        project_residual("od_out", mix_hi, mix_lo)
    att.close()
    odd.close()

    ffn(1)

    with ExitStack() as ph:
        sq, rstd = sb(ph, "sq_fin", [P, KT, SEQ]), sb(ph, "rstd_fin", [P, SEQ])
        ps = banks(ph, "fin")
        n_act, n_pe, _, _, rstd_ready = norm_parts(sq, rstd, ps[0], None)
        out_ready, stored = sem("out_ready"), sem("stored")
        gain = const("g_final")
        with nc.Block() as block:
            @block.scalar
            def _(act):
                n_act(act)

            @block.tensor
            def _(pe):
                n_pe(pe)

            @block.vector
            def _(dve):
                dve.wait_ge(norm_sems["rstd"], rstd_ready)
                for k in range(KT):
                    nc.vector.scalar_tensor_tensor(out=sq[:, k, :], in0=h[:, k, :], scalar=gain[:, k:k + 1],
                                                   in1=rstd[:], op0=ALU.mult, op1=ALU.mult).then_inc(out_ready, 1)

            @block.sync
            def _(sp):
                for k in range(KT):
                    sp.wait_ge(out_ready, k + 1)
                    sp.dma_start(out_t[:, k, :], sq[:, k, :]).then_inc(stored, 16)
                sp.wait_ge(stored, 16 * KT)
    whole.close()


def _unit(w, cols, k0=0):
    n = min(UK, w.shape[0] // P - k0)
    u = np.zeros((P, UK, UM * P), np.float32)
    u[:, :n] = w[k0 * P:(k0 + n) * P, cols:cols + UM * P].reshape(n, P, UM * P).transpose(1, 0, 2)
    return u.reshape(P, -1)


def _blocks(bs):
    u = np.zeros((P, UK * UM * P), np.float32)
    at = 0
    for b in bs:
        u[:, at:at + b.shape[1]] = b
        at += b.shape[1]
    return u


def _stream(a):
    w = a["ev_w_in"][0]
    zq = Q_RANK + KV_RANK + ROPE
    ba = zq + 4 * GDN_HEADS * GDN_D
    kr = w[:, Q_RANK + KV_RANK:zq]
    small = np.concatenate([w[:, ba:ba + 8], np.zeros((D_MODEL, 56), np.float32), kr,
                            kr[:, ROPE // 2:], kr[:, :ROPE // 2]], axis=1)
    units = [_unit(w, 0), _unit(w, 256), _unit(np.concatenate([w[:, 512:640], small], axis=1), 0)]
    units += [_unit(w, zq + 256 * j) for j in range(8)]
    uq = a["ev_w_uq"][0].reshape(3, P, MLA_HEADS, NOPE + ROPE)
    half = NOPE + ROPE // 2
    uq = np.concatenate([uq, uq[..., half:], uq[..., NOPE:half]], axis=-1)
    for heads in (range(5), range(5, 8)):
        units.append(_blocks([uq[k, :, hd] for hd in heads for k in range(3)]))
    ukv = a["ev_w_ukv"][0].reshape(2, P, MLA_HEADS, NOPE + MLA_V)
    units.append(_blocks([ukv[k, :, 2 * j:2 * j + 2, :NOPE].reshape(P, P) for j in range(4) for k in range(2)]
                         + [ukv[k, :, :, NOPE:].reshape(P, -1) for k in range(2)]))
    units += [_unit(a["ev_w_out"][0], 256 * j) for j in range(4)]

    def ffn(n):
        g, u, d = a["ffn_w_gate"][n], a["ffn_w_up"][n], a["ffn_w_down"][n]
        return [_unit(m, 256 * j) for j in range(FT // 2) for m in (g, u)] + \
               [_unit(d, 256 * j, UK * r) for j in range(KT // 2) for r in range(3)]
    units += ffn(0)
    w = a["od_w_in"][0]
    units += [_unit(w, 256 * j) for j in (0, 1, 2, 3, 4, 5, 6, 8, 7, 9)]
    units += [_unit(a[n][0], 0, UK * r) for n in ("od_w1_k", "od_w1_v") for r in range(2)]
    units += [_unit(a["od_w_out"][0], 256 * j) for j in range(4)]
    units += ffn(1)
    assert len(units) == N_UNITS
    return np.stack(units)


def _consts(a):
    c = np.zeros((P, N_COLS), np.float32)

    def put(name, v):
        s, e = COLS[name]
        c[:, s:e] = v
    i = np.arange(P)
    put("ident", np.eye(P, dtype=np.float32))
    put("utri", (i[:, None] <= i[None, :]).astype(np.float32))
    put("ones", 1.0)
    j_, i_ = i[:, None], i[None, :]
    put("level", np.concatenate([((i_ >> (l + 1) == j_ >> (l + 1)) & ((i_ >> l) % 2 == 1) & ((j_ >> l) % 2 == 0))
                                 for l in range(7)], axis=1).astype(np.float32))
    half = ROPE // 2
    inv = np.float32(10000.0) ** (-np.arange(half, dtype=np.float32) / np.float32(half))
    ang = np.arange(SEQ, dtype=np.float32)[None, :] * inv.astype(np.float32)[:, None]
    rope = np.zeros((P, SEQ), np.float32)
    rope[64:96] = np.concatenate([np.cos(ang)] * 2)
    rope[96:128] = np.concatenate([-np.sin(ang), np.sin(ang)])
    put("rope", rope)
    rel = np.arange(SEQ)[None, :] - (SEQ - P) - i[:, None]
    put("rel", np.where(rel <= 0, rel, NEG).astype(np.float32))
    put("causal", np.where(rel <= 0, 0.0, NEG).astype(np.float32))
    pos = (np.arange(NQT)[None, :] * P + i[:, None]).astype(np.float32)
    put("any_valid", (pos >= CMP_BLOCK - 1).astype(np.float32))
    slopes = (2.0 ** (-8.0 * np.arange(1, NSA_HEADS + 1, dtype=np.float32) / NSA_HEADS)).astype(np.float32)
    scale = np.float32(NSA_DIM ** 0.5)
    put("slope", (slopes * scale)[None, :])
    n = np.arange(NCMP)
    centre = (n * CMP_STRIDE + 0.5 * (CMP_BLOCK - 1)).astype(np.float32)
    valid = (n * CMP_STRIDE + CMP_BLOCK - 1)[None, None, :] <= pos[:, :, None]
    bias = (slopes * scale)[None, None, :, None] * (centre[None, None, None, :] - pos[:, :, None, None])
    bias = np.where(valid[:, :, None, :], bias, NEG).astype(np.float32)
    for name, v in (("g_ev", a["ev_attn_norm"][0]), ("g_od", a["od_attn_norm"][0]), ("g_ffn0", a["ffn_norm"][0]),
                    ("g_ffn1", a["ffn_norm"][1]), ("g_final", a["final_norm"]), ("g_q", a["ev_q_norm"][0]),
                    ("g_kv", a["ev_kv_norm"][0]), ("g_gdn", a["ev_gdn_norm"][0]),
                    ("pe_k", a["od_pe_k"][0].reshape(-1)), ("pe_v", a["od_pe_v"][0].reshape(-1))):
        put(name, v.reshape(-1, P).T)
    put("conv", a["ev_conv_w"][0].reshape(GDN_CONV, 12, P).transpose(2, 1, 0).reshape(P, -1))
    put("a_log", a["ev_a_log"])
    put("dt_bias", a["ev_dt_bias"])
    put("eps", EPS)
    g0 = NSA_HEADS * NSA_DIM + 6 * NSA_GROUPS * NSA_DIM
    put("w_gate", a["od_w_in"][0][:, g0:].reshape(KT, P, 48).transpose(1, 0, 2).reshape(P, -1))
    return c, bias.reshape(P, -1)


def kernel(**inputs):
    import concourse.bacc as bacc
    from concourse.bass_utils import run_bass_kernel_spmd

    a = {k: np.asarray(v) for k, v in inputs.items()}
    consts, cmp_bias = _consts(a)
    arrays = {
        "x_t": np.ascontiguousarray(a["x"][0].T.reshape(KT, P, SEQ).transpose(1, 0, 2)),
        "stream": _stream(a),
        "consts": consts,
        "cmp_bias": cmp_bias,
        "w2": np.ascontiguousarray(np.stack([a["od_w2_k"][0], a["od_w2_v"][0]]).reshape(2, 2, P, NSA_DIM)
                                   .transpose(2, 0, 1, 3).reshape(P, -1)),
    }
    nc = bacc.Bacc("TRN2", target_bir_lowering=False, num_devices=1, dynamic_dma_scratch_size=1024)
    args = [nc.dram_tensor(n, v.shape, mybir.dt.float32, kind="ExternalInput").ap() for n, v in arrays.items()]
    out = nc.dram_tensor("out_t", (P, KT, SEQ), mybir.dt.float32, kind="ExternalOutput").ap()
    build_program(nc, *args, out)
    res = run_bass_kernel_spmd(nc, [arrays], core_ids=[0])
    got = res.results[0]["out_t"]
    return np.ascontiguousarray(got.transpose(1, 0, 2).reshape(D_MODEL, SEQ).T)[None]
```

```python
import math
from contextlib import ExitStack

import numpy as np

import concourse.bass as bass
from concourse import mybir

D_MODEL, SEQ, EPS = 1024, 512, 1e-6
MLA_HEADS, Q_RANK, KV_RANK, NOPE, ROPE, MLA_V = 8, 384, 256, 64, 32, 64
GDN_HEADS, GDN_D, GDN_CONV = 4, 128, 4
NSA_HEADS, NSA_GROUPS, NSA_DIM = 16, 4, 64
NSA_HPG = NSA_HEADS // NSA_GROUPS
CMP_BLOCK, CMP_STRIDE, CMP_HIDDEN = 32, 16, 256
FFN_HIDDEN = ((8 * D_MODEL + 3 * 256 - 1) // (3 * 256)) * 256
P = 128
KT = D_MODEL // P
NQT = SEQ // P
FT = FFN_HIDDEN // P
UK, UM = 8, 2
NCMP = 32
NEG = -1e30
BIG = 3.0e38

UNITS = {}
_at = 0
for _name, _n in (("ev_in", 11), ("mla", 3), ("ev_out", 4), ("gu0", FT), ("down0", 12), ("od_in", 10),
                  ("cmp", 4), ("od_out", 4), ("gu1", FT), ("down1", 12)):
    UNITS[_name] = (_at, _at + _n)
    _at += _n
N_UNITS = _at

COLS = {}
_at = 0
for _name, _n in (("ident", P), ("utri", P), ("ones", P), ("level", 7 * P), ("rope", SEQ),
                  ("rel", SEQ), ("causal", SEQ), ("any_valid", NQT),
                  ("g_ev", KT), ("g_od", KT), ("g_ffn0", KT), ("g_ffn1", KT), ("g_final", KT),
                  ("g_q", 3), ("g_kv", 2), ("g_gdn", 1), ("conv", 12 * GDN_CONV), ("a_log", GDN_HEADS),
                  ("dt_bias", GDN_HEADS), ("eps", 1), ("slope", NSA_HEADS), ("pe_k", 16), ("pe_v", 16), ("w_gate", KT * 48)):
    COLS[_name] = (_at, _at + _n)
    _at += _n
N_COLS = _at


def build_program(nc, x_t, stream, consts, cmp_bias_in, w2_in, out_t, dbg=None):
    F32, F32R = mybir.dt.float32, mybir.dt.float32r
    ACT, ALU, AX = mybir.ActivationFunctionType, mybir.AluOpType, mybir.AxisListType
    whole = ExitStack()

    def sb(ctx, name, shape, dt=F32, side=None):
        return ctx.enter_context(nc.sbuf_tensor(name, shape, dt, side=side))

    def banks(ctx, tag):
        return [ctx.enter_context(nc.psum_tensor(f"ps_{tag}{i}", [P, 512], F32)) for i in range(8)]

    sem_of = {}

    def sem(name):
        sem_of[name] = whole.enter_context(nc.semaphore(name))
        return sem_of[name]

    cst = sb(whole, "cst", [P, N_COLS])
    h = sb(whole, "h", [P, KT, SEQ])
    raw = sb(whole, "raw", [P, 2, UK * UM * P])
    whi = sb(whole, "whi", [P, 2, UK * UM * P], F32R)
    wlo = sb(whole, "wlo", [P, 2, UK * UM * P], F32R)

    def const(name, rows=slice(0, P)):
        a, b = COLS[name]
        return cst[rows, a:b]

    ident, utri, ones = const("ident"), const("utri"), const("ones")
    eps = const("eps")

    unit_landed = [sem("unit_landed0"), sem("unit_landed1")]
    hi_ready, lo_ready, tiles_done = sem("hi_ready"), sem("lo_ready"), sem("tiles_done")

    def load_unit(sp, u, slot, landed):
        sp.wait_ge(lo_ready, u - 1)
        sp.dma_start(raw[:, slot, :], stream[u]).then_inc(landed, 16)

    def load_units(sp, name):
        a, b = UNITS[name][0] + 2, min(UNITS[name][1] + 2, N_UNITS)
        pairs = (b - a) // 2
        if pairs == 1:
            load_unit(sp, a, a % 2, unit_landed[a % 2])
            load_unit(sp, a + 1, (a + 1) % 2, unit_landed[(a + 1) % 2])
        elif pairs:
            with sp.Fori(0, pairs) as i:
                for s in range(2):
                    load_unit(sp, a + s + 2 * i, (a + s) % 2, unit_landed[(a + s) % 2])
        if (b - a) % 2:
            load_unit(sp, b - 1, (b - 1) % 2, unit_landed[(b - 1) % 2])

    def split_hi(act, base, i):
        s = base % 2
        act.wait_ge(unit_landed[s], 16 * (base // 2 + 1) + 16 * i)
        if not (isinstance(i, int) and base + 2 * i < 2):
            act.wait_ge(tiles_done, 2 * (base - 1) + 4 * i)
        nc.scalar.activation(whi[:, s, :], raw[:, s, :], ACT.Copy).then_inc(hi_ready, 1)

    def split_lo(pool, base, i):
        s = base % 2
        pool.wait_ge(hi_ready, base + 1 + 2 * i)
        nc.gpsimd.tensor_tensor(wlo[:, s, :], raw[:, s, :], whi[:, s, :].bitcast(F32),
                                ALU.subtract).then_inc(lo_ready, 1)

    def split_los(pool, name):
        a, b = UNITS[name][0] + 1, min(UNITS[name][1] + 1, N_UNITS)
        if (b - a) // 2 == 1:
            split_lo(pool, a, 0)
            split_lo(pool, a + 1, 0)
        elif (b - a) // 2:
            with pool.Fori(0, (b - a) // 2) as i:
                split_lo(pool, a, i)
                split_lo(pool, a + 1, i)
        if (b - a) % 2:
            split_lo(pool, b - 1, 0)

    def three_passes(acc, lhs_hi, lhs_lo, rhs_hi, rhs_lo, start, stop):
        nc.tensor.matmul(acc, lhs_hi, rhs_hi, start=start, stop=False)
        nc.tensor.matmul(acc, lhs_hi, rhs_lo, start=False, stop=False)
        return nc.tensor.matmul(acc, lhs_lo, rhs_hi, start=False, stop=stop)

    def unit_block(s, k, m):
        c = (k * UM + m) * P
        return whi[:, s, c:c + P], wlo[:, s, c:c + P]

    def column_tile(acc, s, m, x_hi, x_lo, k0=0, nk=UK, first=True, last=True):
        for k in range(nk):
            w_hi, w_lo = unit_block(s, k, m)
            mm = three_passes(acc, w_hi, w_lo, x_hi[:, k0 + k, :], x_lo[:, k0 + k, :],
                              first and k == 0, last and k == nk - 1)
        return mm

    norm_sems = {n: sem("norm_" + n) for n in ("sq", "summed", "ms", "ln", "rstd", "xn", "xh", "xl")}
    sumsq = sb(whole, "sumsq", [P, SEQ])
    norms, sums = [0], [0]

    def square_sum(sq2):
        n = sums[0]
        sums[0] += 1
        s = norm_sems
        SQ, SM = KT * n, (KT + 1) * n

        def clear(dve):
            if n:
                dve.wait_ge(s["xn"], KT * n)
            nc.vector.memset(sumsq[:], 0.0).then_inc(s["summed"], 1)

        def square(act, t):
            if t >= 2:
                act.wait_ge(s["summed"], SM + t)
            nc.scalar.activation(sq2[:, t % 2, :], h[:, t, :], ACT.Square).then_inc(s["sq"], 1)

        def add(dve, t):
            dve.wait_ge(s["sq"], SQ + t + 1)
            dve.wait_ge(s["summed"], SM + t + 1)
            nc.vector.tensor_tensor(sumsq[:], sumsq[:], sq2[:, t % 2, :], ALU.add).then_inc(s["summed"], 1)
        return clear, square, add

    def keep_busy(bank, n):
        for _ in range(n):
            nc.tensor.matmul(bank[:], ones, cst[:, 0:512], start=True, stop=True)

    def norm_parts(xn, bank, gain, xh=None, xl=None):
        n = norms[0]
        norms[0] += 1
        nk = KT * n
        s = norm_sems

        def on_act(act):
            act.wait_ge(s["ms"], n + 1)
            nc.scalar.activation(sumsq[:], bank[:], ACT.Ln, bias=eps, scale=1.0 / D_MODEL).then_inc(s["ln"], 1)
            act.wait_ge(s["ln"], n + 1)
            nc.scalar.activation(sumsq[:], sumsq[:], ACT.Exp, scale=-0.5).then_inc(s["rstd"], 1)
            if xh is not None:
                for k in range(KT):
                    act.wait_ge(s["xn"], nk + k + 1)
                    nc.scalar.activation(xh[:, k, :], xn[:, k, :], ACT.Copy).then_inc(s["xh"], 1)

        def on_pe(pe):
            pe.wait_ge(s["summed"], (KT + 1) * (n + 1))
            nc.tensor.matmul(bank[:], ones, sumsq[:], start=True, stop=True).then_inc(s["ms"], 1)

        def on_dve(dve):
            def lo(k):
                dve.wait_ge(s["xh"], nk + k + 1)
                nc.vector.tensor_tensor(xl[:, k, :], xn[:, k, :], xh[:, k, :].bitcast(F32),
                                        ALU.subtract).then_inc(s["xl"], 1)
            dve.wait_ge(s["rstd"], n + 1)
            for k in range(KT):
                nc.vector.scalar_tensor_tensor(out=xn[:, k, :], in0=h[:, k, :], scalar=gain[:, k:k + 1],
                                               in1=sumsq[:], op0=ALU.mult, op1=ALU.mult).then_inc(s["xn"], 1)
                if xh is not None and k:
                    lo(k - 1)
            if xh is not None:
                lo(KT - 1)

        def wait_tile(pe, k):
            pe.wait_ge(s["xl"], nk + k + 1)

        return on_act, on_pe, on_dve, wait_tile, nk

    def first_unit(pe, u, banks2, xh, xl, wait_tile):
        pe.wait_ge(lo_ready, u + 1)
        for k in range(KT):
            wait_tile(pe, k)
            for m in range(2):
                w_hi, w_lo = unit_block(u % 2, k, m)
                mm = three_passes(banks2[m][:], w_hi, w_lo, xh[:, k, :], xl[:, k, :], k == 0, k == KT - 1)
                if k == KT - 1:
                    mm.then_inc(tiles_done, 1)

    def attention(tag, n_groups, per_group, c, s_banks, t_banks, o_banks, prob, prob_t, neg_max, row_sum,
                  query, keys, values, bias, take, bias_ready=None):
        n_heads = n_groups * per_group
        n_items = NQT * n_heads
        scores_done, biased = sem(f"scores_{tag}"), sem(f"biased_{tag}")
        probs_ready, turned = sem(f"probs_{tag}"), sem(f"turned_{tag}")
        copied = [sem(f"copied_even_{tag}"), sem(f"copied_odd_{tag}")]
        pv_done, o_taken = sem(f"pv_{tag}"), sem(f"o_taken_{tag}")
        LAG = 3

        def width(qt):
            return (qt + 1) * P

        def copy(engine, do, a, qt):
            engine.wait_ge(turned, NQT * a + qt + 1)
            if not (isinstance(a, int) and NQT * a + qt < 2):
                engine.wait_ge(pv_done, NQT * a + qt - 1)
            do(prob_t[:, qt % 2, 0:width(qt)], t_banks[qt % 2][:, 0:width(qt)]).then_inc(copied[qt % 2], 1)

        def act_copy(out, in_):
            return nc.scalar.activation(out, in_, ACT.Copy)

        def on_act(act):
            def group(g, first):
                for br in range(per_group):
                    a = per_group * g + br
                    for qt in range(NQT):
                        act.wait_ge(biased, NQT * a + qt + 1)
                        nc.scalar.activation(prob[:, qt, 0:width(qt)], prob[:, qt, 0:width(qt)], ACT.Exp,
                                             bias=neg_max[:, qt:qt + 1], scale=-1.0,
                                             accum_out=row_sum(g, br)[:, qt:qt + 1]).then_inc(probs_ready, 1)
                        if qt == 1 and not (first and br == 0):
                            copy(act, act_copy, a - 1, 2)
                        if qt == 3:
                            copy(act, act_copy, a, 0)
            group(0, True)
            with act.Fori(1, n_groups) as g:
                group(g, False)
            copy(act, act_copy, n_heads - 1, 2)

        def on_dve(dve):
            def group(g, first):
                if bias_ready is not None:
                    dve.wait_ge(bias_ready, g + 1)
                for br in range(per_group):
                    a = per_group * g + br
                    for qt in range(NQT):
                        dve.wait_ge(scores_done, NQT * a + qt + 1)
                        if not (first and br == 0):
                            dve.wait_ge(turned, NQT * a + qt - 3)
                        nc.vector.tensor_tensor_reduce(
                            out=prob[:, qt, 0:width(qt)], in0=s_banks[qt][:, 0:width(qt)], in1=bias(g, qt),
                            scale=-c, scalar=BIG, op0=ALU.add, op1=ALU.min,
                            accum_out=neg_max[:, qt:qt + 1]).then_inc(biased, 1)
                        if qt == 2 and a:
                            copy(dve, nc.vector.tensor_copy, a - 1, 3)
                        if qt == 0 and a:
                            copy(dve, nc.vector.tensor_copy, a - 1, 1)
                            if a >= 2:
                                dve.wait_ge(pv_done, NQT * (a - 1))
                                gb = divmod(a - 2, per_group)
                                take(dve, *gb, o_banks[gb[1]]).then_inc(o_taken, 1)
            for g in range(n_groups):
                group(g, g == 0)
            for qt in (1, 3):
                copy(dve, nc.vector.tensor_copy, n_heads - 1, qt)
            for a in (n_heads - 2, n_heads - 1):
                dve.wait_ge(pv_done, NQT * (a + 1))
                gb = divmod(a, per_group)
                take(dve, *gb, o_banks[gb[1]]).then_inc(o_taken, 1)

        def on_pe(pe):
            for t in range(n_items + LAG + 1):
                if t < n_items:
                    a, qt = divmod(t, NQT)
                    if t >= 4:
                        pe.wait_ge(biased, t - 3)
                    nc.tensor.matmul(s_banks[qt][:, 0:width(qt)], query(a, qt), keys(a, width(qt)),
                                     start=True, stop=True).then_inc(scores_done, 1)
                if LAG <= t < n_items + LAG:
                    a, qt = divmod(t - LAG, NQT)
                    pe.wait_ge(probs_ready, t - LAG + 1)
                    if t >= LAG + 2:
                        pe.wait_ge(copied[qt % 2], (t - LAG - 2) // 2 + 1)
                    for kt in range(qt + 1):
                        tr = nc.tensor.transpose(t_banks[qt % 2][:, kt * P:(kt + 1) * P],
                                                 prob[:, qt, kt * P:(kt + 1) * P], ident)
                    tr.then_inc(turned, 1)
                if t > LAG:
                    a, qt = divmod(t - LAG - 1, NQT)
                    pe.wait_ge(copied[qt % 2], (t - LAG - 1) // 2 + 1)
                    if qt == 0 and a >= 2:
                        pe.wait_ge(o_taken, a - 1)
                    for kt in range(qt + 1):
                        pv = nc.tensor.matmul(o_banks[a % 2][:, qt * P:(qt + 1) * P],
                                              prob_t[:, qt % 2, kt * P:(kt + 1) * P], values(a, kt),
                                              start=(kt == 0), stop=(kt == qt))
                    pv.then_inc(pv_done, 1)
        return on_act, on_dve, on_pe

    even, even_in = ExitStack(), ExitStack()
    zg = sb(even, "zg", [P, GDN_HEADS, SEQ])
    misc = sb(even, "misc", [P, SEQ])
    qkv = sb(even, "qkv", [P, 12, SEQ])
    lat = sb(even_in, "lat", [P, 5, SEQ])

    in_landed = sem("in_landed")
    with ExitStack() as ph:
        xh, xl = sb(ph, "xh_ev", [P, KT, SEQ], F32R), sb(ph, "xl_ev", [P, KT, SEQ], F32R)
        xn, sq2 = sb(ph, "xn_ev", [P, KT, SEQ]), sb(ph, "sq2_ev", [P, 2, SEQ])
        ps = banks(ph, "evin")
        clear, square, add_square = square_sum(sq2)
        n_act, n_pe, n_dve, wait_tile, _ = norm_parts(xn, ps[4], const("g_ev"), xh, xl)
        z = sb(ph, "z", [P, 4, SEQ + 4])
        conv_w = const("conv")
        conv_step, conv_ready, padded_z = sem("conv_step"), sem("conv_ready"), sem("padded_z")
        out_a, out_v = sem("evin_out_act"), sem("evin_out_dve")
        with nc.Block() as block:
            @block.sync
            def _(sp):
                sp.dma_start(cst[:], consts).then_inc(in_landed, 16)
                sp.dma_start(h[:], x_t).then_inc(in_landed, 16)
                sp.dma_start(raw[:, 0, :], stream[0]).then_inc(unit_landed[0], 16)
                sp.dma_start(raw[:, 1, :], stream[1]).then_inc(unit_landed[1], 16)
                load_units(sp, "ev_in")

            @block.gpsimd
            def _(pool):
                nc.gpsimd.memset(z[:, :, 0:3], 0.0).then_inc(padded_z, 1)
                split_lo(pool, 0, 0)
                split_los(pool, "ev_in")

            def out_of(t):
                return lat[:, t, :] if t < 5 else misc[:]

            @block.scalar
            def _(act):
                act.preload_act_table_set("natural_log_exp_and_others")
                act.wait_ge(in_landed, 32)
                for t in range(KT):
                    square(act, t)
                split_hi(act, 0, 0)
                n_act(act)
                for u in range(3):
                    split_hi(act, u + 1, 0)
                    act.wait_ge(tiles_done, 2 * u + 1)
                    nc.scalar.activation(out_of(2 * u), ps[2 * u % 4][:], ACT.Copy).then_inc(out_a, 1)

                act.preload_act_table(ACT.Silu)

                def silu(t, i):
                    act.wait_ge(conv_ready, t + 1 + 4 * i)
                    tile = qkv[:, t + 4 * i, :]
                    nc.scalar.activation(tile, tile, ACT.Silu)

                def z_unit(i, s):
                    split_hi(act, 4 + s, i)
                    act.wait_ge(tiles_done, 6 + 2 * s + 1 + 4 * i)
                    if not isinstance(i, int):
                        act.wait_ge(conv_ready, 4 * i + 2 * s - 3)
                    nc.scalar.activation(z[:, 2 * s, 3:3 + SEQ], ps[(2 + 2 * s) % 4][:], ACT.Copy).then_inc(out_a, 1)
                    if s or not isinstance(i, int):
                        for m in range(2):
                            silu(2 * s - 2 + m, i)
                for s in range(2):
                    z_unit(0, s)
                with act.Fori(1, 3) as i:
                    for s in range(2):
                        z_unit(i, s)
                for s in range(2):
                    split_hi(act, 10 + s, 0)
                    for m in range(2):
                        act.wait_ge(tiles_done, 18 + 2 * s + m + 1)
                        nc.scalar.activation(zg[:, 2 * s + m, :], ps[(2 + 2 * s) % 4 + m][:], ACT.Silu)
                    if s == 0:
                        for m in range(2):
                            silu(10 + m, 0)

            @block.vector
            def _(dve):
                clear(dve)
                dve.wait_ge(in_landed, 32)
                for t in range(KT):
                    add_square(dve, t)
                n_dve(dve)
                for u in range(3):
                    dve.wait_ge(tiles_done, 2 * u + 2)
                    nc.vector.tensor_copy(out_of(2 * u + 1), ps[(2 * u + 1) % 4][:]).then_inc(out_v, 1)

                dve.wait_ge(padded_z, 1)

                def z_unit(i, s):
                    dve.wait_ge(tiles_done, 6 + 2 * s + 2 + 4 * i)
                    if not isinstance(i, int):
                        dve.wait_ge(conv_ready, 4 * i + 2 * s - 2)
                    nc.vector.tensor_copy(z[:, 2 * s + 1, 3:3 + SEQ], ps[(3 + 2 * s) % 4][:]).then_inc(out_v, 1)
                    dve.wait_ge(out_a, 4 + s + 2 * i)
                    dve.wait_ge(out_v, 4 + s + 2 * i)
                    for m in range(2):
                        t = 4 * i + 2 * s + m
                        w = conv_w[:, bass.ds(t * GDN_CONV, GDN_CONV)]
                        tile = z[:, 2 * s + m, :]
                        nc.vector.tensor_scalar(qkv[:, t, :], tile[:, 0:SEQ], w[:, 0:1], None, ALU.mult).then_inc(conv_step, 1)
                        for j in range(1, GDN_CONV):
                            dve.wait_ge(conv_step, 3 * t + j)
                            nc.vector.scalar_tensor_tensor(out=qkv[:, t, :], in0=tile[:, j:j + SEQ], scalar=w[:, j:j + 1],
                                                           in1=qkv[:, t, :], op0=ALU.mult, op1=ALU.add
                                                           ).then_inc(conv_step if j < GDN_CONV - 1 else conv_ready, 1)
                for s in range(2):
                    z_unit(0, s)
                with dve.Fori(1, 3) as i:
                    for s in range(2):
                        z_unit(i, s)

            @block.tensor
            def _(pe):
                pe.wait_ge(in_landed, 32)
                keep_busy(ps[5], 3)
                n_pe(pe)
                keep_busy(ps[5], 2)

                def unit(u, i):
                    pe.wait_ge(lo_ready, u + 1 + 2 * i)
                    b = 2 * (u % 2)
                    if not (isinstance(i, int) and u < 2):
                        pe.wait_ge(out_a, u - 1 + 2 * i)
                        pe.wait_ge(out_v, u - 1 + 2 * i)
                    column_tile(ps[b][:], u % 2, 0, xh, xl).then_inc(tiles_done, 1)
                    column_tile(ps[b + 1][:], u % 2, 1, xh, xl).then_inc(tiles_done, 1)

                first_unit(pe, 0, ps[0:2], xh, xl, wait_tile)
                for u in range(1, 3):
                    unit(u, 0)
                with pe.Fori(0, 4) as i:
                    unit(3, i)
                    unit(4, i)

    mla = ExitStack()
    q_all = sb(mla, "q_all", [96, MLA_HEADS, SEQ], side="right")
    k_all = sb(mla, "k_all", [96, MLA_HEADS, SEQ], side="right")
    v_all = sb(mla, "v_all", [P, NQT, MLA_HEADS * MLA_V], side="right")
    with ExitStack() as ph:
        lat_hi, lat_lo = sb(ph, "lat_hi", [P, 5, SEQ], F32R), sb(ph, "lat_lo", [P, 5, SEQ], F32R)
        sq, rstd = sb(ph, "sq_lat", [P, 5, SEQ]), sb(ph, "rstd_lat", [P, 2, SEQ])
        rot_a, rot_b = sb(ph, "rot_a", [P, 2, SEQ]), sb(ph, "rot_b", [P, 2, SEQ])
        ps = banks(ph, "lat")
        g_lat = cst[:, COLS["g_q"][0]:COLS["g_kv"][1]]
        rope = const("rope")
        lat_sq, lat_ms, lat_ln, lat_rstd = sem("lat_sq"), sem("lat_ms"), sem("lat_ln"), sem("lat_rstd")
        lat_scaled, lat_hi_ready, lat_ready = sem("lat_scaled"), sem("lat_hi_ready"), sem("lat_ready")
        head_done, nope_out, rot_done, rope_out = sem("head_done"), sem("nope_out"), sem("rot_done"), sem("rope_out")
        kr_mul, kr_ready, kr_out = sem("kr_mul"), sem("kr_ready"), sem("kr_out")
        kv_done, kv_out_a, kv_out_v = sem("kv_done"), sem("kv_out_act"), sem("kv_out_dve")
        U = UNITS["mla"][0]
        PARTS = ((0, 3, Q_RANK), (3, 5, KV_RANK))

        def wait_head(e, hd):
            if hd == 4:
                e.wait_ge(tiles_done, 2 * (U + 1))
            elif hd == 7:
                e.wait_ge(tiles_done, 2 * (U + 2))
            else:
                e.wait_ge(head_done, hd + 1 - (hd > 4))

        with nc.Block() as block:
            @block.sync
            def _(sp):
                load_units(sp, "mla")

            @block.gpsimd
            def _(pool):
                split_los(pool, "mla")
                pool.wait_ge(lo_ready, UNITS["mla"][1] + 1)
                pool.wait_ge(kr_mul, 2)
                for hd in range(MLA_HEADS):
                    nc.gpsimd.tensor_tensor(k_all[64:96, hd, :], rot_a[64:96, 1, :], rot_b[64:96, 1, :],
                                            ALU.add).then_inc(kr_out, 1)

            @block.scalar
            def _(act):
                act.preload_act_table_set("natural_log_exp_and_others")
                for t in range(5):
                    nc.scalar.activation(sq[:, t, :], lat[:, t, :], ACT.Square).then_inc(lat_sq, 1)
                split_hi(act, U + 1, 0)
                for n, (a, b, rank) in enumerate(PARTS):
                    act.wait_ge(lat_ms, n + 1)
                    nc.scalar.activation(rstd[:, n, :], ps[n][:], ACT.Ln, bias=eps,
                                         scale=1.0 / rank).then_inc(lat_ln, 1)
                act.wait_ge(lat_ln, 2)
                for n in range(2):
                    nc.scalar.activation(rstd[:, n, :], rstd[:, n, :], ACT.Exp, scale=-0.5).then_inc(lat_rstd, 1)
                for t in range(5):
                    act.wait_ge(lat_scaled, t + 1)
                    nc.scalar.activation(lat_hi[:, t, :], sq[:, t, :], ACT.Copy,
                                         scale=g_lat[:, t:t + 1]).then_inc(lat_hi_ready, 1)
                for hd in range(MLA_HEADS):
                    wait_head(act, hd)
                    nc.scalar.activation(q_all[0:64, hd, :], ps[2 + hd % 2][0:64, :], ACT.Copy).then_inc(nope_out, 1)
                    if hd == 4:
                        split_hi(act, U + 2, 0)
                    if hd == 7:
                        split_hi(act, U + 3, 0)
                for j in range(4):
                    act.wait_ge(kv_done, j + 1)
                    nc.scalar.activation(k_all[0:64, 2 * j, :], ps[4 + j % 2][0:64, :], ACT.Copy).then_inc(kv_out_a, 1)
                for tt in range(0, NQT, 2):
                    act.wait_ge(kv_done, 4 + tt + 1)
                    nc.scalar.activation(v_all[:, tt, :], ps[4 + tt % 2][:], ACT.Copy).then_inc(kv_out_a, 1)

            @block.vector
            def _(dve):
                nc.vector.tensor_tensor(rot_a[64:96, 1, :], misc[64:96, :], rope[64:96, :], ALU.mult).then_inc(kr_mul, 1)
                nc.vector.tensor_tensor(rot_b[64:96, 1, :], misc[96:128, :], rope[96:128, :], ALU.mult).then_inc(kr_mul, 1)
                for n, (a, b, rank) in enumerate(PARTS):
                    dve.wait_ge(lat_rstd, n + 1)
                    for t in range(a, b):
                        nc.vector.tensor_tensor(sq[:, t, :], lat[:, t, :], rstd[:, n, :], ALU.mult).then_inc(lat_scaled, 1)
                for t in range(5):
                    dve.wait_ge(lat_hi_ready, t + 1)
                    nc.vector.scalar_tensor_tensor(out=lat_lo[:, t, :], in0=sq[:, t, :], scalar=g_lat[:, t:t + 1],
                                                   in1=lat_hi[:, t, :].bitcast(F32), op0=ALU.mult,
                                                   op1=ALU.subtract).then_inc(lat_ready, 1)
                for hd in range(MLA_HEADS):
                    wait_head(dve, hd)
                    if hd:
                        dve.wait_ge(rope_out, hd)
                    b = ps[2 + hd % 2]
                    nc.vector.tensor_tensor(rot_a[64:96, 0, :], b[64:96, :], rope[64:96, :], ALU.mult).then_inc(rot_done, 1)
                    nc.vector.tensor_tensor(rot_b[64:96, 0, :], b[96:128, :], rope[96:128, :], ALU.mult).then_inc(rot_done, 1)
                    dve.wait_ge(rot_done, 2 * hd + 2)
                    nc.vector.tensor_tensor(q_all[64:96, hd, :], rot_a[64:96, 0, :], rot_b[64:96, 0, :],
                                            ALU.add).then_inc(rope_out, 1)
                for j in range(4):
                    dve.wait_ge(kv_done, j + 1)
                    nc.vector.tensor_copy(k_all[0:64, 2 * j + 1, :], ps[4 + j % 2][64:128, :]).then_inc(kv_out_v, 1)
                for tt in range(1, NQT, 2):
                    if tt == 3:
                        dve.wait_ge(tiles_done, 2 * (U + 3))
                    else:
                        dve.wait_ge(kv_done, 4 + tt + 1)
                    nc.vector.tensor_copy(v_all[:, tt, :], ps[4 + tt % 2][:]).then_inc(kv_out_v, 1)

            @block.tensor
            def _(pe):
                for n, (a, b, rank) in enumerate(PARTS):
                    for t in range(a, b):
                        pe.wait_ge(lat_sq, t + 1)
                        mm = nc.tensor.matmul(ps[n][:], ones, sq[:, t, :], start=(t == a), stop=(t == b - 1))
                    mm.then_inc(lat_ms, 1)
                pe.wait_ge(lat_ready, 5)
                for hd in range(MLA_HEADS):
                    s = (U + (hd > 4)) % 2
                    pe.wait_ge(lo_ready, U + (hd > 4) + 1)
                    if hd >= 2:
                        pe.wait_ge(nope_out, hd - 1)
                        pe.wait_ge(rope_out, hd - 1)
                    for k in range(3):
                        c = (3 * (hd - 5 * (hd > 4)) + k) * P
                        mm = three_passes(ps[2 + hd % 2][:], whi[:, s, c:c + P], wlo[:, s, c:c + P],
                                          lat_hi[:, k, :], lat_lo[:, k, :], k == 0, k == 2)
                    if hd in (4, 7):
                        mm.then_inc(tiles_done, 2)
                    else:
                        mm.then_inc(head_done, 1)
                s = (U + 2) % 2
                pe.wait_ge(lo_ready, U + 3)
                for j in range(4):
                    if j >= 2:
                        pe.wait_ge(kv_out_a, j - 1)
                        pe.wait_ge(kv_out_v, j - 1)
                    for k in range(2):
                        c = (2 * j + k) * P
                        mm = three_passes(ps[4 + j % 2][:], whi[:, s, c:c + P], wlo[:, s, c:c + P],
                                          lat_hi[:, 3 + k, :], lat_lo[:, 3 + k, :], k == 0, k == 1)
                    mm.then_inc(kv_done, 1)
                for tt in range(NQT):
                    if tt < 2:
                        pe.wait_ge(kv_out_a, 3 + tt)
                        pe.wait_ge(kv_out_v, 3 + tt)
                    elif tt == 2:
                        pe.wait_ge(kv_out_a, 5)
                    else:
                        pe.wait_ge(kv_out_v, 5)
                    tok = slice(tt * P, (tt + 1) * P)
                    for k in range(2):
                        c = (8 + 4 * k) * P
                        mm = three_passes(ps[4 + tt % 2][:], lat_hi[:, 3 + k, tok], lat_lo[:, 3 + k, tok],
                                          whi[:, s, c:c + 512], wlo[:, s, c:c + 512], k == 0, k == 1)
                    if tt == 3:
                        mm.then_inc(tiles_done, 2)
                    else:
                        mm.then_inc(kv_done, 1)
    even_in.close()

    mix_hi = sb(even, "mix_hi", [P, KT, SEQ], F32R)
    mix_lo = sb(even, "mix_lo", [P, KT, SEQ], F32R)
    with ExitStack() as ph:
        prob, prob_t = sb(ph, "prob_m", [P, NQT, SEQ]), sb(ph, "prob_t_m", [P, 2, SEQ])
        neg_max, row_sum = sb(ph, "neg_max_m", [P, NQT]), sb(ph, "row_sum_m", [P, MLA_HEADS, NQT])
        inv = sb(ph, "inv_m", [P, NQT])
        o_nat = sb(ph, "o_nat", [P, NQT, MLA_HEADS * MLA_V])
        ps = banks(ph, "mla")
        causal = const("causal")
        inv_ready, o_scaled, mix_turned, mix_hi_out, mix_lo_out = (
            sem("m_inv"), sem("m_scaled"), sem("m_turned"), sem("m_hi_out"), sem("m_lo_out"))

        def take(dve, g, br, bank):
            a = 2 * g + br
            if a:
                dve.wait_ge(sem_of["o_taken_mla"], a)
            nc.vector.reciprocal(inv[:], row_sum[:, a, :]).then_inc(inv_ready, 1)
            dve.wait_ge(inv_ready, a + 1)
            return nc.vector.tensor_tensor(o_nat[:, :, bass.ts(a, MLA_V)],
                                           bank[:].rearrange("p (t d) -> p t d", t=NQT)[:, :, br * MLA_V:(br + 1) * MLA_V],
                                           inv[:, :, None].to_broadcast([P, NQT, MLA_V]), ALU.mult)

        with nc.Block() as block:
            on_act, on_dve, on_pe = attention(
                "mla", MLA_HEADS // 2, 2, float((NOPE + ROPE) ** -0.5), ps[0:4], ps[4:6], ps[6:8], prob, prob_t,
                neg_max, lambda g, br: row_sum[:, 2 * g + br, :],
                query=lambda a, qt: q_all[:, a, qt * P:(qt + 1) * P],
                keys=lambda a, w: k_all[:, a, 0:w],
                values=lambda a, kt: v_all[:, kt, a // 2 * P:(a // 2 + 1) * P],
                bias=lambda g, qt: causal[:, (NQT - 1 - qt) * P:SEQ], take=take)

            @block.scalar
            def _(act):
                on_act(act)
                for f in range(4):
                    act.wait_ge(mix_turned, f + 1)
                    nc.scalar.activation(mix_hi[:, f, :], ps[f][:], ACT.Copy).then_inc(mix_hi_out, 1)

            @block.vector
            def _(dve):
                on_dve(dve)
                for f in range(4):
                    dve.wait_ge(mix_hi_out, f + 1)
                    nc.vector.tensor_tensor(mix_lo[:, f, :], ps[f][:], mix_hi[:, f, :].bitcast(F32),
                                            ALU.subtract).then_inc(mix_lo_out, 1)

            @block.tensor
            def _(pe):
                on_pe(pe)
                pe.wait_ge(sem_of["o_taken_mla"], MLA_HEADS)
                for f in range(4):
                    for qt in range(NQT):
                        tr = nc.tensor.transpose(ps[f][:, qt * P:(qt + 1) * P], o_nat[:, qt, f * P:(f + 1) * P], ident)
                    tr.then_inc(mix_turned, 1)
    mla.close()

    NC, HD, C = NQT, GDN_HEADS, P
    with ExitStack() as ph:
        def tile(name, *shape):
            return sb(ph, name, [P, *shape])
        ba = tile("g_ba", NC, 8)
        col = {n: tile("g_" + n, NC, HD) for n in ("beta", "soft", "tmp", "g", "gc", "egc", "bg", "last", "kd", "elast", "ea", "nbeta")}
        norm = tile("g_norm", 2, 512)
        kbg, kdec, vb = (tile("g_" + n, NC, HD * C) for n in ("kbg", "kdec", "vb"))
        nat, intra = tile("g_nat", NC, HD * C), tile("g_intra", NC, HD * C)
        t_, tt_ = tile("g_t", NC, HD * C), tile("g_tt", NC, HD * C)
        dec = tile("g_dec", 2, HD * C)
        xb = tile("g_x", 2, HD * C)
        off = tile("g_off", 2, HD * C)
        state = tile("g_state", HD * C)
        vn = tile("g_vn", HD * C)
        ps = banks(ph, "gdn")
        vrows = const("level")

        def heads(ap):
            return ap.rearrange("p (h c) -> p h c", h=HD)

        def over(c4):
            return c4[:, :, None].to_broadcast([P, HD, C])

        def per_head(mat):
            return mat[:, None, :].to_broadcast([P, HD, C])

        def chained(engine, s):
            n = [0]

            def step(ins):
                ins.then_inc(s, 1)
                n[0] += 1
                engine.wait_ge(s, n[0])
            return step
        E_SEMS = {n: sem("gdn_" + n) for n in (
            "sq", "ms", "ln", "rs", "normed", "ba_turned", "ba_out", "act_col", "dve_col", "g_ready", "gc_done", "gc_out",
            "rows_done", "diff", "dec", "dec_masked", "decb", "pairs_done", "nat_out", "intra_out", "qd_row", "qd_out",
            "k_turned", "k_out", "v_turned", "v_out", "off_ready", "x_done", "x_out", "u_done", "t_out", "tt_out",
            "w_done", "w_out", "vn_done", "vn_out", "o_done", "o_out", "s_done", "s_out", "o_sq", "o_ms", "o_ln", "o_rs",
            "y1", "y2", "y_hi", "y_lo", "id_out")}
        S_ = E_SEMS
        with nc.Block() as block:
            @block.scalar
            def _(act):
                act.preload_act_table_set("natural_log_exp_and_others")
                for n in range(10):
                    if n < 8:
                        if n >= 2:
                            act.wait_ge(S_["ms"], n - 1)
                        nc.scalar.activation(xb[:, n % 2, :], qkv[:, n, :], ACT.Square).then_inc(S_["sq"], 1)
                    if n < 2:
                        continue
                    t = n - 2
                    act.wait_ge(S_["ms"], t + 1)
                    if t >= 2:
                        act.wait_ge(S_["normed"], t - 1)
                    nc.scalar.activation(norm[:, t % 2, :], ps[t % 4][:], ACT.Ln, bias=eps).then_inc(S_["ln"], 1)
                    act.wait_ge(S_["ln"], t + 1)
                    nc.scalar.activation(norm[:, t % 2, :], norm[:, t % 2, :], ACT.Exp, scale=-0.5).then_inc(S_["rs"], 1)
                step = chained(act, S_["act_col"])
                act.wait_ge(S_["ba_out"], 1)
                nc.scalar.activation(col["beta"][:], ba[:, :, 0:4], ACT.Exp, scale=-1.0).then_inc(S_["dec"], 1)
                act.wait_ge(S_["dve_col"], 1)
                step(nc.scalar.activation(col["tmp"][:], col["soft"][:], ACT.Abs))
                step(nc.scalar.activation(col["tmp"][:], col["tmp"][:], ACT.Exp, scale=-1.0))
                step(nc.scalar.activation(col["tmp"][:], col["tmp"][:], ACT.Ln, bias=1.0))
                step(nc.scalar.activation(col["ea"][:, 0, :], const("a_log"), ACT.Exp))
                act.wait_ge(S_["gc_done"], 1)
                nc.scalar.activation(col["gc"][:], ps[4][:, 0:NC * HD], ACT.Copy).then_inc(S_["gc_out"], 1)
                nc.scalar.activation(col["egc"][:], ps[4][:, 0:NC * HD], ACT.Exp).then_inc(S_["gc_out"], 1)
                nc.scalar.activation(col["elast"][:], ps[4][:, 64:64 + NC * HD], ACT.Exp).then_inc(S_["gc_out"], 1)
                nc.scalar.activation(col["last"][:], ps[4][:, 64:64 + NC * HD], ACT.Copy).then_inc(S_["gc_out"], 1)
                act.wait_ge(S_["diff"], 1)
                nc.scalar.activation(col["kd"][:], col["kd"][:], ACT.Exp).then_inc(S_["gc_out"], 1)

            @block.tensor
            def _(pe):
                for c in range(NC):
                    tr = nc.tensor.transpose(ps[5][:, 8 * c:8 * c + 8], misc[0:8, c * P:(c + 1) * P], ident[0:8, 0:8])
                tr.then_inc(S_["ba_turned"], 1)
                for t in range(8):
                    pe.wait_ge(S_["sq"], t + 1)
                    if t >= 4:
                        pe.wait_ge(S_["ln"], t - 3)
                    nc.tensor.matmul(ps[t % 4][:], ones, xb[:, t % 2, :], start=True, stop=True).then_inc(S_["ms"], 1)
                pe.wait_ge(S_["g_ready"], 1)
                nc.tensor.matmul(ps[4][:, 0:NC * HD], utri, col["g"][:].rearrange("p c h -> p (c h)"), start=True, stop=True)
                nc.tensor.matmul(ps[4][:, 64:64 + NC * HD], ones, col["g"][:].rearrange("p c h -> p (c h)"),
                                 start=True, stop=True).then_inc(S_["gc_done"], 1)

            @block.vector
            def _(dve):
                dve.wait_ge(S_["ba_turned"], 1)
                nc.vector.tensor_copy(ba[:].rearrange("p c h -> p (c h)"), ps[5][:, 0:8 * NC]).then_inc(S_["ba_out"], 1)
                dve.wait_ge(S_["ba_out"], 1)
                dtb = const("dt_bias")[:, None, :].to_broadcast([P, NC, HD])
                nc.vector.tensor_tensor(col["soft"][:], ba[:, :, 4:8], dtb, ALU.add).then_inc(S_["dve_col"], 1)
                for t in range(8):
                    dve.wait_ge(S_["rs"], t + 1)
                    nc.vector.scalar_tensor_tensor(out=qkv[:, t, :], in0=qkv[:, t, :],
                                                   scalar=float(GDN_D ** -0.5) if t < 4 else 1.0,
                                                   in1=norm[:, t % 2, :], op0=ALU.mult, op1=ALU.mult
                                                   ).then_inc(S_["normed"], 1)
                step = chained(dve, S_["decb"])
                dve.wait_ge(S_["dec"], 1)
                step(nc.vector.tensor_scalar(col["beta"][:], col["beta"][:], 1.0, None, ALU.add))
                step(nc.vector.reciprocal(col["beta"][:], col["beta"][:]))
                step(nc.vector.tensor_scalar(col["nbeta"][:], col["beta"][:], -1.0, None, ALU.mult))
                dve.wait_ge(S_["act_col"], 4)
                step(nc.vector.scalar_tensor_tensor(out=col["soft"][:], in0=col["soft"][:], scalar=0.0,
                                                    in1=col["tmp"][:], op0=ALU.max, op1=ALU.add))
                eab = col["ea"][:, 0:1, :].to_broadcast([P, NC, HD])
                nc.vector.scalar_tensor_tensor(out=col["g"][:], in0=col["soft"][:], scalar=-1.0, in1=eab,
                                               op0=ALU.mult, op1=ALU.mult).then_inc(S_["g_ready"], 1)
                dve.wait_ge(S_["gc_out"], 4)
                nc.vector.tensor_tensor(col["kd"][:], col["last"][:], col["gc"][:], ALU.subtract).then_inc(S_["diff"], 1)
                nc.vector.tensor_tensor(col["bg"][:], col["beta"][:], col["egc"][:], ALU.mult)

        with nc.Block() as block:
            def k_tile(hd, c):
                return qkv[:, 4 + hd, c * C:(c + 1) * C]

            def q_tile(hd, c):
                return qkv[:, hd, c * C:(c + 1) * C]

            def q_chunk(c):
                return qkv[:, 0:4, c * C:(c + 1) * C]

            @block.tensor
            def _(pe):
                keep_busy(ps[6], 4)
                for c in range(NC):
                    if c:
                        pe.wait_ge(S_["diff"], 1 + c)
                        pe.wait_ge(S_["qd_row"], c)
                        pe.wait_ge(S_["dec_masked"], c)
                    for hd in range(HD):
                        nc.tensor.matmul(ps[0][:, hd * C:(hd + 1) * C], col["g"][:, c, hd:hd + 1].to_broadcast([P, C]),
                                         utri, start=True, stop=True)
                        mm = nc.tensor.matmul(ps[1][:, hd * C:(hd + 1) * C], col["nbeta"][:, c, hd:hd + 1].to_broadcast([P, C]),
                                              ident, start=True, stop=True)
                    mm.then_inc(S_["rows_done"], 1)
                    if c:
                        pe.wait_ge(S_["nat_out"], c)
                        pe.wait_ge(S_["intra_out"], c)
                    for hd in range(HD):
                        nc.tensor.matmul(ps[2][:, hd * C:(hd + 1) * C], k_tile(hd, c), k_tile(hd, c), start=True, stop=True)
                        mm = nc.tensor.matmul(ps[3][:, hd * C:(hd + 1) * C], k_tile(hd, c), q_tile(hd, c), start=True, stop=True)
                    mm.then_inc(S_["pairs_done"], 1)
                    if c:
                        pe.wait_ge(S_["k_out"], 2 * c)
                    for hd in range(HD):
                        tr = nc.tensor.transpose(ps[4][:, hd * C:(hd + 1) * C], k_tile(hd, c), ident)
                    tr.then_inc(S_["k_turned"], 1)
                    if c:
                        pe.wait_ge(S_["v_out"], c)
                    for hd in range(HD):
                        tr = nc.tensor.transpose(ps[5][:, hd * C:(hd + 1) * C], qkv[:, 8 + hd, c * C:(c + 1) * C], ident)
                    tr.then_inc(S_["v_turned"], 1)

            @block.vector
            def _(dve):
                for c in range(NC):
                    dve.wait_ge(S_["rows_done"], c + 1)
                    if c:
                        dve.wait_ge(S_["nat_out"], c)
                        dve.wait_ge(S_["intra_out"], c)
                    nc.vector.tensor_tensor(heads(dec[:, 0, :]), heads(ps[0][:]), over(col["gc"][:, c, :]),
                                            ALU.subtract).then_inc(S_["diff"], 1)
                    dve.wait_ge(S_["diff"], 2 + c)
                    nc.vector.tensor_scalar(dec[:, 0, :], dec[:, 0, :], 0.0, None, ALU.min).then_inc(S_["y1"], 1)
                    dve.wait_ge(S_["k_turned"], c + 1)
                    nc.vector.tensor_tensor(heads(kbg[:, c, :]), heads(ps[4][:]), over(col["bg"][:, c, :]), ALU.mult).then_inc(S_["k_out"], 1)
                    nc.vector.tensor_tensor(heads(kdec[:, c, :]), heads(ps[4][:]), over(col["kd"][:, c, :]), ALU.mult).then_inc(S_["k_out"], 1)
                    dve.wait_ge(S_["v_turned"], c + 1)
                    nc.vector.tensor_tensor(heads(vb[:, c, :]), heads(ps[5][:]), over(col["beta"][:, c, :]), ALU.mult).then_inc(S_["v_out"], 1)
                    dve.wait_ge(S_["dec"], 2 + c)
                    nc.vector.tensor_tensor(heads(dec[:, 1, :]), heads(dec[:, 0, :]), per_head(utri), ALU.mult).then_inc(S_["y2"], 1)
                    dve.wait_ge(S_["y2"], c + 1)
                    nc.vector.tensor_tensor(dec[:, 0, :], dec[:, 1, :], ps[1][:], ALU.mult).then_inc(S_["dec_masked"], 1)
                    dve.wait_ge(S_["dec_masked"], c + 1)
                    dve.wait_ge(S_["pairs_done"], c + 1)
                    nc.vector.tensor_tensor(nat[:, c, :], ps[2][:], dec[:, 0, :], ALU.mult).then_inc(S_["nat_out"], 1)
                    nc.vector.tensor_tensor(intra[:, c, :], ps[3][:], dec[:, 1, :], ALU.mult).then_inc(S_["intra_out"], 1)
                    dve.wait_ge(S_["qd_row"], c + 1)
                    nc.vector.tensor_tensor(q_chunk(c), q_chunk(c), heads(norm[:, c % 2, :]), ALU.mult).then_inc(S_["qd_out"], 1)

            @block.scalar
            def _(act):
                for c in range(NC):
                    act.wait_ge(S_["diff"], 2 + c)
                    if c >= 2:
                        act.wait_ge(S_["qd_out"], c - 1)
                    nc.scalar.activation(norm[:, c % 2, :], ps[0][:], ACT.Exp).then_inc(S_["qd_row"], 1)
                    act.wait_ge(S_["y1"], c + 1)
                    nc.scalar.activation(dec[:, 0, :], dec[:, 0, :], ACT.Exp).then_inc(S_["dec"], 1)

        LEVELS = 7
        with nc.Block() as block:
            def level(l):
                return vrows[:, l * P:(l + 1) * P]

            @block.gpsimd
            def _(pool):
                for l in range(LEVELS):
                    for c in range(NC):
                        n = l * NC + c
                        if n >= 2:
                            pool.wait_ge(S_["x_done"], n - 1)
                            if n < NC + 2:
                                pool.wait_ge(S_["tt_out"], n - 1)
                        nc.gpsimd.tensor_tensor(heads(off[:, n % 2, :]), heads(nat[:, c, :]), per_head(level(l)),
                                                ALU.mult).then_inc(S_["off_ready"], 1)

            @block.tensor
            def _(pe):
                keep_busy(ps[6], 4)
                for l in range(LEVELS):
                    for c in range(NC):
                        n = l * NC + c
                        pe.wait_ge(S_["off_ready"], n + 1)
                        if n >= 2:
                            pe.wait_ge(S_["x_out"], n - 1)
                        if l:
                            pe.wait_ge(S_["t_out"], n - NC + 1)
                        for hd in range(HD):
                            r = slice(hd * C, (hd + 1) * C)
                            mm = nc.tensor.matmul(ps[n % 2][:, r], off[:, n % 2, r], t_[:, c, r] if l else ident,
                                                  start=True, stop=True)
                        mm.then_inc(S_["x_done"], 1)
                        if l:
                            m = n - NC
                            pe.wait_ge(S_["x_out"], n + 1)
                            pe.wait_ge(S_["tt_out"], n - NC + 1)
                            if l < LEVELS - 1:
                                if m >= 2:
                                    pe.wait_ge(S_["t_out"], n - 1)
                                for hd in range(HD):
                                    r = slice(hd * C, (hd + 1) * C)
                                    nc.tensor.matmul(ps[2 + n % 2][:, r], tt_[:, c, r], xb[:, n % 2, r], start=True, stop=True)
                            if m >= 2:
                                pe.wait_ge(S_["tt_out"], n - 1)
                            for hd in range(HD):
                                r = slice(hd * C, (hd + 1) * C)
                                mm = nc.tensor.matmul(ps[4 + n % 2][:, r], xb[:, n % 2, r], tt_[:, c, r], start=True, stop=True)
                            mm.then_inc(S_["u_done"], 1)

            @block.scalar
            def _(act):
                for n in range(LEVELS * NC):
                    act.wait_ge(S_["x_done"], n + 1)
                    if n >= NC + 2:
                        act.wait_ge(S_["u_done"], n - NC - 1)
                    elif n >= 2:
                        act.wait_ge(S_["t_out"], n - 1)
                    nc.scalar.activation(xb[:, n % 2, :], ps[n % 2][:], ACT.Copy).then_inc(S_["x_out"], 1)

            @block.vector
            def _(dve):
                for l in range(LEVELS):
                    for c in range(NC):
                        n = l * NC + c
                        if l == 0:
                            dve.wait_ge(S_["x_out"], n + 1)
                            nc.vector.tensor_tensor(heads(t_[:, c, :]), heads(xb[:, n % 2, :]), per_head(ident), ALU.add).then_inc(S_["t_out"], 1)
                            nc.vector.tensor_tensor(heads(tt_[:, c, :]), heads(off[:, n % 2, :]), per_head(ident), ALU.add).then_inc(S_["tt_out"], 1)
                        else:
                            dve.wait_ge(S_["u_done"], n - NC + 1)
                            if l < LEVELS - 1:
                                nc.vector.tensor_tensor(t_[:, c, :], t_[:, c, :], ps[2 + n % 2][:], ALU.add).then_inc(S_["t_out"], 1)
                            nc.vector.tensor_tensor(tt_[:, c, :], tt_[:, c, :], ps[4 + n % 2][:], ALU.add).then_inc(S_["tt_out"], 1)

        nw = t_
        o_t = nat
        with nc.Block() as block:
            def o_chunk(c):
                return o_t[:, :, c * C:(c + 1) * C]

            @block.tensor
            def _(pe):
                for c in range(NC):
                    if c >= 2:
                        pe.wait_ge(S_["w_out"], c - 1)
                    for hd in range(HD):
                        r = slice(hd * C, (hd + 1) * C)
                        mm = nc.tensor.matmul(ps[c % 2][:, r], kbg[:, c, r], tt_[:, c, r], start=True, stop=True)
                    mm.then_inc(S_["w_done"], 1)
                for c in range(NC):
                    if c:
                        pe.wait_ge(S_["w_out"], c + 1)
                        pe.wait_ge(S_["s_out"], c)
                        pe.wait_ge(S_["vn_out"], c)
                    for hd in range(HD):
                        r = slice(hd * C, (hd + 1) * C)
                        mm = nc.tensor.matmul(ps[2][:, r], tt_[:, c, r], vb[:, c, r], start=True, stop=c == 0)
                        if c:
                            mm = nc.tensor.matmul(ps[2][:, r], nw[:, c, r], state[:, r], start=False, stop=True)
                    mm.then_inc(S_["vn_done"], 1)
                    pe.wait_ge(S_["vn_out"], c + 1)
                    if c:
                        pe.wait_ge(S_["s_out"], c)
                    for hd in range(HD):
                        r = slice(hd * C, (hd + 1) * C)
                        if c < NC - 1:
                            mm = nc.tensor.matmul(ps[3][:, r], kdec[:, c, r], vn[:, r], start=True, stop=True)
                    if c < NC - 1:
                        mm.then_inc(S_["s_done"], 1)
                    if c:
                        pe.wait_ge(S_["o_out"], c)
                    for hd in range(HD):
                        r = slice(hd * C, (hd + 1) * C)
                        if c:
                            nc.tensor.matmul(ps[4][:, r], state[:, r], q_tile(hd, c), start=True, stop=False)
                        mm = nc.tensor.matmul(ps[4][:, r], vn[:, r], intra[:, c, r], start=c == 0, stop=True)
                    mm.then_inc(S_["o_done"], 1)
                for hd in range(HD):
                    pe.wait_ge(S_["o_sq"], hd + 1)
                    nc.tensor.matmul(ps[hd][:], ones, xb[:, hd % 2, :], start=True, stop=True).then_inc(S_["o_ms"], 1)

            @block.scalar
            def _(act):
                act.preload_act_table_set("natural_log_exp_and_others")
                for c in range(NC):
                    act.wait_ge(S_["w_done"], c + 1)
                    nc.scalar.activation(nw[:, c, :], ps[c % 2][:], ACT.Copy, scale=-1.0).then_inc(S_["w_out"], 1)
                for c in range(NC):
                    act.wait_ge(S_["vn_done"], c + 1)
                    if c:
                        act.wait_ge(S_["o_done"], c)
                    nc.scalar.activation(vn[:], ps[2][:], ACT.Copy).then_inc(S_["vn_out"], 1)
                act.wait_ge(S_["o_out"], NC)
                for hd in range(HD):
                    if hd >= 2:
                        act.wait_ge(S_["o_ms"], hd - 1)
                    nc.scalar.activation(xb[:, hd % 2, :], o_t[:, hd, :], ACT.Square).then_inc(S_["o_sq"], 1)
                for hd in range(HD):
                    act.wait_ge(S_["o_ms"], hd + 1)
                    if hd >= 2:
                        act.wait_ge(S_["y_lo"], hd - 1)
                    nc.scalar.activation(norm[:, hd % 2, :], ps[hd][:], ACT.Ln, bias=eps, scale=1.0 / GDN_D).then_inc(S_["o_ln"], 1)
                    act.wait_ge(S_["o_ln"], hd + 1)
                    nc.scalar.activation(norm[:, hd % 2, :], norm[:, hd % 2, :], ACT.Exp, scale=-0.5).then_inc(S_["o_rs"], 1)
                for hd in range(HD):
                    act.wait_ge(S_["id_out"], hd + 1)
                    nc.scalar.activation(mix_hi[:, 4 + hd, :], o_t[:, hd, :], ACT.Copy).then_inc(S_["y_hi"], 1)

            @block.vector
            def _(dve):
                for c in range(NC):
                    if c < NC - 1:
                        dve.wait_ge(S_["s_done"], c + 1)
                        if c == 0:
                            nc.vector.tensor_copy(state[:], ps[3][:]).then_inc(S_["s_out"], 1)
                    dve.wait_ge(S_["o_done"], c + 1)
                    if 0 < c < NC - 1:
                        nc.vector.tensor_tensor(heads(state[:]), heads(state[:]), over(col["elast"][:, c, :]), ALU.mult).then_inc(S_["v_turned"], 1)
                        dve.wait_ge(S_["v_turned"], NC + c)
                        nc.vector.tensor_tensor(state[:], state[:], ps[3][:], ALU.add).then_inc(S_["s_out"], 1)
                    nc.vector.tensor_copy(o_chunk(c), heads(ps[4][:])).then_inc(S_["o_out"], 1)
                for hd in range(HD):
                    dve.wait_ge(S_["o_sq"], hd + 1)
                    dve.wait_ge(S_["o_rs"], hd + 1)
                    nc.vector.scalar_tensor_tensor(out=o_t[:, hd, :], in0=o_t[:, hd, :], scalar=const("g_gdn"), in1=norm[:, hd % 2, :],
                                                   op0=ALU.mult, op1=ALU.mult).then_inc(S_["y_lo"], 1)
                    dve.wait_ge(S_["y_lo"], hd + 1)
                    nc.vector.tensor_tensor(o_t[:, hd, :], o_t[:, hd, :], zg[:, hd, :], ALU.mult).then_inc(S_["id_out"], 1)
                for hd in range(HD):
                    dve.wait_ge(S_["y_hi"], hd + 1)
                    nc.vector.tensor_tensor(mix_lo[:, 4 + hd, :], o_t[:, hd, :], mix_hi[:, 4 + hd, :].bitcast(F32), ALU.subtract)

    def project_residual(name, x_hi, x_lo):
        U = UNITS[name][0]
        added = sem(f"added_{name}")
        with ExitStack() as ph:
            sq2 = sb(ph, f"sq2_{name}", [P, 2, SEQ])
            clear, square, add_square = square_sum(sq2)
            ps = banks(ph, name)
            with nc.Block() as block:
                @block.sync
                def _(sp):
                    load_units(sp, name)

                @block.gpsimd
                def _(pool):
                    split_los(pool, name)

                @block.scalar
                def _(act):
                    act.preload_act_table_set("natural_log_exp_and_others")
                    split_hi(act, U + 1, 0)
                    for u in range(4):
                        if u < 3:
                            split_hi(act, U + 2 + u, 0)
                        for t in (2 * u, 2 * u + 1):
                            act.wait_ge(added, t + 1)
                            square(act, t)

                @block.vector
                def _(dve):
                    clear(dve)
                    for t in range(KT):
                        dve.wait_ge(tiles_done, 2 * U + t + 1)
                        nc.vector.tensor_tensor(h[:, t, :], h[:, t, :], ps[t % 4][:], ALU.add).then_inc(added, 1)
                        if t:
                            add_square(dve, t - 1)
                    add_square(dve, KT - 1)

                @block.tensor
                def _(pe):
                    with pe.Fori(0, 2) as i:
                        for j in range(2):
                            pe.wait_ge(lo_ready, U + j + 1 + 2 * i)
                            for m in range(2):
                                pe.wait_ge(added, 4 * i)
                                column_tile(ps[2 * j + m][:], (U + j) % 2, m, x_hi, x_lo).then_inc(tiles_done, 1)

    project_residual("ev_out", mix_hi, mix_lo)
    even.close()

    def ffn(n):
        gu, down = f"gu{n}", f"down{n}"
        with ExitStack() as ph:
            hid_hi, hid_lo = sb(ph, f"hid_hi{n}", [P, FT, SEQ], F32R), sb(ph, f"hid_lo{n}", [P, FT, SEQ], F32R)
            ps = banks(ph, f"ffn{n}")
            with ExitStack() as up:
                xh, xl = sb(up, f"xh_f{n}", [P, KT, SEQ], F32R), sb(up, f"xl_f{n}", [P, KT, SEQ], F32R)
                xn = sb(up, f"xn_f{n}", [P, KT, SEQ])
                n_act, n_pe, n_dve, wait_tile, _ = norm_parts(xn, ps[4], const(f"g_ffn{n}"), xh, xl)
                silu, prod = xn[:, 0:2, :], xn[:, 2:4, :]
                silu_done, prod_done, hi_done, lo_done = (sem(f"silu{n}"), sem(f"prod{n}"), sem(f"hid_hi_out{n}"),
                                                          sem(f"hid_lo_out{n}"))
                U = UNITS[gu][0]
                with nc.Block() as block:
                    @block.sync
                    def _(sp):
                        load_units(sp, gu)

                    @block.gpsimd
                    def _(pool):
                        split_los(pool, gu)

                    @block.scalar
                    def _(act):
                        n_act(act)
                        act.preload_act_table(ACT.Silu)
                        wait_tile(act, KT - 1)
                        with act.Fori(0, FT // 2) as i:
                            split_hi(act, U + 1, i)
                            for m in range(2):
                                act.wait_ge(tiles_done, 2 * U + m + 1 + 4 * i)
                                nc.scalar.activation(silu[:, m, :], ps[m][:], ACT.Silu).then_inc(silu_done, 1)
                            split_hi(act, U + 2, i)
                            for m in range(2):
                                act.wait_ge(prod_done, m + 1 + 2 * i)
                                nc.scalar.activation(hid_hi[:, 2 * i + m, :], prod[:, m, :], ACT.Copy).then_inc(hi_done, 1)

                    @block.vector
                    def _(dve):
                        n_dve(dve)
                        with dve.Fori(0, FT // 2) as i:
                            dve.wait_ge(lo_done, 2 * i)
                            for m in range(2):
                                dve.wait_ge(tiles_done, 2 * U + m + 3 + 4 * i)
                                dve.wait_ge(silu_done, m + 1 + 2 * i)
                                nc.vector.tensor_tensor(prod[:, m, :], silu[:, m, :], ps[2 + m][:],
                                                        ALU.mult).then_inc(prod_done, 1)
                            for m in range(2):
                                dve.wait_ge(hi_done, m + 1 + 2 * i)
                                nc.vector.tensor_tensor(hid_lo[:, 2 * i + m, :], prod[:, m, :],
                                                        hid_hi[:, 2 * i + m, :].bitcast(F32),
                                                        ALU.subtract).then_inc(lo_done, 1)

                    @block.tensor
                    def _(pe):
                        keep_busy(ps[5], 2)
                        n_pe(pe)
                        keep_busy(ps[5], 3)

                        def unit(j, i):
                            pe.wait_ge(lo_ready, U + j + 1 + 2 * i)
                            if not isinstance(i, int):
                                pe.wait_ge(prod_done if j else silu_done, 2 * i)
                            for m in range(2):
                                column_tile(ps[2 * j + m][:], (U + j) % 2, m, xh, xl).then_inc(tiles_done, 1)
                        first_unit(pe, U, ps[0:2], xh, xl, wait_tile)
                        unit(1, 0)
                        with pe.Fori(1, FT // 2) as i:
                            unit(0, i)
                            unit(1, i)
            U = UNITS[down][0]
            added = sem(f"added_{down}")
            sq2 = sb(ph, f"sq2_{down}", [P, 2, SEQ])
            clear, square, add_square = square_sum(sq2)
            with nc.Block() as block:
                @block.sync
                def _(sp):
                    load_units(sp, down)

                @block.gpsimd
                def _(pool):
                    split_los(pool, down)

                @block.scalar
                def _(act):
                    act.preload_act_table_set("natural_log_exp_and_others")
                    for j in range(12):
                        if U + j + 1 < N_UNITS:
                            split_hi(act, U + j + 1, 0)
                        for t in {3: (0, 1), 6: (2, 3), 9: (4, 5), 11: (6, 7)}.get(j, ()):
                            act.wait_ge(added, t + 1)
                            square(act, t)

                @block.vector
                def _(dve):
                    clear(dve)
                    for t in range(KT):
                        dve.wait_ge(tiles_done, 2 * (U + 3 * (t // 2) + 2) + t % 2 + 1)
                        nc.vector.tensor_tensor(h[:, t, :], h[:, t, :], ps[4 + t % 4][:], ALU.add).then_inc(added, 1)
                        if t % 2:
                            add_square(dve, t - 1)
                            add_square(dve, t)

                @block.tensor
                def _(pe):
                    with pe.Fori(0, KT // 4) as i:
                        for j in range(6):
                            pe.wait_ge(lo_ready, U + j + 1 + 6 * i)
                            if j % 3 == 0:
                                pe.wait_ge(added, 4 * i)
                            r = j % 3
                            for m in range(2):
                                column_tile(ps[4 + 2 * (j // 3) + m][:], (U + j) % 2, m, hid_hi, hid_lo, k0=UK * r,
                                            nk=min(UK, FT - UK * r), first=r == 0, last=r == 2).then_inc(tiles_done, 1)

    ffn(0)

    odd, cmp_in = ExitStack(), ExitStack()
    G, CW = NSA_GROUPS, SEQ + CMP_STRIDE
    q_n = sb(odd, "q_n", [P, NSA_HEADS // 2, SEQ])
    k_two = [sb(odd, f"k_{n}", [P, G, SEQ]) for n in ("sel", "win")]
    v_two = [sb(odd, f"v_{n}", [P, NQT, G * NSA_DIM]) for n in ("sel", "win")]
    gates = sb(odd, "gates", [P, NQT, 3 * NSA_HEADS])
    k_cmp = sb(odd, "k_cmp", [P, G * NCMP])
    v_cmp = sb(odd, "v_cmp", [P, G * NSA_DIM])
    seq_hi = [sb(cmp_in, f"seq_hi_{n}", [P, G + 1, CW], F32R) for n in "kv"]
    seq_lo = [sb(cmp_in, f"seq_lo_{n}", [P, G + 1, CW], F32R) for n in "kv"]
    with ExitStack() as ph:
        xh, xl = sb(ph, "xh_od", [P, KT, SEQ], F32R), sb(ph, "xl_od", [P, KT, SEQ], F32R)
        xn = sb(ph, "xn_od", [P, KT, SEQ])
        ps = banks(ph, "odin")
        n_act, n_pe, n_dve, wait_tile, _ = norm_parts(xn, ps[4], const("g_od"), xh, xl)
        out_a, out_v, padded, piece_hi = sem("odin_out_act"), sem("odin_out_dve"), sem("od_padded"), sem("od_piece_hi")
        piece_lo = sem("od_piece_lo")
        gate_done, gate_exp, gate_step = sem("gate_done"), sem("gate_exp"), sem("gate_step")
        U = UNITS["od_in"][0]
        w_gate = const("w_gate")
        HALF = NSA_DIM

        def half(t):
            return slice(t * HALF, (t + 1) * HALF)

        with nc.Block() as block:
            @block.sync
            def _(sp):
                load_units(sp, "od_in")

            @block.gpsimd
            def _(pool):
                for t in seq_hi + seq_lo:
                    nc.gpsimd.memset(t[:].bitcast(F32), 0.0).then_inc(padded, 1)
                split_los(pool, "od_in")

            @block.scalar
            def _(act):
                n_act(act)
                with act.Fori(0, 2) as i:
                    for j in range(2):
                        split_hi(act, U + 1 + j, i)
                        act.wait_ge(tiles_done, 2 * (U + j) + 1 + 4 * i)
                        nc.scalar.activation(q_n[:, 4 * i + 2 * j, :], ps[2 * j][:], ACT.Copy).then_inc(out_a, 1)
                act.wait_ge(padded, 4)
                for v in range(2):
                    nc.scalar.activation(seq_hi[v][:, G, 0:CMP_BLOCK:2], const("pe_v" if v else "pe_k"),
                                         ACT.Copy).then_inc(piece_hi, 1)
                    split_hi(act, U + 5 + v, 0)
                    for m in range(2):
                        act.wait_ge(tiles_done, 2 * (U + 4 + v) + m + 1)
                        for g in range(2):
                            src = ps[2 * v + m][half(g), :]
                            nc.scalar.activation(seq_hi[v][0:64, 2 * m + g, 0:SEQ], src, ACT.Copy).then_inc(piece_hi, 1)
                            nc.scalar.activation(seq_hi[v][64:128, 2 * m + g, 0:SEQ - 1], src[:, 1:SEQ],
                                                 ACT.Copy).then_inc(piece_hi, 1)
                for v in range(2):
                    split_hi(act, U + 7 + v, 0)
                    for m in range(2):
                        act.wait_ge(tiles_done, 2 * (U + 6 + v) + m + 1)
                        for r in range(2):
                            nc.scalar.activation(k_two[v][half(r), 2 * m, :], ps[2 * v + m][half(0), :],
                                                 ACT.Copy).then_inc(out_a, 1)
                for v in range(2):
                    split_hi(act, U + 9 + v, 0)
                    act.wait_ge(tiles_done, 2 * (U + 8 + v) + 1)
                    nc.scalar.activation(v_two[v][:, 0:2, :], ps[2 * v][:], ACT.Copy).then_inc(out_a, 1)
                act.wait_ge(gate_done, 1)
                nc.scalar.activation(gates[:], ps[5][:, 0:NQT * 48], ACT.Exp, scale=-1.0).then_inc(gate_exp, 1)

            @block.vector
            def _(dve):
                n_dve(dve)
                with dve.Fori(0, 2) as i:
                    for j in range(2):
                        dve.wait_ge(tiles_done, 2 * (U + j) + 2 + 4 * i)
                        nc.vector.tensor_copy(q_n[:, 4 * i + 2 * j + 1, :], ps[2 * j + 1][:]).then_inc(out_v, 1)
                dve.wait_ge(padded, 4)
                for v in range(2):
                    dve.wait_ge(piece_hi, 9 * v + 1)
                    nc.vector.tensor_tensor(seq_lo[v][:, G, 0:CMP_BLOCK:2], const("pe_v" if v else "pe_k"),
                                            seq_hi[v][:, G, 0:CMP_BLOCK:2].bitcast(F32), ALU.subtract)
                    for m in range(2):
                        dve.wait_ge(piece_hi, 9 * v + 4 * m + 5)
                        for g in range(2):
                            src = ps[2 * v + m][half(g), :]
                            nc.vector.tensor_tensor(seq_lo[v][0:64, 2 * m + g, 0:SEQ], src,
                                                    seq_hi[v][0:64, 2 * m + g, 0:SEQ].bitcast(F32),
                                                    ALU.subtract).then_inc(piece_lo, 1)
                            nc.vector.tensor_tensor(seq_lo[v][64:128, 2 * m + g, 0:SEQ - 1], src[:, 1:SEQ],
                                                    seq_hi[v][64:128, 2 * m + g, 0:SEQ - 1].bitcast(F32),
                                                    ALU.subtract).then_inc(piece_lo, 1)
                for v in range(2):
                    for m in range(2):
                        dve.wait_ge(tiles_done, 2 * (U + 6 + v) + m + 1)
                        for r in range(2):
                            nc.vector.tensor_copy(k_two[v][half(r), 2 * m + 1, :], ps[2 * v + m][half(1), :]).then_inc(out_v, 1)
                for v in range(2):
                    dve.wait_ge(tiles_done, 2 * (U + 8 + v) + 2)
                    nc.vector.tensor_copy(v_two[v][:, 2:4, :], ps[2 * v + 1][:]).then_inc(out_v, 1)
                dve.wait_ge(gate_exp, 1)
                nc.vector.tensor_scalar(gates[:], gates[:], 1.0, None, ALU.add).then_inc(gate_step, 1)
                dve.wait_ge(gate_step, 1)
                nc.vector.reciprocal(gates[:], gates[:])

            @block.tensor
            def _(pe):
                keep_busy(ps[5], 2)
                n_pe(pe)
                keep_busy(ps[5], 3)

                def unit(u, i, *free):
                    pe.wait_ge(lo_ready, U + u + 1 + 2 * i)
                    for s, v in free:
                        pe.wait_ge(s, v)
                    for m in range(2):
                        column_tile(ps[2 * (u % 2) + m][:], (U + u) % 2, m, xh, xl).then_inc(tiles_done, 1)
                first_unit(pe, U, ps[0:2], xh, xl, wait_tile)
                unit(1, 0)
                unit(2, 0, (out_a, 1), (out_v, 1))
                unit(3, 0, (out_a, 2), (out_v, 2))
                unit(4, 0, (out_a, 3), (out_v, 3))
                unit(5, 0, (out_a, 4), (out_v, 4))
                unit(6, 0, (piece_lo, 8))
                unit(7, 0, (piece_lo, 16))
                for v in range(2):
                    u = 8 + v
                    pe.wait_ge(lo_ready, U + u + 1)
                    pe.wait_ge(out_a, 4 + 4 * (v + 1))
                    pe.wait_ge(out_v, 4 + 4 * (v + 1))
                    for tt in range(NQT):
                        tok = slice(tt * P, (tt + 1) * P)
                        acc = ps[2 * v + tt // 2][:, (tt % 2) * 256:(tt % 2) * 256 + 256]
                        for k in range(KT):
                            c = slice(k * 256, (k + 1) * 256)
                            s = (U + u) % 2
                            mm = three_passes(acc, xh[:, k, tok], xl[:, k, tok], whi[:, s, c], wlo[:, s, c],
                                              k == 0, k == KT - 1)
                        if tt % 2:
                            mm.then_inc(tiles_done, 1)
                for tt in range(NQT):
                    tok = slice(tt * P, (tt + 1) * P)
                    for part, x in enumerate((xh, xl)):
                        for k in range(KT):
                            mm = nc.tensor.matmul(ps[5][:, tt * 48:(tt + 1) * 48], x[:, k, tok].bitcast(F32),
                                                  w_gate[:, k * 48:(k + 1) * 48],
                                                  start=part == 0 and k == 0, stop=part == 1 and k == KT - 1)
                mm.then_inc(gate_done, 1)

    w2_landed = sem("w2_landed")
    with ExitStack() as ph:
        w2 = sb(ph, "w2_sb", [P, 4 * NSA_DIM])
        first = sb(ph, "cmp_first", [P, 2])
        hidden = sb(ph, "cmp_hidden", [P, 4, G * NCMP])
        ps = banks(ph, "cmp")
        bias_out, hidden_out, cmp_done, k_out, zeroed = (sem("cmp_bias_out"), sem("cmp_hidden_out"), sem("cmp_done"),
                                                 sem("cmp_k_out"), sem("cmp_zeroed"))
        U, N = UNITS["cmp"][0], G * NCMP
        with nc.Block() as block:
            @block.sync
            def _(sp):
                sp.dma_start(w2[:], w2_in).then_inc(w2_landed, 16)
                load_units(sp, "cmp")

            @block.gpsimd
            def _(pool):
                nc.gpsimd.memset(v_cmp[:], 0.0).then_inc(zeroed, 1)
                split_los(pool, "cmp")

            @block.tensor
            def _(pe):
                keep_busy(ps[6], 3)
                for v in range(2):
                    for r in range(2):
                        u = 2 * v + r
                        pe.wait_ge(lo_ready, U + u + 1)
                        for m in range(2):
                            for k in range(UK):
                                w_hi, w_lo = unit_block((U + u) % 2, k, m)
                                t0 = 2 * (UK * r + k)
                                cols = slice(t0, t0 + CMP_STRIDE * (NCMP - 1) + 1, CMP_STRIDE)
                                mm = three_passes(ps[2 * v + m][:, 0:N + NCMP], w_hi, w_lo, seq_hi[v][:, :, cols],
                                                  seq_lo[v][:, :, cols], r == 0 and k == 0, r == 1 and k == UK - 1)
                            mm.then_inc(tiles_done, 1)
                pe.wait_ge(w2_landed, 16)
                for v in range(2):
                    pe.wait_ge(hidden_out, 2 * v + 2)
                    for m in range(2):
                        w = w2[:, (2 * v + m) * NSA_DIM:(2 * v + m + 1) * NSA_DIM]
                        if v == 0:
                            mm = nc.tensor.matmul(ps[4][0:64, 0:N], w, hidden[:, m, :], start=m == 0, stop=m == 1)
                        else:
                            mm = nc.tensor.matmul(ps[5][:, 0:NSA_DIM], hidden[:, 2 + m, :], w, start=m == 0, stop=m == 1)
                    mm.then_inc(cmp_done, 1)

            @block.scalar
            def _(act):
                for u in range(4):
                    split_hi(act, U + u + 1, 0)
                for v in range(2):
                    for m in range(2):
                        act.wait_ge(tiles_done, 2 * (U + 2 * v + 1) + m + 1)
                        nc.scalar.activation(first[:, m:m + 1], ps[2 * v + m][:, N:N + 1], ACT.Copy).then_inc(bias_out, 1)
                        act.wait_ge(bias_out, 2 * v + m + 1)
                        nc.scalar.activation(hidden[:, 2 * v + m, :], ps[2 * v + m][:, 0:N], ACT.Gelu_apprx_tanh,
                                             bias=first[:, m:m + 1]).then_inc(hidden_out, 1)
                act.wait_ge(cmp_done, 1)
                nc.scalar.activation(k_cmp[0:64, :], ps[4][0:64, 0:N], ACT.Copy)
                nc.scalar.activation(k_cmp[64:128, :], ps[4][0:64, 0:N], ACT.Copy)

            @block.vector
            def _(dve):
                dve.wait_ge(zeroed, 1)
                dve.wait_ge(cmp_done, 2)
                for g in range(G):
                    r = slice(g * NCMP, (g + 1) * NCMP)
                    nc.vector.tensor_copy(v_cmp[r, g * NSA_DIM:(g + 1) * NSA_DIM], ps[5][r, 0:NSA_DIM])
    cmp_in.close()

    att = ExitStack()
    o_acc = sb(att, "o_acc", [P, NQT, NSA_HEADS * NSA_DIM])
    with ExitStack() as ph:
        cmp_bias = sb(ph, "cmp_bias_sb", [P, NQT, NSA_HEADS * NCMP])
        probs = sb(ph, "c_probs", [P, 2, NSA_HEADS * NCMP])
        stat = sb(ph, "c_stat", [P, 2, 3, NSA_HEADS])
        turned_sb = sb(ph, "c_turned", [P, 2, SEQ])
        tmp = sb(ph, "c_tmp", [P, 2, 2, 2])
        ps = banks(ph, "natt")
        bias_landed = sem("cmp_bias_landed")
        names = ("s", "biased", "max", "sub", "exp", "sum", "inv", "gate", "valid", "turned", "copied", "o", "o_out")
        cs = {n: sem("c_" + n) for n in names}
        with nc.Block() as block:
            @block.sync
            def _(sp):
                sp.dma_start(cmp_bias[:], cmp_bias_in.rearrange("p (t n) -> p t n", t=NQT)).then_inc(bias_landed, 16)

            def keys3(ap):
                return ap.rearrange("p (h n) -> p h n", n=NCMP)

            @block.tensor
            def _(pe):
                def outputs(qt):
                    pe.wait_ge(cs["exp"], qt + 1)
                    if qt:
                        pe.wait_ge(cs["copied"], qt)
                    for r in range(NSA_HPG):
                        tr = nc.tensor.transpose(ps[4][:, r * P:(r + 1) * P], probs[:, qt % 2, r * P:(r + 1) * P], ident)
                    tr.then_inc(cs["turned"], 1)
                    pe.wait_ge(cs["copied"], qt + 1)
                    if qt:
                        pe.wait_ge(cs["o_out"], 2 * qt)
                    for r in range(NSA_HPG):
                        mm = nc.tensor.matmul(ps[5 + r // 2][:, (r % 2) * 256:(r % 2) * 256 + 256],
                                              turned_sb[:, qt % 2, r * P:(r + 1) * P], v_cmp[:], start=True, stop=True)
                    mm.then_inc(cs["o"], 1)
                for qt in range(NQT):
                    if qt >= 2:
                        pe.wait_ge(cs["biased"], 2 * (qt - 1))
                    for hd in range(NSA_HEADS):
                        rows = slice((hd % 2) * 64, (hd % 2) * 64 + 64)
                        mm = nc.tensor.matmul(ps[2 * (qt % 2) + hd % 2][:, (hd // 2) * NCMP:(hd // 2 + 1) * NCMP],
                                              q_n[rows, hd // 2, qt * P:(qt + 1) * P],
                                              k_cmp[rows, (hd // NSA_HPG) * NCMP:(hd // NSA_HPG + 1) * NCMP],
                                              start=True, stop=True)
                    mm.then_inc(cs["s"], 1)
                    if qt:
                        outputs(qt - 1)
                outputs(NQT - 1)

            @block.scalar
            def _(act):
                for qt in range(NQT):
                    act.wait_ge(cs["sub"], qt + 1)
                    nc.scalar.activation(probs[:, qt % 2, :], probs[:, qt % 2, :], ACT.Exp,
                                         scale=float(NSA_DIM ** -0.5)).then_inc(cs["exp"], 1)
                    act.wait_ge(cs["turned"], qt + 1)
                    if qt >= 2:
                        act.wait_ge(cs["o"], qt - 1)
                    nc.scalar.activation(turned_sb[:, qt % 2, :], ps[4][:], ACT.Copy).then_inc(cs["copied"], 1)

            @block.vector
            def _(dve):
                dve.wait_ge(bias_landed, 16)

                def flat(qt):
                    return keys3(probs[:, qt % 2, :])

                def finish(qt):
                    st = stat[:, qt % 2]
                    dve.wait_ge(cs["exp"], qt + 1)
                    nc.vector.tensor_reduce(st[:, 1, :], flat(qt), AX.X, ALU.add).then_inc(cs["sum"], 1)
                    dve.wait_ge(cs["sum"], qt + 1)
                    nc.vector.reciprocal(st[:, 1, :], st[:, 1, :]).then_inc(cs["inv"], 1)
                    dve.wait_ge(cs["inv"], qt + 1)
                    g0 = gates[:, qt, :].rearrange("p (g r t) -> p r g t", g=G, t=3)[:, :, :, 0]
                    nc.vector.tensor_tensor(st[:, 2, :].rearrange("p (r g) -> p r g", g=G),
                                            st[:, 1, :].rearrange("p (r g) -> p r g", g=G), g0, ALU.mult).then_inc(cs["gate"], 1)
                    dve.wait_ge(cs["gate"], qt + 1)
                    nc.vector.tensor_scalar(st[:, 2, :], st[:, 2, :], const("any_valid")[:, qt:qt + 1], None,
                                            ALU.mult).then_inc(cs["valid"], 1)
                    dve.wait_ge(cs["valid"], qt + 1)
                    dve.wait_ge(cs["o"], qt + 1)
                    for b in range(2):
                        src = ps[5 + b][:].rearrange("p (r g d) -> p r g d", r=2, g=G)
                        dst = o_acc[:, qt, :].rearrange("p (g r d) -> p r g d", g=G, r=NSA_HPG)[:, 2 * b:2 * b + 2]
                        co = st[:, 2, :].rearrange("p (b r g) -> p b r g", r=2, g=G)[:, b]
                        nc.vector.tensor_tensor(dst, src, co[:, :, :, None].to_broadcast([P, 2, G, NSA_DIM]),
                                                ALU.mult).then_inc(cs["o_out"], 1)

                for qt in range(NQT):
                    dve.wait_ge(cs["s"], qt + 1)
                    if qt >= 2:
                        dve.wait_ge(cs["turned"], qt - 1)
                        dve.wait_ge(cs["sum"], qt - 1)
                    bq = cmp_bias[:, qt, :].rearrange("p (g b a n) -> p a g b n", g=G, a=2, n=NCMP)
                    dst = probs[:, qt % 2, :].rearrange("p (b a g n) -> p a g b n", g=G, a=2, n=NCMP)
                    for a in range(2):
                        src = ps[2 * (qt % 2) + a][:, 0:8 * NCMP].rearrange("p (g b n) -> p g b n", g=G, n=NCMP)
                        nc.vector.tensor_tensor(dst[:, a], src, bq[:, a], ALU.add).then_inc(cs["biased"], 1)
                    dve.wait_ge(cs["biased"], 2 * qt + 2)
                    nc.vector.tensor_reduce(stat[:, qt % 2, 0, :], flat(qt), AX.X, ALU.max).then_inc(cs["max"], 1)
                    dve.wait_ge(cs["max"], qt + 1)
                    nc.vector.tensor_tensor(flat(qt), flat(qt),
                                            stat[:, qt % 2, 0, :, None].to_broadcast([P, NSA_HEADS, NCMP]),
                                            ALU.subtract).then_inc(cs["sub"], 1)
                    if qt:
                        finish(qt - 1)
                finish(NQT - 1)

    with ExitStack() as ph:
        dist = sb(ph, "dist", [P, NSA_HEADS, SEQ])
        prob, prob_t = sb(ph, "prob_n", [P, NQT, SEQ]), sb(ph, "prob_t_n", [P, 2, SEQ])
        neg_max, row_sum = sb(ph, "neg_max_n", [P, NQT]), sb(ph, "row_sum_n", [P, 2 * NSA_HEADS, NQT])
        coef, part = sb(ph, "coef_n", [P, 2, NQT]), sb(ph, "part_n", [P, 2, NQT, NSA_DIM])
        ps = banks(ph, "nat2")
        coef_ready, part_gated, part_added, dist_ready = sem("n_coef"), sem("n_gated"), sem("n_added"), sem("n_dist")
        rel, slope = const("rel"), const("slope")

        def take(dve, g, br, bank):
            n = 2 * g + br
            if n >= 2:
                dve.wait_ge(sem_of["o_taken_nsa"], n - 1)
            nc.vector.reciprocal(coef[:, n % 2], row_sum[:, n, :]).then_inc(coef_ready, 1)
            dve.wait_ge(coef_ready, n + 1)
            if n >= 2:
                dve.wait_ge(part_added, n - 1)
            own = g // NSA_HPG % 2 * NSA_DIM
            return nc.vector.tensor_tensor(part[:, n % 2], bank[:].rearrange("p (t d) -> p t d", t=NQT)[:, :, own:own + NSA_DIM],
                                           coef[:, n % 2, :, None].to_broadcast([P, NQT, NSA_DIM]), ALU.mult)

        on_act, on_dve, on_pe = attention(
            "nsa", NSA_HEADS, 2, float(NSA_DIM ** -0.5), ps[0:4], ps[4:6], ps[6:8], prob, prob_t, neg_max,
            lambda g, br: row_sum[:, 2 * g + br, :],
            query=lambda a, qt: q_n[(a // 2 % 2) * 64:(a // 2 % 2) * 64 + 64, a // 4, qt * P:(qt + 1) * P],
            keys=lambda a, w: k_two[a % 2][(a // 2 % 2) * 64:(a // 2 % 2) * 64 + 64, a // 8, 0:w],
            values=lambda a, kt: v_two[a % 2][:, kt, a // 16 * P:(a // 16 + 1) * P],
            bias=lambda g, qt: dist[:, g, (NQT - 1 - qt) * P:SEQ], take=take, bias_ready=dist_ready)
        with nc.Block() as block:
            @block.gpsimd
            def _(pool):
                def distances(hd):
                    nc.gpsimd.tensor_scalar(dist[:, hd, :], rel, slope[:, hd:hd + 1], None, ALU.mult).then_inc(dist_ready, 1)

                def add_part(n):
                    pool.wait_ge(sem_of["o_taken_nsa"], n + 1)
                    gate = gates[:, :, 3 * (n // 2) + 1 + n % 2, None].to_broadcast([P, NQT, NSA_DIM])
                    nc.gpsimd.tensor_tensor(part[:, n % 2], part[:, n % 2], gate, ALU.mult).then_inc(part_gated, 1)
                    pool.wait_ge(part_gated, n + 1)
                    if n % 2:
                        pool.wait_ge(part_added, n)
                    cols = slice(n // 2 * NSA_DIM, (n // 2 + 1) * NSA_DIM)
                    nc.gpsimd.tensor_tensor(o_acc[:, :, cols], o_acc[:, :, cols], part[:, n % 2], ALU.add).then_inc(part_added, 1)

                for hd in range(3):
                    distances(hd)
                for n in range(2 * NSA_HEADS):
                    if n + 3 < NSA_HEADS:
                        distances(n + 3)
                    add_part(n)

            @block.scalar
            def _(act):
                on_act(act)

            @block.vector
            def _(dve):
                on_dve(dve)

            @block.tensor
            def _(pe):
                keep_busy(ps[7], 4)
                on_pe(pe)

    with ExitStack() as tail:
        mix_hi = sb(tail, "mix_hi_od", [P, KT, SEQ], F32R)
        mix_lo = sb(tail, "mix_lo_od", [P, KT, SEQ], F32R)
        turned, hi_out = sem("od_turned"), sem("od_hi_out")
        with ExitStack() as ph:
            ps = banks(ph, "odmix")
            with nc.Block() as block:
                @block.tensor
                def _(pe):
                    for f in range(KT):
                        for qt in range(NQT):
                            tr = nc.tensor.transpose(ps[f][:, qt * P:(qt + 1) * P], o_acc[:, qt, f * P:(f + 1) * P], ident)
                        tr.then_inc(turned, 1)

                @block.scalar
                def _(act):
                    for f in range(KT):
                        act.wait_ge(turned, f + 1)
                        nc.scalar.activation(mix_hi[:, f, :], ps[f][:], ACT.Copy).then_inc(hi_out, 1)

                @block.vector
                def _(dve):
                    for f in range(KT):
                        dve.wait_ge(hi_out, f + 1)
                        nc.vector.tensor_tensor(mix_lo[:, f, :], ps[f][:], mix_hi[:, f, :].bitcast(F32), ALU.subtract)
        project_residual("od_out", mix_hi, mix_lo)
    att.close()
    odd.close()

    ffn(1)

    with ExitStack() as ph:
        y = sb(ph, "y", [P, KT, SEQ])
        ps = banks(ph, "fin")
        n_act, n_pe, n_dve, _, y_before = norm_parts(y, ps[0], const("g_final"))
        stored = sem("stored")
        with nc.Block() as block:
            @block.scalar
            def _(act):
                n_act(act)

            @block.tensor
            def _(pe):
                n_pe(pe)

            @block.vector
            def _(dve):
                n_dve(dve)

            @block.sync
            def _(sp):
                for k in range(KT):
                    sp.wait_ge(norm_sems["xn"], y_before + k + 1)
                    sp.dma_start(out_t[:, k, :], y[:, k, :]).then_inc(stored, 16)
                sp.wait_ge(stored, 16 * KT)
    whole.close()


def _unit(w, cols, k0=0):
    n = min(UK, w.shape[0] // P - k0)
    u = np.zeros((P, UK, UM * P), np.float32)
    u[:, :n] = w[k0 * P:(k0 + n) * P, cols:cols + UM * P].reshape(n, P, UM * P).transpose(1, 0, 2)
    return u.reshape(P, -1)


def _blocks(bs):
    u = np.zeros((P, UK * UM * P), np.float32)
    at = 0
    for b in bs:
        u[:, at:at + b.shape[1]] = b
        at += b.shape[1]
    return u


def _stream(a):
    w = a["ev_w_in"][0]
    zq = Q_RANK + KV_RANK + ROPE
    ba = zq + 4 * GDN_HEADS * GDN_D
    kr = w[:, Q_RANK + KV_RANK:zq]
    small = np.concatenate([w[:, ba:ba + 8], np.zeros((D_MODEL, 56), np.float32), kr,
                            kr[:, ROPE // 2:], kr[:, :ROPE // 2]], axis=1)
    units = [_unit(w, 0), _unit(w, 256), _unit(np.concatenate([w[:, 512:640], small], axis=1), 0)]
    units += [_unit(w, zq + 256 * j) for j in range(8)]
    uq = a["ev_w_uq"][0].reshape(3, P, MLA_HEADS, NOPE + ROPE)
    half = NOPE + ROPE // 2
    uq = np.concatenate([uq, uq[..., half:], uq[..., NOPE:half]], axis=-1)
    for heads in (range(5), range(5, 8)):
        units.append(_blocks([uq[k, :, hd] for hd in heads for k in range(3)]))
    ukv = a["ev_w_ukv"][0].reshape(2, P, MLA_HEADS, NOPE + MLA_V)
    units.append(_blocks([ukv[k, :, 2 * j:2 * j + 2, :NOPE].reshape(P, P) for j in range(4) for k in range(2)]
                         + [ukv[k, :, :, NOPE:].reshape(P, -1) for k in range(2)]))
    units += [_unit(a["ev_w_out"][0], 256 * j) for j in range(4)]

    def ffn(n):
        g, u, d = a["ffn_w_gate"][n], a["ffn_w_up"][n], a["ffn_w_down"][n]
        return [_unit(m, 256 * j) for j in range(FT // 2) for m in (g, u)] + \
               [_unit(d, 256 * j, UK * r) for j in range(KT // 2) for r in range(3)]
    units += ffn(0)
    w = a["od_w_in"][0]
    units += [_unit(w, 256 * j) for j in (0, 1, 2, 3, 4, 5, 6, 8, 7, 9)]
    units += [_unit(a[n][0], 0, UK * r) for n in ("od_w1_k", "od_w1_v") for r in range(2)]
    units += [_unit(a["od_w_out"][0], 256 * j) for j in range(4)]
    units += ffn(1)
    assert len(units) == N_UNITS
    return np.stack(units)


def _consts(a):
    c = np.zeros((P, N_COLS), np.float32)

    def put(name, v):
        s, e = COLS[name]
        c[:, s:e] = v
    i = np.arange(P)
    put("ident", np.eye(P, dtype=np.float32))
    put("utri", (i[:, None] <= i[None, :]).astype(np.float32))
    put("ones", 1.0)
    j_, i_ = i[:, None], i[None, :]
    put("level", np.concatenate([((i_ >> (l + 1) == j_ >> (l + 1)) & ((i_ >> l) % 2 == 1) & ((j_ >> l) % 2 == 0))
                                 for l in range(7)], axis=1).astype(np.float32))
    half = ROPE // 2
    inv = np.float32(10000.0) ** (-np.arange(half, dtype=np.float32) / np.float32(half))
    ang = np.arange(SEQ, dtype=np.float32)[None, :] * inv.astype(np.float32)[:, None]
    rope = np.zeros((P, SEQ), np.float32)
    rope[64:96] = np.concatenate([np.cos(ang)] * 2)
    rope[96:128] = np.concatenate([-np.sin(ang), np.sin(ang)])
    put("rope", rope)
    rel = np.arange(SEQ)[None, :] - (SEQ - P) - i[:, None]
    put("rel", np.where(rel <= 0, rel, NEG).astype(np.float32))
    put("causal", np.where(rel <= 0, 0.0, NEG).astype(np.float32))
    pos = (np.arange(NQT)[None, :] * P + i[:, None]).astype(np.float32)
    put("any_valid", (pos >= CMP_BLOCK - 1).astype(np.float32))
    slopes = (2.0 ** (-8.0 * np.arange(1, NSA_HEADS + 1, dtype=np.float32) / NSA_HEADS)).astype(np.float32)
    scale = np.float32(NSA_DIM ** 0.5)
    put("slope", (slopes * scale)[None, :])
    n = np.arange(NCMP)
    centre = (n * CMP_STRIDE + 0.5 * (CMP_BLOCK - 1)).astype(np.float32)
    valid = (n * CMP_STRIDE + CMP_BLOCK - 1)[None, None, :] <= pos[:, :, None]
    bias = (slopes * scale)[None, None, :, None] * (centre[None, None, None, :] - pos[:, :, None, None])
    bias = np.where(valid[:, :, None, :], bias, NEG).astype(np.float32)
    for name, v in (("g_ev", a["ev_attn_norm"][0]), ("g_od", a["od_attn_norm"][0]), ("g_ffn0", a["ffn_norm"][0]),
                    ("g_ffn1", a["ffn_norm"][1]), ("g_final", a["final_norm"]), ("g_q", a["ev_q_norm"][0]),
                    ("g_kv", a["ev_kv_norm"][0]), ("g_gdn", a["ev_gdn_norm"][0]),
                    ("pe_k", a["od_pe_k"][0].reshape(-1)), ("pe_v", a["od_pe_v"][0].reshape(-1))):
        put(name, v.reshape(-1, P).T)
    put("conv", a["ev_conv_w"][0].reshape(GDN_CONV, 12, P).transpose(2, 1, 0).reshape(P, -1))
    put("a_log", a["ev_a_log"])
    put("dt_bias", a["ev_dt_bias"])
    put("eps", EPS)
    g0 = NSA_HEADS * NSA_DIM + 6 * NSA_GROUPS * NSA_DIM
    put("w_gate", a["od_w_in"][0][:, g0:].reshape(KT, P, 48).transpose(1, 0, 2).reshape(P, -1))
    return c, bias.reshape(P, -1)


def kernel(**inputs):
    import concourse.bacc as bacc
    from concourse.bass_utils import run_bass_kernel_spmd

    a = {k: np.asarray(v) for k, v in inputs.items()}
    consts, cmp_bias = _consts(a)
    arrays = {
        "x_t": np.ascontiguousarray(a["x"][0].T.reshape(KT, P, SEQ).transpose(1, 0, 2)),
        "stream": _stream(a),
        "consts": consts,
        "cmp_bias": cmp_bias,
        "w2": np.ascontiguousarray(np.stack([a["od_w2_k"][0], a["od_w2_v"][0]]).reshape(2, 2, P, NSA_DIM)
                                   .transpose(2, 0, 1, 3).reshape(P, -1)),
    }
    nc = bacc.Bacc("TRN2", target_bir_lowering=False, num_devices=1, dynamic_dma_scratch_size=1024)
    args = [nc.dram_tensor(n, v.shape, mybir.dt.float32, kind="ExternalInput").ap() for n, v in arrays.items()]
    out = nc.dram_tensor("out_t", (P, KT, SEQ), mybir.dt.float32, kind="ExternalOutput").ap()
    build_program(nc, *args, out)
    res = run_bass_kernel_spmd(nc, [arrays], core_ids=[0])
    got = res.results[0]["out_t"]
    return np.ascontiguousarray(got.transpose(1, 0, 2).reshape(D_MODEL, SEQ).T)[None]
```

```python
import math
from contextlib import ExitStack

import numpy as np

import concourse.bass as bass
from concourse import mybir

D_MODEL, SEQ, EPS = 1024, 512, 1e-6
MLA_HEADS, Q_RANK, KV_RANK, NOPE, ROPE, MLA_V = 8, 384, 256, 64, 32, 64
GDN_HEADS, GDN_D, GDN_CONV = 4, 128, 4
NSA_HEADS, NSA_GROUPS, NSA_DIM = 16, 4, 64
NSA_HPG = NSA_HEADS // NSA_GROUPS
CMP_BLOCK, CMP_STRIDE, CMP_HIDDEN = 32, 16, 256
FFN_HIDDEN = ((8 * D_MODEL + 3 * 256 - 1) // (3 * 256)) * 256
P = 128
KT = D_MODEL // P
NQT = SEQ // P
FT = FFN_HIDDEN // P
UK, UM = 8, 2
NCMP = 32
NEG = -1e30
BIG = 3.0e38

UNITS = {}
_at = 0
for _name, _n in (("ev_in", 11), ("mla", 3), ("ev_out", 4), ("gu0", FT), ("down0", 12), ("od_in", 10),
                  ("cmp", 4), ("od_out", 4), ("gu1", FT), ("down1", 12)):
    UNITS[_name] = (_at, _at + _n)
    _at += _n
N_UNITS = _at

COLS = {}
_at = 0
for _name, _n in (("ones", P), ("eps", 1), ("g_ev", KT), ("ident", P), ("utri", P), ("level", 7 * P), ("rope", SEQ),
                  ("rel", SEQ), ("causal", SEQ), ("any_valid", NQT),
                  ("g_od", KT), ("g_ffn0", KT), ("g_ffn1", KT), ("g_final", KT),
                  ("g_q", 3), ("g_kv", 2), ("g_gdn", 1), ("conv", 12 * GDN_CONV), ("a_log", GDN_HEADS),
                  ("dt_bias", GDN_HEADS), ("slope", NSA_HEADS), ("pe_k", 16), ("pe_v", 16), ("w_gate", KT * 48)):
    COLS[_name] = (_at, _at + _n)
    _at += _n
N_COLS = _at
FIRST_COLS = COLS["g_ev"][1]


def build_program(nc, x_t, stream, consts, cmp_bias_in, w2_in, out_t, dbg=None):
    F32, F32R = mybir.dt.float32, mybir.dt.float32r
    ACT, ALU, AX = mybir.ActivationFunctionType, mybir.AluOpType, mybir.AxisListType
    whole = ExitStack()

    def sb(ctx, name, shape, dt=F32, side=None):
        return ctx.enter_context(nc.sbuf_tensor(name, shape, dt, side=side))

    def banks(ctx, tag):
        return [ctx.enter_context(nc.psum_tensor(f"ps_{tag}{i}", [P, 512], F32)) for i in range(8)]

    sem_of = {}

    def sem(name):
        sem_of[name] = whole.enter_context(nc.semaphore(name))
        return sem_of[name]

    cst = sb(whole, "cst", [P, N_COLS])
    h = sb(whole, "h", [P, KT, SEQ])
    raw = sb(whole, "raw", [P, 2, UK * UM * P])
    whi = sb(whole, "whi", [P, 2, UK * UM * P], F32R)
    wlo = sb(whole, "wlo", [P, 2, UK * UM * P], F32R)

    def const(name, rows=slice(0, P)):
        a, b = COLS[name]
        return cst[rows, a:b]

    ident, utri, ones = const("ident"), const("utri"), const("ones")
    eps = const("eps")

    unit_landed = [sem("unit_landed0"), sem("unit_landed1")]
    hi_ready, lo_ready, tiles_done = sem("hi_ready"), sem("lo_ready"), sem("tiles_done")

    def load_unit(sp, u, slot, landed):
        sp.wait_ge(lo_ready, u - 1)
        sp.dma_start(raw[:, slot, :], stream[u]).then_inc(landed, 16)

    def load_units(sp, name):
        a, b = UNITS[name][0] + 2, min(UNITS[name][1] + 2, N_UNITS)
        pairs = (b - a) // 2
        if pairs == 1:
            load_unit(sp, a, a % 2, unit_landed[a % 2])
            load_unit(sp, a + 1, (a + 1) % 2, unit_landed[(a + 1) % 2])
        elif pairs:
            with sp.Fori(0, pairs) as i:
                for s in range(2):
                    load_unit(sp, a + s + 2 * i, (a + s) % 2, unit_landed[(a + s) % 2])
        if (b - a) % 2:
            load_unit(sp, b - 1, (b - 1) % 2, unit_landed[(b - 1) % 2])

    def split_hi(act, base, i):
        s = base % 2
        act.wait_ge(unit_landed[s], 16 * (base // 2 + 1) + 16 * i)
        if not (isinstance(i, int) and base + 2 * i < 2):
            act.wait_ge(tiles_done, 2 * (base - 1) + 4 * i)
        nc.scalar.activation(whi[:, s, :], raw[:, s, :], ACT.Copy).then_inc(hi_ready, 1)

    def split_lo(engine, base, i, on=nc.gpsimd):
        s = base % 2
        engine.wait_ge(hi_ready, base + 1 + 2 * i)
        on.tensor_tensor(wlo[:, s, :], raw[:, s, :], whi[:, s, :].bitcast(F32),
                                ALU.subtract).then_inc(lo_ready, 1)

    def split_los(pool, name):
        a, b = UNITS[name][0] + 1, min(UNITS[name][1] + 1, N_UNITS)
        if (b - a) // 2 == 1:
            split_lo(pool, a, 0)
            split_lo(pool, a + 1, 0)
        elif (b - a) // 2:
            with pool.Fori(0, (b - a) // 2) as i:
                split_lo(pool, a, i)
                split_lo(pool, a + 1, i)
        if (b - a) % 2:
            split_lo(pool, b - 1, 0)

    def three_passes(acc, lhs_hi, lhs_lo, rhs_hi, rhs_lo, start, stop):
        nc.tensor.matmul(acc, lhs_hi, rhs_hi, start=start, stop=False)
        nc.tensor.matmul(acc, lhs_hi, rhs_lo, start=False, stop=False)
        return nc.tensor.matmul(acc, lhs_lo, rhs_hi, start=False, stop=stop)

    def unit_block(s, k, m):
        c = (k * UM + m) * P
        return whi[:, s, c:c + P], wlo[:, s, c:c + P]

    def column_tile(acc, s, m, x_hi, x_lo, k0=0, nk=UK, first=True, last=True):
        for k in range(nk):
            w_hi, w_lo = unit_block(s, k, m)
            mm = three_passes(acc, w_hi, w_lo, x_hi[:, k0 + k, :], x_lo[:, k0 + k, :],
                              first and k == 0, last and k == nk - 1)
        return mm

    norm_sems = {n: sem("norm_" + n) for n in ("sq", "summed", "ms", "ln", "rstd", "xn", "xh", "xl")}
    sumsq = sb(whole, "sumsq", [P, SEQ])
    norms, sums = [0], [0]
    added = sem("added")

    def square_sum(sq2):
        n = sums[0]
        sums[0] += 1
        s = norm_sems
        SQ, SM = KT * n, (KT + 1) * n

        def clear(dve):
            if n:
                dve.wait_ge(s["xn"], KT * n)
            nc.vector.memset(sumsq[:], 0.0).then_inc(s["summed"], 1)

        def square(act, t):
            if t >= 2:
                act.wait_ge(s["summed"], SM + t)
            nc.scalar.activation(sq2[:, t % 2, :], h[:, t, :], ACT.Square).then_inc(s["sq"], 1)

        def add(dve, t):
            dve.wait_ge(s["sq"], SQ + t + 1)
            dve.wait_ge(s["summed"], SM + t + 1)
            nc.vector.tensor_tensor(sumsq[:], sumsq[:], sq2[:, t % 2, :], ALU.add).then_inc(s["summed"], 1)
        def total(pe, bank):
            pe.wait_ge(s["summed"], (KT + 1) * (n + 1))
            nc.tensor.matmul(bank[:], ones, sumsq[:], start=True, stop=True).then_inc(s["ms"], 1)

        def rsqrt(act, bank):
            act.wait_ge(s["ms"], n + 1)
            nc.scalar.activation(sumsq[:], bank[:], ACT.Ln, bias=eps, scale=1.0 / D_MODEL).then_inc(s["ln"], 1)
            act.wait_ge(s["ln"], n + 1)
            nc.scalar.activation(sumsq[:], sumsq[:], ACT.Exp, scale=-0.5).then_inc(s["rstd"], 1)
        return clear, square, add, total, rsqrt

    def keep_busy(bank, n, moving=None):
        for _ in range(n):
            nc.tensor.matmul(bank[:, 0:256], ones, cst[:, 0:256] if moving is None else moving, start=True, stop=True)

    def norm_parts(xn, gain, xh=None, xl=None):
        n = norms[0]
        norms[0] += 1
        nk = KT * n
        s = norm_sems

        def on_act(act, next_unit):
            for k in range(KT):
                if k == 2:
                    split_hi(act, next_unit, 0)
                act.wait_ge(s["xn"], nk + k + 1)
                nc.scalar.activation(xh[:, k, :], xn[:, k, :], ACT.Copy).then_inc(s["xh"], 1)

        def on_dve(dve):
            def lo(k):
                dve.wait_ge(s["xh"], nk + k + 1)
                nc.vector.tensor_tensor(xl[:, k, :], xn[:, k, :], xh[:, k, :].bitcast(F32),
                                        ALU.subtract).then_inc(s["xl"], 1)
            dve.wait_ge(s["rstd"], n + 1)
            for k in range(KT):
                nc.vector.scalar_tensor_tensor(out=xn[:, k, :], in0=h[:, k, :], scalar=gain[:, k:k + 1],
                                               in1=sumsq[:], op0=ALU.mult, op1=ALU.mult).then_inc(s["xn"], 1)
                if xh is not None and k:
                    lo(k - 1)
            if xh is not None:
                lo(KT - 1)

        def wait_tile(pe, k):
            pe.wait_ge(s["xl"], nk + k + 1)

        return on_act, on_dve, wait_tile, nk

    def first_unit(pe, u, banks2, xh, xl, wait_tile):
        pe.wait_ge(lo_ready, u + 1)
        for k in range(KT):
            wait_tile(pe, k)
            for m in range(2):
                w_hi, w_lo = unit_block(u % 2, k, m)
                mm = three_passes(banks2[m][:], w_hi, w_lo, xh[:, k, :], xl[:, k, :], k == 0, k == KT - 1)
                if k == KT - 1:
                    mm.then_inc(tiles_done, 1)

    def attention(tag, n_groups, per_group, c, s_banks, t_banks, o_banks, prob, prob_t, neg_max, row_sum,
                  products, values, bias, take, before_head=None):
        n_heads = n_groups * per_group
        n_items = NQT * n_heads
        scores_done, biased = sem(f"scores_{tag}"), sem(f"biased_{tag}")
        probs_ready, turned = sem(f"probs_{tag}"), sem(f"turned_{tag}")
        copied = [sem(f"copied_even_{tag}"), sem(f"copied_odd_{tag}")]
        pv_done, o_taken = sem(f"pv_{tag}"), sem(f"o_taken_{tag}")
        LAG = 3

        def width(qt):
            return (qt + 1) * P

        def copy(engine, do, a, qt):
            engine.wait_ge(turned, NQT * a + qt + 1)
            if not (isinstance(a, int) and NQT * a + qt < 2):
                engine.wait_ge(pv_done, NQT * a + qt - 1)
            do(prob_t[:, qt % 2, 0:width(qt)], t_banks[qt % 2][:, 0:width(qt)]).then_inc(copied[qt % 2], 1)

        def act_copy(out, in_):
            return nc.scalar.activation(out, in_, ACT.Copy)

        def on_act(act):
            def group(g, first):
                for br in range(per_group):
                    a = per_group * g + br
                    for qt in range(NQT):
                        act.wait_ge(biased, NQT * a + qt + 1)
                        nc.scalar.activation(prob[:, qt, 0:width(qt)], prob[:, qt, 0:width(qt)], ACT.Exp,
                                             bias=neg_max[:, qt:qt + 1], scale=-1.0,
                                             accum_out=row_sum(g, br)[:, qt:qt + 1]).then_inc(probs_ready, 1)
                        if qt == 0 and not (first and br == 0):
                            copy(act, act_copy, a - 1, 2)
                        if qt == 2:
                            copy(act, act_copy, a, 0)
            group(0, True)
            with act.Fori(1, n_groups) as g:
                group(g, False)
            copy(act, act_copy, n_heads - 1, 2)

        def on_dve(dve):
            def group(g, first):
                if before_head is not None:
                    before_head(dve, g)
                for br in range(per_group):
                    a = per_group * g + br
                    for qt in range(NQT):
                        dve.wait_ge(scores_done, NQT * a + qt + 1)
                        if not (first and br == 0):
                            dve.wait_ge(turned, NQT * a + qt - 3)
                        nc.vector.tensor_tensor_reduce(
                            out=prob[:, qt, 0:width(qt)], in0=s_banks[qt][:, 0:width(qt)], in1=bias(g, qt),
                            scale=-c, scalar=BIG, op0=ALU.add, op1=ALU.min,
                            accum_out=neg_max[:, qt:qt + 1]).then_inc(biased, 1)
                        if qt == 2 and a:
                            copy(dve, nc.vector.tensor_copy, a - 1, 3)
                        if qt == 0 and a:
                            copy(dve, nc.vector.tensor_copy, a - 1, 1)
                            if a >= 2:
                                dve.wait_ge(pv_done, NQT * (a - 1))
                                gb = divmod(a - 2, per_group)
                                take(dve, *gb, o_banks[gb[1]]).then_inc(o_taken, 1)
            for g in range(n_groups):
                group(g, g == 0)
            for qt in (1, 3):
                copy(dve, nc.vector.tensor_copy, n_heads - 1, qt)
            for a in (n_heads - 2, n_heads - 1):
                dve.wait_ge(pv_done, NQT * (a + 1))
                gb = divmod(a, per_group)
                take(dve, *gb, o_banks[gb[1]]).then_inc(o_taken, 1)

        def on_pe(pe):
            for t in range(n_items + LAG + 1):
                if t < n_items:
                    a, qt = divmod(t, NQT)
                    if t >= 4:
                        pe.wait_ge(biased, t - 3)
                    pairs = products(pe, a, qt, width(qt))
                    for n, (q, k) in enumerate(pairs):
                        mm = nc.tensor.matmul(s_banks[qt][:, 0:width(qt)], q, k, start=n == 0, stop=n == len(pairs) - 1)
                    mm.then_inc(scores_done, 1)
                if LAG <= t < n_items + LAG:
                    a, qt = divmod(t - LAG, NQT)
                    pe.wait_ge(probs_ready, t - LAG + 1)
                    if t >= LAG + 2:
                        pe.wait_ge(copied[qt % 2], (t - LAG - 2) // 2 + 1)
                    for kt in range(qt + 1):
                        tr = nc.tensor.transpose(t_banks[qt % 2][:, kt * P:(kt + 1) * P],
                                                 prob[:, qt, kt * P:(kt + 1) * P], ident)
                    tr.then_inc(turned, 1)
                if t > LAG:
                    a, qt = divmod(t - LAG - 1, NQT)
                    pe.wait_ge(copied[qt % 2], (t - LAG - 1) // 2 + 1)
                    if qt == 0 and a >= 2:
                        pe.wait_ge(o_taken, a - 1)
                    for kt in range(qt + 1):
                        pv = nc.tensor.matmul(o_banks[a % 2][:, qt * P:(qt + 1) * P],
                                              prob_t[:, qt % 2, kt * P:(kt + 1) * P], values(a, kt),
                                              start=(kt == 0), stop=(kt == qt))
                    pv.then_inc(pv_done, 1)
        return on_act, on_dve, on_pe

    even, even_in = ExitStack(), ExitStack()
    zg = sb(even, "zg", [P, GDN_HEADS, SEQ])
    misc = sb(even, "misc", [P, SEQ])
    qkv = sb(even, "qkv", [P, 12, SEQ])
    NC, HD, C = NQT, GDN_HEADS, P
    ba = sb(even, "g_ba", [P, NC, 8])
    col = {n: sb(even, "g_" + n, [P, NC, HD]) for n in ("beta", "soft", "tmp", "g", "gc", "egc", "bg", "last", "kd", "elast", "ea", "nbeta")}
    lat = sb(even_in, "lat", [P, 5, SEQ])

    in_landed, second_landed, consts_landed = sem("in_landed"), sem("second_landed"), sem("consts_landed")
    with ExitStack() as ph:
        xh, xl = sb(ph, "xh_ev", [P, KT, SEQ], F32R), sb(ph, "xl_ev", [P, KT, SEQ], F32R)
        xn, sq2 = sb(ph, "xn_ev", [P, KT, SEQ]), sb(ph, "sq2_ev", [P, 2, SEQ])
        ps = banks(ph, "evin")
        clear, square, add_square, total, rsqrt_mean = square_sum(sq2)
        n_act, n_dve, wait_tile, _ = norm_parts(xn, const("g_ev"), xh, xl)
        z = sb(ph, "z", [P, 4, SEQ + 4])
        conv_w = const("conv")
        conv_step, conv_ready, padded_z = sem("conv_step"), sem("conv_ready"), sem("padded_z")
        out_a, out_v = sem("evin_out_act"), sem("evin_out_dve")
        with nc.Block() as block:
            @block.sync
            def _(sp):
                sp.dma_start(cst[:, 0:FIRST_COLS], consts[:, 0:FIRST_COLS]).then_inc(in_landed, 16)
                sp.dma_start(raw[:, 0, :], stream[0]).then_inc(unit_landed[0], 16)
                sp.dma_start(h[:, 0:KT // 2, :], x_t[:, 0:KT // 2, :]).then_inc(in_landed, 16)
                sp.dma_start(h[:, KT // 2:KT, :], x_t[:, KT // 2:KT, :]).then_inc(second_landed, 16)
                sp.dma_start(cst[:, FIRST_COLS:N_COLS], consts[:, FIRST_COLS:N_COLS]).then_inc(consts_landed, 16)
                sp.dma_start(raw[:, 1, :], stream[1]).then_inc(unit_landed[1], 16)
                load_units(sp, "ev_in")

            @block.gpsimd
            def _(pool):
                nc.gpsimd.memset(z[:, :, 0:3], 0.0).then_inc(padded_z, 1)
                split_lo(pool, 0, 0)
                split_los(pool, "ev_in")

            def out_of(t):
                return lat[:, t, :] if t < 5 else misc[:]

            @block.scalar
            def _(act):
                act.preload_act_table_set("natural_log_exp_and_others")
                split_hi(act, 0, 0)
                act.wait_ge(in_landed, 32)
                for t in range(KT):
                    if t == KT // 2:
                        act.wait_ge(second_landed, 16)
                    square(act, t)
                rsqrt_mean(act, ps[4])
                n_act(act, 1)
                for u in range(3):
                    if u:
                        split_hi(act, u + 1, 0)
                    act.wait_ge(tiles_done, 2 * u + 1)
                    nc.scalar.activation(out_of(2 * u), ps[2 * u % 4][:], ACT.Copy).then_inc(out_a, 1)

                act.preload_act_table(ACT.Silu)

                def silu(t, i):
                    act.wait_ge(conv_ready, t + 1 + 4 * i)
                    tile = qkv[:, t + 4 * i, :]
                    nc.scalar.activation(tile, tile, ACT.Silu)

                def z_unit(i, s):
                    split_hi(act, 4 + s, i)
                    act.wait_ge(tiles_done, 6 + 2 * s + 1 + 4 * i)
                    if not isinstance(i, int):
                        act.wait_ge(conv_ready, 4 * i + 2 * s - 3)
                    nc.scalar.activation(z[:, 2 * s, 3:3 + SEQ], ps[(2 + 2 * s) % 4][:], ACT.Copy).then_inc(out_a, 1)
                    if s or not isinstance(i, int):
                        for m in range(2):
                            silu(2 * s - 2 + m, i)
                for s in range(2):
                    z_unit(0, s)
                with act.Fori(1, 3) as i:
                    for s in range(2):
                        z_unit(i, s)
                for s in range(2):
                    split_hi(act, 10 + s, 0)
                    for m in range(2):
                        act.wait_ge(tiles_done, 18 + 2 * s + m + 1)
                        nc.scalar.activation(zg[:, 2 * s + m, :], ps[(2 + 2 * s) % 4 + m][:], ACT.Silu)
                    if s == 0:
                        for m in range(2):
                            silu(10 + m, 0)

            @block.vector
            def _(dve):
                clear(dve)
                for t in range(KT):
                    add_square(dve, t)
                dve.wait_ge(in_landed, 32)
                dve.wait_ge(second_landed, 16)
                n_dve(dve)
                for u in range(3):
                    dve.wait_ge(tiles_done, 2 * u + 2)
                    nc.vector.tensor_copy(out_of(2 * u + 1), ps[(2 * u + 1) % 4][:]).then_inc(out_v, 1)

                dve.wait_ge(padded_z, 1)
                dve.wait_ge(consts_landed, 16)

                def z_unit(i, s):
                    dve.wait_ge(tiles_done, 6 + 2 * s + 2 + 4 * i)
                    if not isinstance(i, int):
                        dve.wait_ge(conv_ready, 4 * i + 2 * s - 2)
                    nc.vector.tensor_copy(z[:, 2 * s + 1, 3:3 + SEQ], ps[(3 + 2 * s) % 4][:]).then_inc(out_v, 1)
                    dve.wait_ge(out_a, 4 + s + 2 * i)
                    dve.wait_ge(out_v, 4 + s + 2 * i)
                    for m in range(2):
                        t = 4 * i + 2 * s + m
                        w = conv_w[:, bass.ds(t * GDN_CONV, GDN_CONV)]
                        tile = z[:, 2 * s + m, :]
                        nc.vector.tensor_scalar(qkv[:, t, :], tile[:, 0:SEQ], w[:, 0:1], None, ALU.mult).then_inc(conv_step, 1)
                        for j in range(1, GDN_CONV):
                            dve.wait_ge(conv_step, 3 * t + j)
                            nc.vector.scalar_tensor_tensor(out=qkv[:, t, :], in0=tile[:, j:j + SEQ], scalar=w[:, j:j + 1],
                                                           in1=qkv[:, t, :], op0=ALU.mult, op1=ALU.add
                                                           ).then_inc(conv_step if j < GDN_CONV - 1 else conv_ready, 1)
                for s in range(2):
                    z_unit(0, s)
                with dve.Fori(1, 3) as i:
                    for s in range(2):
                        z_unit(i, s)

            @block.tensor
            def _(pe):
                pe.wait_ge(in_landed, 32)
                keep_busy(ps[5], 10, h[:, 0, 0:256])
                total(pe, ps[4])
                keep_busy(ps[5], 6, h[:, 0, 0:256])

                def unit(u, i):
                    pe.wait_ge(lo_ready, u + 1 + 2 * i)
                    b = 2 * (u % 2)
                    if not (isinstance(i, int) and u < 2):
                        pe.wait_ge(out_a, u - 1 + 2 * i)
                        pe.wait_ge(out_v, u - 1 + 2 * i)
                    column_tile(ps[b][:], u % 2, 0, xh, xl).then_inc(tiles_done, 1)
                    column_tile(ps[b + 1][:], u % 2, 1, xh, xl).then_inc(tiles_done, 1)

                first_unit(pe, 0, ps[0:2], xh, xl, wait_tile)
                for u in range(1, 3):
                    unit(u, 0)
                with pe.Fori(0, 4) as i:
                    unit(3, i)
                    unit(4, i)

    mla = ExitStack()
    q_all = sb(mla, "q_all", [96, MLA_HEADS, SEQ], side="right")
    k_all = sb(mla, "k_all", [96, MLA_HEADS, SEQ], side="right")
    v_all = sb(mla, "v_all", [P, NQT, MLA_HEADS * MLA_V], side="right")
    with ExitStack() as ph:
        lat_hi, lat_lo = sb(ph, "lat_hi", [P, 5, SEQ], F32R), sb(ph, "lat_lo", [P, 5, SEQ], F32R)
        sq, rstd = sb(ph, "sq_lat", [P, 5, SEQ]), sb(ph, "rstd_lat", [P, 2, SEQ])
        rot_a, rot_b = sb(ph, "rot_a", [P, 2, SEQ]), sb(ph, "rot_b", [P, 2, SEQ])
        gsq, norm = sb(ph, "g_sq", [P, 4, SEQ]), sb(ph, "g_rnorm", [P, 2, SEQ])
        S_ = {n: sem("gdn_" + n) for n in (
            "sq", "ms", "ln", "rs", "normed", "ba_turned", "ba_out", "beta_exp", "act_col", "dve_col", "dve_step",
            "g_ready", "gc_done", "gc_out", "last_diff")}
        ps = banks(ph, "lat")
        g_lat = cst[:, COLS["g_q"][0]:COLS["g_kv"][1]]
        rope = const("rope")
        lat_sq, lat_ms, lat_ln, lat_rstd = sem("lat_sq"), sem("lat_ms"), sem("lat_ln"), sem("lat_rstd")
        lat_scaled, lat_hi_ready, lat_ready = sem("lat_scaled"), sem("lat_hi_ready"), sem("lat_ready")
        head_done, nope_out, rot_done, rope_out = sem("head_done"), sem("nope_out"), sem("rot_done"), sem("rope_out")
        kr_mul, kr_ready, kr_out = sem("kr_mul"), sem("kr_ready"), sem("kr_out")
        kv_done, kv_out_a, kv_out_v = sem("kv_done"), sem("kv_out_act"), sem("kv_out_dve")
        U = UNITS["mla"][0]
        PARTS = ((0, 3, Q_RANK), (3, 5, KV_RANK))

        def wait_head(e, hd):
            if hd == 4:
                e.wait_ge(tiles_done, 2 * (U + 1))
            elif hd == 7:
                e.wait_ge(tiles_done, 2 * (U + 2))
            else:
                e.wait_ge(head_done, hd + 1 - (hd > 4))

        def chained(engine, s):
            n = [0]

            def step(ins):
                ins.then_inc(s, 1)
                n[0] += 1
                engine.wait_ge(s, n[0])
            return step

        with nc.Block() as block:
            @block.sync
            def _(sp):
                load_units(sp, "mla")

            @block.gpsimd
            def _(pool):
                def square(t):
                    if t >= 4:
                        pool.wait_ge(S_["ms"], t - 3)
                    nc.gpsimd.tensor_tensor(gsq[:, t % 4, :], qkv[:, t, :], qkv[:, t, :], ALU.mult).then_inc(S_["sq"], 1)
                for t in range(4):
                    square(t)
                split_lo(pool, U + 1, 0)
                for t in range(4, 8):
                    square(t)
                pool.wait_ge(S_["sq"], 8)
                pool.wait_ge(kr_mul, 2)
                for hd in range(MLA_HEADS):
                    nc.gpsimd.tensor_tensor(k_all[64:96, hd, :], rot_a[64:96, 1, :], rot_b[64:96, 1, :],
                                            ALU.add).then_inc(kr_out, 1)
                pool.wait_ge(kr_out, MLA_HEADS)
                split_lo(pool, U + 2, 0)
                split_lo(pool, U + 3, 0)

            @block.scalar
            def _(act):
                act.preload_act_table_set("natural_log_exp_and_others")
                for t in range(5):
                    nc.scalar.activation(sq[:, t, :], lat[:, t, :], ACT.Square).then_inc(lat_sq, 1)
                for n, (a, b, rank) in enumerate(PARTS):
                    act.wait_ge(lat_ms, n + 1)
                    nc.scalar.activation(rstd[:, n, :], ps[n][:], ACT.Ln, bias=eps,
                                         scale=1.0 / rank).then_inc(lat_ln, 1)
                act.wait_ge(lat_ln, 2)
                for n in range(2):
                    nc.scalar.activation(rstd[:, n, :], rstd[:, n, :], ACT.Exp, scale=-0.5).then_inc(lat_rstd, 1)
                for t in range(5):
                    act.wait_ge(lat_scaled, t + 1)
                    nc.scalar.activation(lat_hi[:, t, :], sq[:, t, :], ACT.Copy,
                                         scale=g_lat[:, t:t + 1]).then_inc(lat_hi_ready, 1)
                split_hi(act, U + 1, 0)
                for hd in range(MLA_HEADS):
                    wait_head(act, hd)
                    nc.scalar.activation(q_all[0:64, hd, :], ps[2 + hd % 2][0:64, :], ACT.Copy).then_inc(nope_out, 1)
                    t = hd
                    act.wait_ge(S_["ms"], t + 1)
                    if t >= 2:
                        act.wait_ge(S_["normed"], t - 1)
                    nc.scalar.activation(norm[:, t % 2, :], ps[6 + t % 2][:], ACT.Ln, bias=eps).then_inc(S_["ln"], 1)
                    act.wait_ge(S_["ln"], t + 1)
                    nc.scalar.activation(norm[:, t % 2, :], norm[:, t % 2, :], ACT.Exp, scale=-0.5).then_inc(S_["rs"], 1)
                    if hd == 1:
                        act.wait_ge(S_["ba_out"], 1)
                        nc.scalar.activation(col["beta"][:], ba[:, :, 0:4], ACT.Exp, scale=-1.0).then_inc(S_["beta_exp"], 1)
                        act.wait_ge(S_["dve_col"], 1)
                        step = chained(act, S_["act_col"])
                        step(nc.scalar.activation(col["tmp"][:], col["soft"][:], ACT.Abs))
                        step(nc.scalar.activation(col["tmp"][:], col["tmp"][:], ACT.Exp, scale=-1.0))
                        step(nc.scalar.activation(col["tmp"][:], col["tmp"][:], ACT.Ln, bias=1.0))
                        step(nc.scalar.activation(col["ea"][:, 0, :], const("a_log"), ACT.Exp))
                    if hd == 5:
                        act.wait_ge(S_["gc_done"], 1)
                        nc.scalar.activation(col["gc"][:], ps[0][:, 0:NC * HD], ACT.Copy).then_inc(S_["gc_out"], 1)
                        nc.scalar.activation(col["egc"][:], ps[0][:, 0:NC * HD], ACT.Exp).then_inc(S_["gc_out"], 1)
                        nc.scalar.activation(col["elast"][:], ps[0][:, 64:64 + NC * HD], ACT.Exp).then_inc(S_["gc_out"], 1)
                        nc.scalar.activation(col["last"][:], ps[0][:, 64:64 + NC * HD], ACT.Copy).then_inc(S_["gc_out"], 1)
                    if hd == 4:
                        split_hi(act, U + 2, 0)
                    if hd == 7:
                        split_hi(act, U + 3, 0)
                for j in range(4):
                    act.wait_ge(kv_done, j + 1)
                    nc.scalar.activation(k_all[0:64, 2 * j, :], ps[4 + j % 2][0:64, :], ACT.Copy).then_inc(kv_out_a, 1)
                act.wait_ge(S_["last_diff"], 1)
                nc.scalar.activation(col["kd"][:], col["kd"][:], ACT.Exp)
                for tt in range(0, NQT, 2):
                    act.wait_ge(kv_done, 4 + tt + 1)
                    nc.scalar.activation(v_all[:, tt, :], ps[4 + tt % 2][:], ACT.Copy).then_inc(kv_out_a, 1)

            @block.vector
            def _(dve):
                dve.wait_ge(S_["ba_turned"], 1)
                nc.vector.tensor_copy(ba[:].rearrange("p c h -> p (c h)"), ps[6][:, 0:8 * NC]).then_inc(S_["ba_out"], 1)
                nc.vector.tensor_tensor(rot_a[64:96, 1, :], misc[64:96, :], rope[64:96, :], ALU.mult).then_inc(kr_mul, 1)
                nc.vector.tensor_tensor(rot_b[64:96, 1, :], misc[96:128, :], rope[96:128, :], ALU.mult).then_inc(kr_mul, 1)
                dve.wait_ge(S_["ba_out"], 1)
                dtb = const("dt_bias")[:, None, :].to_broadcast([P, NC, HD])
                nc.vector.tensor_tensor(col["soft"][:], ba[:, :, 4:8], dtb, ALU.add).then_inc(S_["dve_col"], 1)
                for n, (a, b, rank) in enumerate(PARTS):
                    dve.wait_ge(lat_rstd, n + 1)
                    for t in range(a, b):
                        nc.vector.tensor_tensor(sq[:, t, :], lat[:, t, :], rstd[:, n, :], ALU.mult).then_inc(lat_scaled, 1)
                for t in range(5):
                    dve.wait_ge(lat_hi_ready, t + 1)
                    nc.vector.scalar_tensor_tensor(out=lat_lo[:, t, :], in0=sq[:, t, :], scalar=g_lat[:, t:t + 1],
                                                   in1=lat_hi[:, t, :].bitcast(F32), op0=ALU.mult,
                                                   op1=ALU.subtract).then_inc(lat_ready, 1)
                for hd in range(MLA_HEADS):
                    wait_head(dve, hd)
                    if hd:
                        dve.wait_ge(rope_out, hd)
                    b = ps[2 + hd % 2]
                    nc.vector.tensor_tensor(rot_a[64:96, 0, :], b[64:96, :], rope[64:96, :], ALU.mult).then_inc(rot_done, 1)
                    nc.vector.tensor_tensor(rot_b[64:96, 0, :], b[96:128, :], rope[96:128, :], ALU.mult).then_inc(rot_done, 1)
                    dve.wait_ge(rot_done, 2 * hd + 2)
                    nc.vector.tensor_tensor(q_all[64:96, hd, :], rot_a[64:96, 0, :], rot_b[64:96, 0, :],
                                            ALU.add).then_inc(rope_out, 1)
                    dve.wait_ge(S_["rs"], hd + 1)
                    nc.vector.scalar_tensor_tensor(out=qkv[:, hd, :], in0=qkv[:, hd, :],
                                                   scalar=float(GDN_D ** -0.5) if hd < 4 else 1.0,
                                                   in1=norm[:, hd % 2, :], op0=ALU.mult, op1=ALU.mult
                                                   ).then_inc(S_["normed"], 1)
                    if hd == 2:
                        step = chained(dve, S_["dve_step"])
                        dve.wait_ge(S_["beta_exp"], 1)
                        step(nc.vector.tensor_scalar(col["beta"][:], col["beta"][:], 1.0, None, ALU.add))
                        step(nc.vector.reciprocal(col["beta"][:], col["beta"][:]))
                        step(nc.vector.tensor_scalar(col["nbeta"][:], col["beta"][:], -1.0, None, ALU.mult))
                        dve.wait_ge(S_["act_col"], 4)
                        step(nc.vector.scalar_tensor_tensor(out=col["soft"][:], in0=col["soft"][:], scalar=0.0,
                                                            in1=col["tmp"][:], op0=ALU.max, op1=ALU.add))
                        eab = col["ea"][:, 0:1, :].to_broadcast([P, NC, HD])
                        nc.vector.scalar_tensor_tensor(out=col["g"][:], in0=col["soft"][:], scalar=-1.0, in1=eab,
                                                       op0=ALU.mult, op1=ALU.mult).then_inc(S_["g_ready"], 1)
                    if hd == 6:
                        dve.wait_ge(S_["gc_out"], 4)
                        nc.vector.tensor_tensor(col["kd"][:], col["last"][:], col["gc"][:], ALU.subtract).then_inc(S_["last_diff"], 1)
                        nc.vector.tensor_tensor(col["bg"][:], col["beta"][:], col["egc"][:], ALU.mult)
                for j in range(4):
                    dve.wait_ge(kv_done, j + 1)
                    nc.vector.tensor_copy(k_all[0:64, 2 * j + 1, :], ps[4 + j % 2][64:128, :]).then_inc(kv_out_v, 1)
                for tt in range(1, NQT, 2):
                    if tt == 3:
                        dve.wait_ge(tiles_done, 2 * (U + 3))
                    else:
                        dve.wait_ge(kv_done, 4 + tt + 1)
                    nc.vector.tensor_copy(v_all[:, tt, :], ps[4 + tt % 2][:]).then_inc(kv_out_v, 1)

            @block.tensor
            def _(pe):
                def g_sum(t):
                    pe.wait_ge(S_["sq"], t + 1)
                    if t >= 2:
                        pe.wait_ge(S_["ln"], t - 1)
                    nc.tensor.matmul(ps[6 + t % 2][:], ones, gsq[:, t % 4, :], start=True, stop=True).then_inc(S_["ms"], 1)
                for c in range(NC):
                    tr = nc.tensor.transpose(ps[6][:, 8 * c:8 * c + 8], misc[0:8, c * P:(c + 1) * P], ident[0:8, 0:8])
                tr.then_inc(S_["ba_turned"], 1)
                keep_busy(ps[7], 4)
                for n, (a, b, rank) in enumerate(PARTS):
                    for t in range(a, b):
                        pe.wait_ge(lat_sq, t + 1)
                        mm = nc.tensor.matmul(ps[n][:], ones, sq[:, t, :], start=(t == a), stop=(t == b - 1))
                    mm.then_inc(lat_ms, 1)
                pe.wait_ge(S_["ba_out"], 1)
                g_sum(0)
                g_sum(1)
                keep_busy(ps[5], 8)
                pe.wait_ge(lat_ready, 5)
                for hd in range(MLA_HEADS):
                    s = (U + (hd > 4)) % 2
                    pe.wait_ge(lo_ready, U + (hd > 4) + 1)
                    if hd >= 2:
                        pe.wait_ge(nope_out, hd - 1)
                        pe.wait_ge(rope_out, hd - 1)
                    for k in range(3):
                        c = (3 * (hd - 5 * (hd > 4)) + k) * P
                        mm = three_passes(ps[2 + hd % 2][:], whi[:, s, c:c + P], wlo[:, s, c:c + P],
                                          lat_hi[:, k, :], lat_lo[:, k, :], k == 0, k == 2)
                    if hd in (4, 7):
                        mm.then_inc(tiles_done, 2)
                    else:
                        mm.then_inc(head_done, 1)
                    if 1 <= hd < 7:
                        g_sum(hd + 1)
                    if hd == 3:
                        pe.wait_ge(S_["g_ready"], 1)
                        nc.tensor.matmul(ps[0][:, 0:NC * HD], utri, col["g"][:].rearrange("p c h -> p (c h)"), start=True, stop=True)
                        nc.tensor.matmul(ps[0][:, 64:64 + NC * HD], ones, col["g"][:].rearrange("p c h -> p (c h)"),
                                         start=True, stop=True).then_inc(S_["gc_done"], 1)
                s = (U + 2) % 2
                pe.wait_ge(lo_ready, U + 3)
                for j in range(4):
                    if j >= 2:
                        pe.wait_ge(kv_out_a, j - 1)
                        pe.wait_ge(kv_out_v, j - 1)
                    for k in range(2):
                        c = (2 * j + k) * P
                        mm = three_passes(ps[4 + j % 2][:], whi[:, s, c:c + P], wlo[:, s, c:c + P],
                                          lat_hi[:, 3 + k, :], lat_lo[:, 3 + k, :], k == 0, k == 1)
                    mm.then_inc(kv_done, 1)
                for tt in range(NQT):
                    if tt < 2:
                        pe.wait_ge(kv_out_a, 3 + tt)
                        pe.wait_ge(kv_out_v, 3 + tt)
                    elif tt == 2:
                        pe.wait_ge(kv_out_a, 5)
                    else:
                        pe.wait_ge(kv_out_v, 5)
                    tok = slice(tt * P, (tt + 1) * P)
                    for k in range(2):
                        c = (8 + 4 * k) * P
                        mm = three_passes(ps[4 + tt % 2][:], lat_hi[:, 3 + k, tok], lat_lo[:, 3 + k, tok],
                                          whi[:, s, c:c + 512], wlo[:, s, c:c + 512], k == 0, k == 1)
                    if tt == 3:
                        mm.then_inc(tiles_done, 2)
                    else:
                        mm.then_inc(kv_done, 1)
    even_in.close()

    mix_hi = sb(even, "mix_hi", [P, KT, SEQ], F32R)
    mix_lo = sb(even, "mix_lo", [P, KT, SEQ], F32R)
    with ExitStack() as ph:
        prob, prob_t = sb(ph, "prob_m", [P, NQT, SEQ]), sb(ph, "prob_t_m", [P, 2, SEQ])
        neg_max, row_sum = sb(ph, "neg_max_m", [P, NQT]), sb(ph, "row_sum_m", [P, MLA_HEADS, NQT])
        inv = sb(ph, "inv_m", [P, NQT])
        o_nat = sb(ph, "o_nat", [P, NQT, MLA_HEADS * MLA_V])
        ps = banks(ph, "mla")
        causal = const("causal")
        inv_ready, o_scaled, mix_turned, mix_hi_out, mix_lo_out = (
            sem("m_inv"), sem("m_scaled"), sem("m_turned"), sem("m_hi_out"), sem("m_lo_out"))

        def take(dve, g, br, bank):
            a = 2 * g + br
            if a:
                dve.wait_ge(sem_of["o_taken_mla"], a)
            nc.vector.reciprocal(inv[:], row_sum[:, a, :]).then_inc(inv_ready, 1)
            dve.wait_ge(inv_ready, a + 1)
            return nc.vector.tensor_tensor(o_nat[:, :, bass.ts(a, MLA_V)],
                                           bank[:].rearrange("p (t d) -> p t d", t=NQT)[:, :, br * MLA_V:(br + 1) * MLA_V],
                                           inv[:, :, None].to_broadcast([P, NQT, MLA_V]), ALU.mult)

        with nc.Block() as block:
            on_act, on_dve, on_pe = attention(
                "mla", MLA_HEADS // 2, 2, float((NOPE + ROPE) ** -0.5), ps[0:4], ps[4:6], ps[6:8], prob, prob_t,
                neg_max, lambda g, br: row_sum[:, 2 * g + br, :],
                products=lambda pe, a, qt, w: [(q_all[:, a, qt * P:(qt + 1) * P], k_all[:, a, 0:w])],
                values=lambda a, kt: v_all[:, kt, a // 2 * P:(a // 2 + 1) * P],
                bias=lambda g, qt: causal[:, (NQT - 1 - qt) * P:SEQ], take=take)

            @block.scalar
            def _(act):
                on_act(act)
                for f in range(4):
                    act.wait_ge(mix_turned, f + 1)
                    nc.scalar.activation(mix_hi[:, f, :], ps[f][:], ACT.Copy).then_inc(mix_hi_out, 1)

            @block.vector
            def _(dve):
                on_dve(dve)
                for f in range(4):
                    dve.wait_ge(mix_hi_out, f + 1)
                    nc.vector.tensor_tensor(mix_lo[:, f, :], ps[f][:], mix_hi[:, f, :].bitcast(F32),
                                            ALU.subtract).then_inc(mix_lo_out, 1)

            @block.tensor
            def _(pe):
                on_pe(pe)
                pe.wait_ge(sem_of["o_taken_mla"], MLA_HEADS)
                for f in range(4):
                    for qt in range(NQT):
                        tr = nc.tensor.transpose(ps[f][:, qt * P:(qt + 1) * P], o_nat[:, qt, f * P:(f + 1) * P], ident)
                    tr.then_inc(mix_turned, 1)
    mla.close()

    with ExitStack() as ph:
        def tile(name, *shape):
            return sb(ph, name, [P, *shape])
        norm = tile("g_norm", 2, 512)
        kbg, kdec, vb = (tile("g_" + n, NC, HD * C) for n in ("kbg", "kdec", "vb"))
        nat, intra = tile("g_nat", NC, HD * C), tile("g_intra", NC, HD * C)
        t_, tt_ = tile("g_t", NC, HD * C), tile("g_tt", NC, HD * C)
        dec = tile("g_dec", 2, HD * C)
        xb = tile("g_x", 2, HD * C)
        off = tile("g_off", 2, HD * C)
        decayed = tile("g_state_decayed", HD * C)
        ps = banks(ph, "gdn")
        vrows = const("level")

        def heads(ap):
            return ap.rearrange("p (h c) -> p h c", h=HD)

        def over(c4):
            return c4[:, :, None].to_broadcast([P, HD, C])

        def per_head(mat):
            return mat[:, None, :].to_broadcast([P, HD, C])

        E_SEMS = {n: sem("gdn_" + n) for n in (
            "rows_done", "diff", "dec", "dec_masked", "pairs_done", "nat_out", "intra_out", "qd_row", "qd_out",
            "k_turned", "k_out", "v_turned", "v_out", "off_ready", "x_done", "x_out", "u_done", "t_out", "tt_out",
            "w_done", "w_out", "vn_done", "vn_out", "o_done", "o_out", "s_done", "s_out", "o_sq", "o_ms", "o_ln", "o_rs",
            "y1", "y2", "y_hi", "y_lo", "id_out")}
        S_ = E_SEMS
        gc_row, beta_row = (ps[0], ps[6]), (ps[1], ps[7])
        with nc.Block() as block:
            def k_tile(hd, c):
                return qkv[:, 4 + hd, c * C:(c + 1) * C]

            def q_tile(hd, c):
                return qkv[:, hd, c * C:(c + 1) * C]

            def q_chunk(c):
                return qkv[:, 0:4, c * C:(c + 1) * C]

            @block.tensor
            def _(pe):
                def rows(c):
                    if c >= 2:
                        pe.wait_ge(S_["diff"], c - 1)
                        pe.wait_ge(S_["qd_row"], c - 1)
                        pe.wait_ge(S_["dec_masked"], c - 1)
                    for hd in range(HD):
                        nc.tensor.matmul(gc_row[c % 2][:, hd * C:(hd + 1) * C], col["g"][:, c, hd:hd + 1].to_broadcast([P, C]),
                                         utri, start=True, stop=True)
                        mm = nc.tensor.matmul(beta_row[c % 2][:, hd * C:(hd + 1) * C], col["nbeta"][:, c, hd:hd + 1].to_broadcast([P, C]),
                                              ident, start=True, stop=True)
                    mm.then_inc(S_["rows_done"], 1)

                rows(0)
                for c in range(NC):
                    if c:
                        pe.wait_ge(S_["k_out"], 2 * c)
                    for hd in range(HD):
                        tr = nc.tensor.transpose(ps[4][:, hd * C:(hd + 1) * C], k_tile(hd, c), ident)
                    tr.then_inc(S_["k_turned"], 1)
                    if c:
                        pe.wait_ge(S_["v_out"], HD * c)
                    for hd in range(HD):
                        tr = nc.tensor.transpose(ps[5][:, hd * C:(hd + 1) * C], qkv[:, 8 + hd, c * C:(c + 1) * C], ident)
                    tr.then_inc(S_["v_turned"], 1)
                    if c < NC - 1:
                        rows(c + 1)
                    if c:
                        pe.wait_ge(S_["nat_out"], c)
                        pe.wait_ge(S_["intra_out"], c)
                    for hd in range(HD):
                        nc.tensor.matmul(ps[2][:, hd * C:(hd + 1) * C], k_tile(hd, c), k_tile(hd, c), start=True, stop=True)
                        mm = nc.tensor.matmul(ps[3][:, hd * C:(hd + 1) * C], k_tile(hd, c), q_tile(hd, c), start=True, stop=True)
                    mm.then_inc(S_["pairs_done"], 1)

            @block.gpsimd
            def _(pool):
                for c in range(NC):
                    pool.wait_ge(S_["pairs_done"], c + 1)
                    pool.wait_ge(S_["qd_row"], c + 1)
                    nc.gpsimd.tensor_tensor(q_chunk(c), q_chunk(c), heads(norm[:, c % 2, :]), ALU.mult).then_inc(S_["qd_out"], 1)

            @block.vector
            def _(dve):
                for c in range(NC):
                    dve.wait_ge(S_["rows_done"], c + 1)
                    if c:
                        dve.wait_ge(S_["nat_out"], c)
                        dve.wait_ge(S_["intra_out"], c)
                    nc.vector.tensor_tensor(heads(dec[:, 0, :]), heads(gc_row[c % 2][:]), over(col["gc"][:, c, :]),
                                            ALU.subtract).then_inc(S_["diff"], 1)
                    dve.wait_ge(S_["diff"], 1 + c)
                    nc.vector.tensor_scalar(dec[:, 0, :], dec[:, 0, :], 0.0, None, ALU.min).then_inc(S_["y1"], 1)
                    dve.wait_ge(S_["k_turned"], c + 1)
                    nc.vector.tensor_tensor(heads(kbg[:, c, :]), heads(ps[4][:]), over(col["bg"][:, c, :]), ALU.mult).then_inc(S_["k_out"], 1)
                    nc.vector.tensor_tensor(heads(kdec[:, c, :]), heads(ps[4][:]), over(col["kd"][:, c, :]), ALU.mult).then_inc(S_["k_out"], 1)
                    dve.wait_ge(S_["dec"], 1 + c)
                    nc.vector.tensor_tensor(heads(dec[:, 1, :]), heads(dec[:, 0, :]), per_head(utri), ALU.mult).then_inc(S_["y2"], 1)
                    dve.wait_ge(S_["y2"], c + 1)
                    nc.vector.tensor_tensor(dec[:, 0, :], dec[:, 1, :], beta_row[c % 2][:], ALU.mult).then_inc(S_["dec_masked"], 1)
                    dve.wait_ge(S_["dec_masked"], c + 1)
                    dve.wait_ge(S_["pairs_done"], c + 1)
                    nc.vector.tensor_tensor(nat[:, c, :], ps[2][:], dec[:, 0, :], ALU.mult).then_inc(S_["nat_out"], 1)
                    nc.vector.tensor_tensor(intra[:, c, :], ps[3][:], dec[:, 1, :], ALU.mult).then_inc(S_["intra_out"], 1)

            @block.scalar
            def _(act):
                for c in range(NC):
                    act.wait_ge(S_["diff"], 1 + c)
                    if c >= 2:
                        act.wait_ge(S_["qd_out"], c - 1)
                    nc.scalar.activation(norm[:, c % 2, :], gc_row[c % 2][:], ACT.Exp).then_inc(S_["qd_row"], 1)
                    act.wait_ge(S_["v_turned"], c + 1)
                    for hd in range(HD):
                        r = slice(hd * C, (hd + 1) * C)
                        nc.scalar.activation(vb[:, c, r], ps[5][:, r], ACT.Copy,
                                             scale=col["beta"][:, c, hd:hd + 1]).then_inc(S_["v_out"], 1)
                    act.wait_ge(S_["y1"], c + 1)
                    nc.scalar.activation(dec[:, 0, :], dec[:, 0, :], ACT.Exp).then_inc(S_["dec"], 1)

        LEVELS = 7
        with nc.Block() as block:
            def level(l):
                return vrows[:, l * P:(l + 1) * P]

            @block.gpsimd
            def _(pool):
                for l in range(LEVELS):
                    for c in range(NC):
                        n = l * NC + c
                        if n >= 2:
                            pool.wait_ge(S_["x_done"], n - 1)
                            if n < NC + 2:
                                pool.wait_ge(S_["tt_out"], n - 1)
                        nc.gpsimd.tensor_tensor(heads(off[:, n % 2, :]), heads(nat[:, c, :]), per_head(level(l)),
                                                ALU.mult).then_inc(S_["off_ready"], 1)

            @block.tensor
            def _(pe):
                def x_step(n):
                    l, c = divmod(n, NC)
                    pe.wait_ge(S_["off_ready"], n + 1)
                    if n >= 2:
                        pe.wait_ge(S_["x_out"], n - 1)
                    if l:
                        pe.wait_ge(S_["t_out"], n - NC + 1)
                    for hd in range(HD):
                        r = slice(hd * C, (hd + 1) * C)
                        mm = nc.tensor.matmul(ps[n % 2][:, r], off[:, n % 2, r], t_[:, c, r] if l else ident,
                                              start=True, stop=True)
                    mm.then_inc(S_["x_done"], 1)

                def t_step(n):
                    l, c = divmod(n, NC)
                    pe.wait_ge(S_["x_out"], n + 1)
                    pe.wait_ge(S_["tt_out"], n - NC + 1)
                    if l < LEVELS - 1:
                        if n >= NC + 2:
                            pe.wait_ge(S_["t_out"], n - 1)
                        for hd in range(HD):
                            r = slice(hd * C, (hd + 1) * C)
                            nc.tensor.matmul(ps[2 + n % 2][:, r], tt_[:, c, r], xb[:, n % 2, r], start=True, stop=True)
                    if n >= NC + 2:
                        pe.wait_ge(S_["tt_out"], n - 1)
                    for hd in range(HD):
                        r = slice(hd * C, (hd + 1) * C)
                        mm = nc.tensor.matmul(ps[4 + n % 2][:, r], xb[:, n % 2, r], tt_[:, c, r], start=True, stop=True)
                    mm.then_inc(S_["u_done"], 1)

                for n in range(LEVELS * NC):
                    x_step(n)
                    if n > NC:
                        t_step(n - 1)
                t_step(LEVELS * NC - 1)

            @block.scalar
            def _(act):
                for n in range(LEVELS * NC):
                    act.wait_ge(S_["x_done"], n + 1)
                    if n >= NC + 2:
                        act.wait_ge(S_["u_done"], n - NC - 1)
                    elif n >= 2:
                        act.wait_ge(S_["t_out"], n - 1)
                    nc.scalar.activation(xb[:, n % 2, :], ps[n % 2][:], ACT.Copy).then_inc(S_["x_out"], 1)

            @block.vector
            def _(dve):
                for l in range(LEVELS):
                    for c in range(NC):
                        n = l * NC + c
                        if l == 0:
                            dve.wait_ge(S_["x_out"], n + 1)
                            nc.vector.tensor_tensor(heads(t_[:, c, :]), heads(xb[:, n % 2, :]), per_head(ident), ALU.add).then_inc(S_["t_out"], 1)
                            nc.vector.tensor_tensor(heads(tt_[:, c, :]), heads(off[:, n % 2, :]), per_head(ident), ALU.add).then_inc(S_["tt_out"], 1)
                        else:
                            dve.wait_ge(S_["u_done"], n - NC + 1)
                            if l < LEVELS - 1:
                                nc.vector.tensor_tensor(t_[:, c, :], t_[:, c, :], ps[2 + n % 2][:], ALU.add).then_inc(S_["t_out"], 1)
                            nc.vector.tensor_tensor(tt_[:, c, :], tt_[:, c, :], ps[4 + n % 2][:], ALU.add).then_inc(S_["tt_out"], 1)

        nw = t_
        o_t = nat
        state, vn = off, dec
        o_bank, decayed_ready = (ps[5], ps[6]), S_["v_turned"]
        with nc.Block() as block:
            def chunk(tiles, c, first=0):
                return tiles[:, first:first + HD, c * C:(c + 1) * C]

            @block.tensor
            def _(pe):
                def own(c):
                    if c >= 2:
                        pe.wait_ge(S_["vn_out"], c - 1)
                    for hd in range(HD):
                        r = slice(hd * C, (hd + 1) * C)
                        mm = nc.tensor.matmul(ps[2 + c % 2][:, r], tt_[:, c, r], vb[:, c, r], start=hd == 0 or c == 0, stop=c == 0)
                    return mm

                def mean_square(c):
                    pe.wait_ge(S_["o_sq"], c + 1)
                    if c:
                        pe.wait_ge(S_["o_ln"], c)
                    nc.tensor.matmul(ps[7][:], ones, xb[:, c % 2, :], start=True, stop=True).then_inc(S_["o_ms"], 1)

                own(0).then_inc(S_["vn_done"], 1)
                for c in range(1, NC):
                    if c >= 3:
                        pe.wait_ge(S_["w_out"], c - 2)
                    for hd in range(HD):
                        r = slice(hd * C, (hd + 1) * C)
                        mm = nc.tensor.matmul(ps[c % 2][:, r], kbg[:, c, r], tt_[:, c, r], start=True, stop=True)
                    mm.then_inc(S_["w_done"], 1)
                    if c == 1:
                        own(1)
                for c in range(NC):
                    if c:
                        pe.wait_ge(S_["w_out"], c)
                        pe.wait_ge(S_["s_out"], c)
                        for hd in range(HD):
                            r = slice(hd * C, (hd + 1) * C)
                            mm = nc.tensor.matmul(ps[2 + c % 2][:, r], nw[:, c, r], state[:, c % 2, r], start=False, stop=hd == HD - 1)
                        mm.then_inc(S_["vn_done"], 1)
                        if c >= 2:
                            pe.wait_ge(S_["o_out"], c - 1)
                        for hd in range(HD):
                            nc.tensor.matmul(o_bank[c % 2][:, hd * C:(hd + 1) * C], state[:, c % 2, hd * C:(hd + 1) * C],
                                             q_tile(hd, c), start=hd == 0, stop=False)
                    pe.wait_ge(S_["vn_out"], c + 1)
                    for hd in range(HD):
                        r = slice(hd * C, (hd + 1) * C)
                        if c < NC - 1:
                            mm = nc.tensor.matmul(ps[4][:, r], kdec[:, c, r], vn[:, c % 2, r], start=True, stop=True)
                    if c < NC - 1:
                        mm.then_inc(S_["s_done"], 1)
                    for hd in range(HD):
                        r = slice(hd * C, (hd + 1) * C)
                        mm = nc.tensor.matmul(o_bank[c % 2][:, r], vn[:, c % 2, r], intra[:, c, r], start=c == 0, stop=c == 0 or hd == HD - 1)
                    mm.then_inc(S_["o_done"], 1)
                    if c + 2 < NC:
                        own(c + 2)
                    if c:
                        mean_square(c - 1)
                mean_square(NC - 1)

            @block.scalar
            def _(act):
                def v_new(c):
                    act.wait_ge(S_["vn_done"], c + 1)
                    if c >= 2:
                        act.wait_ge(S_["o_done"], c - 1)
                    nc.scalar.activation(vn[:, c % 2, :], ps[2 + c % 2][:], ACT.Copy).then_inc(S_["vn_out"], 1)

                def square(c):
                    act.wait_ge(S_["o_out"], c + 1)
                    if c >= 2:
                        act.wait_ge(S_["o_ms"], c - 1)
                    nc.scalar.activation(heads(xb[:, c % 2, :]), chunk(o_t, c), ACT.Square).then_inc(S_["o_sq"], 1)

                def rsqrt(c):
                    act.wait_ge(S_["o_ms"], c + 1)
                    if c >= 2:
                        act.wait_ge(S_["y_lo"], c - 1)
                    nc.scalar.activation(norm[:, c % 2, :], ps[7][:], ACT.Ln, bias=eps, scale=1.0 / GDN_D).then_inc(S_["o_ln"], 1)
                    act.wait_ge(S_["o_ln"], c + 1)
                    nc.scalar.activation(norm[:, c % 2, :], norm[:, c % 2, :], ACT.Exp, scale=-0.5).then_inc(S_["o_rs"], 1)

                def hi(c):
                    act.wait_ge(S_["id_out"], c + 1)
                    nc.scalar.activation(chunk(mix_hi, c, 4), chunk(o_t, c), ACT.Copy).then_inc(S_["y_hi"], 1)

                act.preload_act_table_set("natural_log_exp_and_others")
                v_new(0)
                for c in range(1, NC):
                    act.wait_ge(S_["w_done"], c)
                    nc.scalar.activation(nw[:, c, :], ps[c % 2][:], ACT.Copy, scale=-1.0).then_inc(S_["w_out"], 1)
                for c in range(1, NC):
                    v_new(c)
                    square(c - 1)
                    if c >= 2:
                        rsqrt(c - 2)
                        if c >= 3:
                            hi(c - 3)
                rsqrt(NC - 2)
                square(NC - 1)
                hi(NC - 3)
                rsqrt(NC - 1)
                hi(NC - 2)
                hi(NC - 1)

            @block.vector
            def _(dve):
                def next_state(c):
                    dve.wait_ge(S_["s_done"], c + 1)
                    new = state[:, (c + 1) % 2, :]
                    if c == 0:
                        nc.vector.tensor_copy(new, ps[4][:]).then_inc(S_["s_out"], 1)
                    else:
                        dve.wait_ge(S_["o_done"], c)
                        dve.wait_ge(decayed_ready, NC + c)
                        nc.vector.tensor_tensor(new, decayed[:], ps[4][:], ALU.add).then_inc(S_["s_out"], 1)
                    if c + 1 < NC - 1:
                        dve.wait_ge(S_["s_out"], c + 1)
                        nc.vector.tensor_tensor(heads(decayed[:]), heads(new), over(col["elast"][:, c + 1, :]),
                                                ALU.mult).then_inc(decayed_ready, 1)

                def output(c):
                    dve.wait_ge(S_["o_done"], c + 1)
                    nc.vector.tensor_copy(chunk(o_t, c), heads(o_bank[c % 2][:])).then_inc(S_["o_out"], 1)

                def scaled(c):
                    dve.wait_ge(S_["o_rs"], c + 1)
                    nc.vector.scalar_tensor_tensor(out=chunk(o_t, c), in0=chunk(o_t, c), scalar=const("g_gdn"),
                                                   in1=heads(norm[:, c % 2, :]), op0=ALU.mult, op1=ALU.mult).then_inc(S_["y_lo"], 1)
                    dve.wait_ge(S_["y_lo"], c + 1)
                    nc.vector.tensor_tensor(chunk(o_t, c), chunk(o_t, c), chunk(zg, c), ALU.mult).then_inc(S_["id_out"], 1)

                def lo(c):
                    dve.wait_ge(S_["y_hi"], c + 1)
                    nc.vector.tensor_tensor(chunk(mix_lo, c, 4), chunk(o_t, c), chunk(mix_hi, c, 4).bitcast(F32), ALU.subtract)

                next_state(0)
                output(0)
                next_state(1)
                output(1)
                next_state(2)
                scaled(0)
                output(2)
                output(3)
                scaled(1)
                lo(0)
                scaled(2)
                lo(1)
                scaled(3)
                lo(2)
                lo(3)

    def project_residual(name, x_hi, x_lo, source=None):
        U = UNITS[name][0]
        with ExitStack() as ph:
            sq2 = sb(ph, f"sq2_{name}", [P, 2, SEQ])
            A = KT * (sums[0] - 1)
            clear, square, add_square, total, rsqrt_mean = square_sum(sq2)
            ps = banks(ph, name)
            if source is not None:
                turned, hi_out, lo_out = sem("od_turned"), sem("od_hi_out"), sem("od_lo_out")
            with nc.Block() as block:
                @block.sync
                def _(sp):
                    load_units(sp, name)

                @block.gpsimd
                def _(pool):
                    split_los(pool, name)

                @block.scalar
                def _(act):
                    act.preload_act_table_set("natural_log_exp_and_others")
                    if source is not None:
                        for f in range(KT):
                            if f == 3:
                                split_hi(act, U + 1, 0)
                            act.wait_ge(turned, f + 1)
                            nc.scalar.activation(x_hi[:, f, :], ps[4 + f % 2][:], ACT.Copy).then_inc(hi_out, 1)
                    else:
                        split_hi(act, U + 1, 0)
                    for u in range(4):
                        if u < 3:
                            split_hi(act, U + 2 + u, 0)
                        for t in (2 * u, 2 * u + 1):
                            act.wait_ge(added, A + t + 1)
                            square(act, t)
                    rsqrt_mean(act, ps[7])

                @block.vector
                def _(dve):
                    clear(dve)
                    for f in range(KT if source is not None else 0):
                        dve.wait_ge(hi_out, f + 1)
                        nc.vector.tensor_tensor(x_lo[:, f, :], ps[4 + f % 2][:], x_hi[:, f, :].bitcast(F32),
                                                ALU.subtract).then_inc(lo_out, 1)
                    for t in range(KT):
                        dve.wait_ge(tiles_done, 2 * U + t + 1)
                        nc.vector.tensor_tensor(h[:, t, :], h[:, t, :], ps[t % 4][:], ALU.add).then_inc(added, 1)
                        if t:
                            add_square(dve, t - 1)
                    add_square(dve, KT - 1)

                @block.tensor
                def _(pe):
                    def turn(f):
                        if f >= 2:
                            pe.wait_ge(lo_out, f - 1)
                        for qt in range(NQT):
                            tr = nc.tensor.transpose(ps[4 + f % 2][:, qt * P:(qt + 1) * P], source[:, qt, f * P:(f + 1) * P], ident)
                        tr.then_inc(turned, 1)

                    def input_tile(pe, k):
                        if k + 2 < KT:
                            turn(k + 2)
                        pe.wait_ge(lo_out, k + 1)

                    if source is not None:
                        turn(0)
                        turn(1)
                        first_unit(pe, U, ps[0:2], x_hi, x_lo, input_tile)
                    for u in range(0 if source is None else 1, 4):
                        pe.wait_ge(lo_ready, U + u + 1)
                        for m in range(2):
                            if u >= 2:
                                pe.wait_ge(added, A + 2 * u - 3 + m)
                            column_tile(ps[2 * (u % 2) + m][:], (U + u) % 2, m, x_hi, x_lo).then_inc(tiles_done, 1)
                    keep_busy(ps[6], 5)
                    total(pe, ps[7])

    project_residual("ev_out", mix_hi, mix_lo)
    even.close()

    def ffn(n):
        gu, down = f"gu{n}", f"down{n}"
        with ExitStack() as ph:
            hid_hi, hid_lo = sb(ph, f"hid_hi{n}", [P, FT, SEQ], F32R), sb(ph, f"hid_lo{n}", [P, FT, SEQ], F32R)
            ps = banks(ph, f"ffn{n}")
            with ExitStack() as up:
                xh, xl = sb(up, f"xh_f{n}", [P, KT, SEQ], F32R), sb(up, f"xl_f{n}", [P, KT, SEQ], F32R)
                xn = sb(up, f"xn_f{n}", [P, KT, SEQ])
                n_act, n_dve, wait_tile, _ = norm_parts(xn, const(f"g_ffn{n}"), xh, xl)
                silu, prod = xn[:, 0:2, :], xn[:, 2:4, :]
                silu_done, prod_done, hi_done, lo_done = (sem(f"silu{n}"), sem(f"prod{n}"), sem(f"hid_hi_out{n}"),
                                                          sem(f"hid_lo_out{n}"))
                U = UNITS[gu][0]
                with nc.Block() as block:
                    @block.sync
                    def _(sp):
                        load_units(sp, gu)

                    @block.gpsimd
                    def _(pool):
                        split_los(pool, gu)

                    @block.scalar
                    def _(act):
                        n_act(act, U + 1)
                        act.preload_act_table(ACT.Silu)
                        wait_tile(act, KT - 1)

                        def turn(i, last):
                            for m in range(2):
                                act.wait_ge(tiles_done, 2 * U + m + 1 + 4 * i)
                                nc.scalar.activation(silu[:, m, :], ps[m][:], ACT.Silu).then_inc(silu_done, 1)
                            split_hi(act, U + 2, i)
                            for m in range(2):
                                act.wait_ge(prod_done, m + 1 + 2 * i)
                                nc.scalar.activation(hid_hi[:, 2 * i + m, :], prod[:, m, :], ACT.Copy).then_inc(hi_done, 1)
                            if not last:
                                split_hi(act, U + 3, i)
                        with act.Fori(0, FT // 2 - 1) as i:
                            turn(i, False)
                        turn(FT // 2 - 1, True)

                    @block.vector
                    def _(dve):
                        n_dve(dve)
                        with dve.Fori(0, FT // 2) as i:
                            dve.wait_ge(lo_done, 2 * i)
                            for m in range(2):
                                dve.wait_ge(tiles_done, 2 * U + m + 3 + 4 * i)
                                dve.wait_ge(silu_done, m + 1 + 2 * i)
                                nc.vector.tensor_tensor(prod[:, m, :], silu[:, m, :], ps[2 + m][:],
                                                        ALU.mult).then_inc(prod_done, 1)
                            for m in range(2):
                                dve.wait_ge(hi_done, m + 1 + 2 * i)
                                nc.vector.tensor_tensor(hid_lo[:, 2 * i + m, :], prod[:, m, :],
                                                        hid_hi[:, 2 * i + m, :].bitcast(F32),
                                                        ALU.subtract).then_inc(lo_done, 1)

                    @block.tensor
                    def _(pe):
                        keep_busy(ps[5], 4)

                        def unit(j, i):
                            pe.wait_ge(lo_ready, U + j + 1 + 2 * i)
                            if not isinstance(i, int):
                                pe.wait_ge(prod_done if j else silu_done, 2 * i)
                            for m in range(2):
                                column_tile(ps[2 * j + m][:], (U + j) % 2, m, xh, xl).then_inc(tiles_done, 1)
                        first_unit(pe, U, ps[0:2], xh, xl, wait_tile)
                        unit(1, 0)
                        with pe.Fori(1, FT // 2) as i:
                            unit(0, i)
                            unit(1, i)
            U = UNITS[down][0]
            sq2 = sb(ph, f"sq2_{down}", [P, 2, SEQ])
            A = KT * (sums[0] - 1)
            clear, square, add_square, total, rsqrt_mean = square_sum(sq2)
            with nc.Block() as block:
                @block.sync
                def _(sp):
                    load_units(sp, down)

                @block.gpsimd
                def _(pool):
                    split_los(pool, down)

                @block.scalar
                def _(act):
                    act.preload_act_table_set("natural_log_exp_and_others")
                    for j in range(12):
                        if U + j + 1 < N_UNITS:
                            split_hi(act, U + j + 1, 0)
                        for t in {3: (0, 1), 6: (2, 3), 9: (4, 5), 11: (6, 7)}.get(j, ()):
                            act.wait_ge(added, A + t + 1)
                            square(act, t)
                    rsqrt_mean(act, ps[0])

                @block.vector
                def _(dve):
                    clear(dve)
                    for t in range(KT):
                        dve.wait_ge(tiles_done, 2 * (U + 3 * (t // 2) + 2) + t % 2 + 1)
                        nc.vector.tensor_tensor(h[:, t, :], h[:, t, :], ps[4 + t % 4][:], ALU.add).then_inc(added, 1)
                        if t % 2:
                            add_square(dve, t - 1)
                            add_square(dve, t)

                @block.tensor
                def _(pe):
                    with pe.Fori(0, KT // 4) as i:
                        for j in range(6):
                            pe.wait_ge(lo_ready, U + j + 1 + 6 * i)
                            if j % 3 == 0:
                                pe.wait_ge(added, A + 4 * i)
                            r = j % 3
                            for m in range(2):
                                column_tile(ps[4 + 2 * (j // 3) + m][:], (U + j) % 2, m, hid_hi, hid_lo, k0=UK * r,
                                            nk=min(UK, FT - UK * r), first=r == 0, last=r == 2).then_inc(tiles_done, 1)
                    keep_busy(ps[1], 5)
                    total(pe, ps[0])

    ffn(0)

    odd, cmp_in = ExitStack(), ExitStack()
    G, CW = NSA_GROUPS, SEQ + CMP_STRIDE
    q_n = sb(odd, "q_n", [P, NSA_HEADS // 2, SEQ])
    k_two = [sb(odd, f"k_{n}", [P, G, SEQ]) for n in ("sel", "win")]
    v_two = [sb(odd, f"v_{n}", [P, NQT, G * NSA_DIM]) for n in ("sel", "win")]
    gates = sb(odd, "gates", [P, NQT, 3 * NSA_HEADS])
    k_cmp = sb(odd, "k_cmp", [P, G, 2, NCMP])
    v_cmp = sb(odd, "v_cmp", [P, G * NSA_DIM])
    seq_hi = [sb(cmp_in, f"seq_hi_{n}", [P, G + 1, CW], F32R) for n in "kv"]
    seq_lo = [sb(cmp_in, f"seq_lo_{n}", [P, G + 1, CW], F32R) for n in "kv"]
    with ExitStack() as ph:
        xh, xl = sb(ph, "xh_od", [P, KT, SEQ], F32R), sb(ph, "xl_od", [P, KT, SEQ], F32R)
        xn = sb(ph, "xn_od", [P, KT, SEQ])
        ps = banks(ph, "odin")
        n_act, n_dve, wait_tile, _ = norm_parts(xn, const("g_od"), xh, xl)
        out_a, out_v, padded, piece_hi = sem("odin_out_act"), sem("odin_out_dve"), sem("od_padded"), sem("od_piece_hi")
        piece_lo = sem("od_piece_lo")
        gate_done, gate_exp, gate_turned, gate_step = sem("gate_done"), sem("gate_exp"), sem("gate_turned"), sem("gate_step")
        gate_t = sb(ph, "gate_t", [48, SEQ])
        U = UNITS["od_in"][0]
        w_gate = const("w_gate")
        HALF = NSA_DIM

        def half(t):
            return slice(t * HALF, (t + 1) * HALF)

        with nc.Block() as block:
            @block.sync
            def _(sp):
                load_units(sp, "od_in")

            @block.gpsimd
            def _(pool):
                for t in seq_hi + seq_lo:
                    nc.gpsimd.memset(t[:].bitcast(F32), 0.0).then_inc(padded, 1)
                split_los(pool, "od_in")

            @block.scalar
            def _(act):
                n_act(act, U + 1)
                for u in range(4):
                    if u:
                        split_hi(act, U + u + 1, 0)
                    act.wait_ge(tiles_done, 2 * (U + u) + 1)
                    nc.scalar.activation(q_n[:, 2 * u, :], ps[2 * (u % 2)][:], ACT.Copy).then_inc(out_a, 1)
                act.wait_ge(padded, 4)
                for v in range(2):
                    nc.scalar.activation(seq_hi[v][:, G, 0:CMP_BLOCK:2], const("pe_v" if v else "pe_k"),
                                         ACT.Copy).then_inc(piece_hi, 1)
                    split_hi(act, U + 5 + v, 0)
                    for m in range(2):
                        act.wait_ge(tiles_done, 2 * (U + 4 + v) + m + 1)
                        for g in range(2):
                            src = ps[2 * v + m][half(g), :]
                            nc.scalar.activation(seq_hi[v][0:64, 2 * m + g, 0:SEQ], src, ACT.Copy).then_inc(piece_hi, 1)
                            nc.scalar.activation(seq_hi[v][64:128, 2 * m + g, 0:SEQ - 1], src[:, 1:SEQ],
                                                 ACT.Copy).then_inc(piece_hi, 1)
                for v in range(2):
                    split_hi(act, U + 7 + v, 0)
                    for m in range(2):
                        act.wait_ge(tiles_done, 2 * (U + 6 + v) + m + 1)
                        for r in range(2):
                            nc.scalar.activation(k_two[v][half(r), 2 * m, :], ps[2 * v + m][half(0), :],
                                                 ACT.Copy).then_inc(out_a, 1)
                for v in range(2):
                    split_hi(act, U + 9 + v, 0)
                    act.wait_ge(tiles_done, 2 * (U + 8 + v) + 1)
                    nc.scalar.activation(v_two[v][:, 0:2, :], ps[2 * v][:], ACT.Copy).then_inc(out_a, 1)
                act.wait_ge(gate_done, 1)
                nc.scalar.activation(gate_t[:], ps[5][0:48, :], ACT.Exp, scale=-1.0).then_inc(gate_exp, 1)

            @block.vector
            def _(dve):
                n_dve(dve)
                with dve.Fori(0, 2) as i:
                    for j in range(2):
                        dve.wait_ge(tiles_done, 2 * (U + j) + 2 + 4 * i)
                        nc.vector.tensor_copy(q_n[:, 4 * i + 2 * j + 1, :], ps[2 * j + 1][:]).then_inc(out_v, 1)
                dve.wait_ge(padded, 4)
                for v in range(2):
                    dve.wait_ge(piece_hi, 9 * v + 1)
                    nc.vector.tensor_tensor(seq_lo[v][:, G, 0:CMP_BLOCK:2], const("pe_v" if v else "pe_k"),
                                            seq_hi[v][:, G, 0:CMP_BLOCK:2].bitcast(F32), ALU.subtract)
                    for m in range(2):
                        dve.wait_ge(piece_hi, 9 * v + 4 * m + 5)
                        for g in range(2):
                            src = ps[2 * v + m][half(g), :]
                            nc.vector.tensor_tensor(seq_lo[v][0:64, 2 * m + g, 0:SEQ], src,
                                                    seq_hi[v][0:64, 2 * m + g, 0:SEQ].bitcast(F32),
                                                    ALU.subtract).then_inc(piece_lo, 1)
                            nc.vector.tensor_tensor(seq_lo[v][64:128, 2 * m + g, 0:SEQ - 1], src[:, 1:SEQ],
                                                    seq_hi[v][64:128, 2 * m + g, 0:SEQ - 1].bitcast(F32),
                                                    ALU.subtract).then_inc(piece_lo, 1)
                for v in range(2):
                    for m in range(2):
                        dve.wait_ge(tiles_done, 2 * (U + 6 + v) + m + 1)
                        for r in range(2):
                            nc.vector.tensor_copy(k_two[v][half(r), 2 * m + 1, :], ps[2 * v + m][half(1), :]).then_inc(out_v, 1)
                for v in range(2):
                    dve.wait_ge(tiles_done, 2 * (U + 8 + v) + 2)
                    nc.vector.tensor_copy(v_two[v][:, 2:4, :], ps[2 * v + 1][:]).then_inc(out_v, 1)
                dve.wait_ge(gate_turned, 1)
                nc.vector.tensor_scalar(gates[:].rearrange("p t n -> p (t n)"), ps[6][:, 0:NQT * 48], 1.0, None,
                                        ALU.add).then_inc(gate_step, 1)
                dve.wait_ge(gate_step, 1)
                nc.vector.reciprocal(gates[:], gates[:])

            @block.tensor
            def _(pe):
                keep_busy(ps[5], 4)

                def unit(u, i, *free):
                    pe.wait_ge(lo_ready, U + u + 1 + 2 * i)
                    for s, v in free:
                        pe.wait_ge(s, v)
                    for m in range(2):
                        column_tile(ps[2 * (u % 2) + m][:], (U + u) % 2, m, xh, xl).then_inc(tiles_done, 1)
                first_unit(pe, U, ps[0:2], xh, xl, wait_tile)
                unit(1, 0)
                unit(2, 0, (out_a, 1), (out_v, 1))
                unit(3, 0, (out_a, 2), (out_v, 2))
                unit(4, 0, (out_a, 3), (out_v, 3))
                unit(5, 0, (out_a, 4), (out_v, 4))
                unit(6, 0, (piece_lo, 8))
                unit(7, 0, (piece_lo, 16))
                for v in range(2):
                    u = 8 + v
                    pe.wait_ge(lo_ready, U + u + 1)
                    pe.wait_ge(out_a, 4 + 4 * (v + 1))
                    pe.wait_ge(out_v, 4 + 4 * (v + 1))
                    for tt in range(NQT):
                        tok = slice(tt * P, (tt + 1) * P)
                        acc = ps[2 * v + tt // 2][:, (tt % 2) * 256:(tt % 2) * 256 + 256]
                        for k in range(KT):
                            c = slice(k * 256, (k + 1) * 256)
                            s = (U + u) % 2
                            mm = three_passes(acc, xh[:, k, tok], xl[:, k, tok], whi[:, s, c], wlo[:, s, c],
                                              k == 0, k == KT - 1)
                        if tt % 2:
                            mm.then_inc(tiles_done, 1)
                for k in range(KT):
                    mm = nc.tensor.matmul(ps[5][0:48, :], w_gate[:, k * 48:(k + 1) * 48], xn[:, k, :],
                                          start=k == 0, stop=k == KT - 1)
                mm.then_inc(gate_done, 1)
                pe.wait_ge(gate_exp, 1)
                for tt in range(NQT):
                    tr = nc.tensor.transpose(ps[6][:, tt * 48:(tt + 1) * 48], gate_t[:, tt * P:(tt + 1) * P],
                                             ident[0:48, 0:48])
                tr.then_inc(gate_turned, 1)

    w2_landed = bias_landed = sem("cmp_landed")
    att = ExitStack()
    o_acc = sb(att, "o_acc", [P, NQT, NSA_HEADS * NSA_DIM], side="right")
    with ExitStack() as ph:
        w2 = sb(ph, "w2_sb", [P, 4 * NSA_DIM])
        first = sb(ph, "cmp_first", [P, 4])
        hidden = sb(ph, "cmp_hidden", [P, 4, G * NCMP])
        cmp_bias = sb(ph, "cmp_bias_sb", [P, NQT, NSA_HEADS * NCMP])
        probs = sb(ph, "c_probs", [P, NQT, NSA_HEADS * NCMP])
        stat = sb(ph, "c_stat", [P, NQT, 3, NSA_HEADS])
        turned_sb = sb(ph, "c_turned", [P, 2, SEQ])
        ps = banks(ph, "cmp")
        s_of = (ps[5], ps[6], ps[0], ps[1])
        bias_out, hidden_out, cmp_done, k_out, v_out, zeroed = (
            sem("cmp_bias_out"), sem("cmp_hidden_out"), sem("cmp_done"), sem("cmp_k_out"), sem("cmp_v_out"), sem("cmp_zeroed"))
        names = ("s", "soft", "exp", "sum", "coef", "turned", "copied", "o", "o_out")
        cs = {n: sem("c_" + n) for n in names}
        U, N = UNITS["cmp"][0], G * NCMP

        with nc.Block() as block:
            @block.sync
            def _(sp):
                sp.dma_start(w2[:], w2_in).then_inc(w2_landed, 16)
                sp.dma_start(cmp_bias[:], cmp_bias_in.rearrange("p (t n) -> p t n", t=NQT)).then_inc(bias_landed, 16)
                load_units(sp, "cmp")

            @block.gpsimd
            def _(pool):
                nc.gpsimd.memset(v_cmp[:], 0.0).then_inc(zeroed, 1)
                nc.gpsimd.memset(k_cmp[:], 0.0).then_inc(zeroed, 1)

            @block.tensor
            def _(pe):
                def network(u):
                    v, r = divmod(u, 2)
                    pe.wait_ge(lo_ready, U + u + 1)
                    for m in range(2):
                        for k in range(UK):
                            w_hi, w_lo = unit_block((U + u) % 2, k, m)
                            t0 = 2 * (UK * r + k)
                            cols = slice(t0, t0 + CMP_STRIDE * (NCMP - 1) + 1, CMP_STRIDE)
                            mm = three_passes(ps[2 * v + m][:, 0:N + NCMP], w_hi, w_lo, seq_hi[v][:, :, cols],
                                              seq_lo[v][:, :, cols], r == 0 and k == 0, r == 1 and k == UK - 1)
                        mm.then_inc(tiles_done, 1)

                def turn(qt):
                    pe.wait_ge(cs["exp"], qt + 1)
                    if qt:
                        pe.wait_ge(cs["copied"], qt)
                    for r in range(NSA_HPG):
                        tr = nc.tensor.transpose(ps[7][:, r * P:(r + 1) * P], probs[:, qt, r * P:(r + 1) * P], ident)
                    tr.then_inc(cs["turned"], 1)

                def outputs(qt):
                    pe.wait_ge(cs["copied"], qt + 1)
                    if qt:
                        pe.wait_ge(cs["o_out"], 2 * qt)
                    for r in range(NSA_HPG):
                        mm = nc.tensor.matmul(ps[2 + r // 2][:, (r % 2) * 256:(r % 2) * 256 + 256],
                                              turned_sb[:, qt % 2, r * P:(r + 1) * P], v_cmp[:], start=True, stop=True)
                    mm.then_inc(cs["o"], 1)

                keep_busy(ps[6], 4)
                for u in range(3):
                    network(u)
                pe.wait_ge(w2_landed, 32)
                pe.wait_ge(hidden_out, 2)
                for m in range(2):
                    mm = nc.tensor.matmul(ps[4][0:64, 0:N], w2[:, m * NSA_DIM:(m + 1) * NSA_DIM], hidden[:, m, :],
                                          start=m == 0, stop=m == 1)
                mm.then_inc(cmp_done, 1)
                network(3)
                pe.wait_ge(k_out, 2)
                for qt in range(NQT):
                    for j in range(NSA_HEADS // 2):
                        mm = nc.tensor.matmul(s_of[qt][:, j * 2 * NCMP:(j + 1) * 2 * NCMP], q_n[:, j, qt * P:(qt + 1) * P],
                                              k_cmp[:, 2 * j // NSA_HPG].rearrange("p a n -> p (a n)"), start=True, stop=True)
                    mm.then_inc(cs["s"], 1)
                pe.wait_ge(hidden_out, 4)
                for m in range(2):
                    mm = nc.tensor.matmul(ps[4][:, 256:256 + NSA_DIM], hidden[:, 2 + m, :],
                                          w2[:, (2 + m) * NSA_DIM:(3 + m) * NSA_DIM], start=m == 0, stop=m == 1)
                mm.then_inc(cmp_done, 1)
                turn(0)
                pe.wait_ge(v_out, G)
                for qt in range(NQT):
                    outputs(qt) if qt == NQT - 1 else (turn(qt + 1), outputs(qt))

            @block.scalar
            def _(act):
                def hidden_of(v):
                    for m in range(2):
                        act.wait_ge(tiles_done, 2 * (U + 2 * v + 1) + m + 1)
                        b = first[:, 2 * v + m:2 * v + m + 1]
                        nc.scalar.activation(b, ps[2 * v + m][:, N:N + 1], ACT.Copy).then_inc(bias_out, 1)
                        act.wait_ge(bias_out, 2 * v + m + 1)
                        nc.scalar.activation(hidden[:, 2 * v + m, :], ps[2 * v + m][:, 0:N], ACT.Gelu_apprx_tanh,
                                             bias=b).then_inc(hidden_out, 1)
                act.preload_act_table(ACT.Gelu_apprx_tanh)
                for u in range(3):
                    split_hi(act, U + u + 1, 0)
                hidden_of(0)
                act.wait_ge(zeroed, 2)
                act.wait_ge(cmp_done, 1)
                for a in range(2):
                    nc.scalar.activation(k_cmp[a * 64:(a + 1) * 64, :, a, :], ps[4][0:64, 0:N].rearrange("p (g n) -> p g n", g=G),
                                         ACT.Copy).then_inc(k_out, 1)
                split_hi(act, U + 4, 0)
                hidden_of(1)
                for qt in range(NQT):
                    act.wait_ge(cs["soft"], 3 * qt + 3)
                    nc.scalar.activation(probs[:, qt, :], probs[:, qt, :], ACT.Exp,
                                         scale=float(NSA_DIM ** -0.5)).then_inc(cs["exp"], 1)
                    act.wait_ge(cs["turned"], qt + 1)
                    if qt >= 2:
                        act.wait_ge(cs["o"], qt - 1)
                    nc.scalar.activation(turned_sb[:, qt % 2, :], ps[7][:], ACT.Copy).then_inc(cs["copied"], 1)

            @block.vector
            def _(dve):
                for u in range(4):
                    split_lo(dve, U + u + 1, 0, nc.vector)
                dve.wait_ge(bias_landed, 32)

                def keys3(ap):
                    return ap.rearrange("p (h n) -> p h n", n=NCMP)

                def softmax(qt):
                    dve.wait_ge(cs["s"], qt + 1)
                    nc.vector.tensor_tensor(probs[:, qt, :].rearrange("p (r g n) -> p g r n", g=G, n=NCMP),
                                            s_of[qt][:].rearrange("p (g r n) -> p g r n", g=G, n=NCMP),
                                            cmp_bias[:, qt, :].rearrange("p (g r n) -> p g r n", g=G, n=NCMP),
                                            ALU.add).then_inc(cs["soft"], 1)
                    dve.wait_ge(cs["soft"], 3 * qt + 1)
                    nc.vector.tensor_reduce(stat[:, qt, 0, :], keys3(probs[:, qt, :]), AX.X, ALU.max).then_inc(cs["soft"], 1)
                    dve.wait_ge(cs["soft"], 3 * qt + 2)
                    nc.vector.tensor_tensor(keys3(probs[:, qt, :]), keys3(probs[:, qt, :]),
                                            stat[:, qt, 0, :, None].to_broadcast([P, NSA_HEADS, NCMP]),
                                            ALU.subtract).then_inc(cs["soft"], 1)

                def coefficients(qt):
                    st = stat[:, qt]
                    dve.wait_ge(cs["exp"], qt + 1)
                    nc.vector.tensor_reduce(st[:, 1, :], keys3(probs[:, qt, :]), AX.X, ALU.add).then_inc(cs["sum"], 1)
                    dve.wait_ge(cs["sum"], qt + 1)
                    nc.vector.reciprocal(st[:, 1, :], st[:, 1, :]).then_inc(cs["coef"], 1)
                    dve.wait_ge(cs["coef"], 3 * qt + 1)
                    g0 = gates[:, qt, :].rearrange("p (g r t) -> p r g t", g=G, t=3)[:, :, :, 0]
                    nc.vector.tensor_tensor(st[:, 2, :].rearrange("p (r g) -> p r g", g=G),
                                            st[:, 1, :].rearrange("p (r g) -> p r g", g=G), g0, ALU.mult).then_inc(cs["coef"], 1)
                    dve.wait_ge(cs["coef"], 3 * qt + 2)
                    nc.vector.tensor_scalar(st[:, 2, :], st[:, 2, :], const("any_valid")[:, qt:qt + 1], None,
                                            ALU.mult).then_inc(cs["coef"], 1)

                def output(qt):
                    dve.wait_ge(cs["coef"], 3 * qt + 3)
                    dve.wait_ge(cs["o"], qt + 1)
                    for b in range(2):
                        src = ps[2 + b][:].rearrange("p (r g d) -> p r g d", r=2, g=G)
                        dst = o_acc[:, qt, :].rearrange("p (g r d) -> p r g d", g=G, r=NSA_HPG)[:, 2 * b:2 * b + 2]
                        co = stat[:, qt, 2, :].rearrange("p (b r g) -> p b r g", r=2, g=G)[:, b]
                        nc.vector.tensor_tensor(dst, src, co[:, :, :, None].to_broadcast([P, 2, G, NSA_DIM]),
                                                ALU.mult).then_inc(cs["o_out"], 1)
                softmax(0)
                softmax(1)
                dve.wait_ge(cmp_done, 2)
                for g in range(G):
                    r = slice(g * NCMP, (g + 1) * NCMP)
                    nc.vector.tensor_copy(v_cmp[r, g * NSA_DIM:(g + 1) * NSA_DIM], ps[4][r, 256:256 + NSA_DIM]).then_inc(v_out, 1)
                coefficients(0)
                softmax(2)
                coefficients(1)
                output(0)
                softmax(3)
                output(1)
                coefficients(2)
                output(2)
                coefficients(3)
                output(3)
    cmp_in.close()

    with ExitStack() as ph:
        dist = sb(ph, "dist", [P, 4, SEQ])
        q_parts = sb(ph, "q_parts", [P, NSA_HEADS, SEQ], F32R)
        k_hi = [sb(ph, f"k_hi_{n}", [P, 2, SEQ], F32R) for n in ("sel", "win")]
        k_lo = [sb(ph, f"k_lo_{n}", [P, 2, SEQ], F32R) for n in ("sel", "win")]
        prob, prob_t = sb(ph, "prob_n", [P, NQT, SEQ]), sb(ph, "prob_t_n", [P, 2, SEQ])
        neg_max, row_sum = sb(ph, "neg_max_n", [P, NQT]), sb(ph, "row_sum_n", [P, 2 * NSA_HEADS, NQT])
        coef, part = sb(ph, "coef_n", [P, 2, NQT]), sb(ph, "part_n", [P, 2, NQT, NSA_DIM])
        ps = banks(ph, "nat2")
        coef_ready, part_gated, part_added, dist_ready = sem("n_coef"), sem("n_gated"), sem("n_added"), sem("n_dist")
        q_hi_ready, q_ready, k_ready = sem("n_q_hi"), sem("n_q"), sem("n_k")
        rel, slope = const("rel"), const("slope")

        def own_rows(hd):
            return slice(hd % 2 * 64, hd % 2 * 64 + 64)

        def other_rows(hd):
            return slice(64 - hd % 2 * 64, 128 - hd % 2 * 64)

        def split_keys(dve, g):
            for v in range(2):
                nc.vector.tensor_copy(k_hi[v][:, g % 2, :], k_two[v][:, g, :]).then_inc(k_ready, 1)
                dve.wait_ge(k_ready, 4 * g + 2 * v + 1)
                nc.vector.tensor_tensor(k_lo[v][:, g % 2, :], k_two[v][:, g, :], k_hi[v][:, g % 2, :].bitcast(F32),
                                        ALU.subtract).then_inc(k_ready, 1)

        def query_hi(hd):
            nc.vector.tensor_copy(q_parts[own_rows(hd), hd, :], q_n[own_rows(hd), hd // 2, :]).then_inc(q_hi_ready, 1)

        def before_head(dve, hd):
            if hd + 2 < NSA_HEADS:
                query_hi(hd + 2)
            if hd % NSA_HPG == 2 and hd + 2 < NSA_HEADS:
                split_keys(dve, (hd + 2) // NSA_HPG)
            dve.wait_ge(dist_ready, hd + 1)

        def products(pe, a, qt, w):
            hd, v = divmod(a, 2)
            g = hd // NSA_HPG
            if qt == 0:
                pe.wait_ge(q_ready, hd + 1)
                pe.wait_ge(k_ready, 4 * g + 2 * v + 2)
            q = q_parts[:, hd, qt * P:(qt + 1) * P]
            return [(q, k_hi[v][:, g % 2, 0:w]), (q, k_lo[v][:, g % 2, 0:w])]

        def take(dve, g, br, bank):
            n = 2 * g + br
            if n >= 2:
                dve.wait_ge(sem_of["o_taken_nsa"], n - 1)
            nc.vector.reciprocal(coef[:, n % 2], row_sum[:, n, :]).then_inc(coef_ready, 1)
            dve.wait_ge(coef_ready, n + 1)
            if n >= 2:
                dve.wait_ge(part_added, n - 1)
            own = g // NSA_HPG % 2 * NSA_DIM
            return nc.vector.tensor_tensor(part[:, n % 2], bank[:].rearrange("p (t d) -> p t d", t=NQT)[:, :, own:own + NSA_DIM],
                                           coef[:, n % 2, :, None].to_broadcast([P, NQT, NSA_DIM]), ALU.mult)

        on_act, on_dve, on_pe = attention(
            "nsa", NSA_HEADS, 2, float(NSA_DIM ** -0.5), ps[0:4], ps[4:6], ps[6:8], prob, prob_t, neg_max,
            lambda g, br: row_sum[:, 2 * g + br, :],
            products=products,
            values=lambda a, kt: v_two[a % 2][:, kt, a // 16 * P:(a // 16 + 1) * P],
            bias=lambda g, qt: dist[:, g % 4, (NQT - 1 - qt) * P:SEQ], take=take, before_head=before_head)
        with nc.Block() as block:
            @block.gpsimd
            def _(pool):
                def query_lo(hd):
                    pool.wait_ge(q_hi_ready, hd + 1)
                    if hd == 1:
                        pool.wait_ge(dist_ready, 1)
                    elif hd > 2:
                        pool.wait_ge(part_added, 2 * (hd - 2))
                    elif hd == 2:
                        pool.wait_ge(dist_ready, 2)
                    nc.gpsimd.tensor_tensor(q_parts[other_rows(hd), hd, :], q_n[own_rows(hd), hd // 2, :],
                                            q_parts[own_rows(hd), hd, :].bitcast(F32), ALU.subtract).then_inc(q_ready, 1)
                    pool.wait_ge(q_ready, hd + 1)

                def distances(hd):
                    if hd >= 4:
                        pool.wait_ge(sem_of["biased_nsa"], 2 * NQT * (hd - 3))
                    nc.gpsimd.tensor_scalar(dist[:, hd % 4, :], rel, slope[:, hd:hd + 1], None, ALU.mult).then_inc(dist_ready, 1)

                def add_part(n):
                    pool.wait_ge(sem_of["o_taken_nsa"], n + 1)
                    gate = gates[:, :, 3 * (n // 2) + 1 + n % 2, None].to_broadcast([P, NQT, NSA_DIM])
                    nc.gpsimd.tensor_tensor(part[:, n % 2], part[:, n % 2], gate, ALU.mult).then_inc(part_gated, 1)
                    pool.wait_ge(part_gated, n + 1)
                    if n % 2:
                        pool.wait_ge(part_added, n)
                    cols = slice(n // 2 * NSA_DIM, (n // 2 + 1) * NSA_DIM)
                    nc.gpsimd.tensor_tensor(o_acc[:, :, cols], o_acc[:, :, cols], part[:, n % 2], ALU.add).then_inc(part_added, 1)

                for hd in range(2):
                    query_lo(hd)
                    distances(hd)
                for n in range(2 * NSA_HEADS):
                    if n % 2 == 0 and n // 2 + 2 < NSA_HEADS:
                        query_lo(n // 2 + 2)
                    if n % 2 and n // 2 + 2 < NSA_HEADS:
                        distances(n // 2 + 2)
                    add_part(n)

            @block.scalar
            def _(act):
                on_act(act)

            @block.vector
            def _(dve):
                query_hi(0)
                split_keys(dve, 0)
                query_hi(1)
                on_dve(dve)

            @block.tensor
            def _(pe):
                keep_busy(ps[7], 6)
                on_pe(pe)

    with ExitStack() as tail:
        mix_hi = sb(tail, "mix_hi_od", [P, KT, SEQ], F32R)
        mix_lo = sb(tail, "mix_lo_od", [P, KT, SEQ], F32R)
        project_residual("od_out", mix_hi, mix_lo, o_acc)
    att.close()
    odd.close()

    ffn(1)

    with ExitStack() as ph:
        y = sb(ph, "y", [P, KT, SEQ])
        ps = banks(ph, "fin")
        n_act, n_dve, _, y_before = norm_parts(y, const("g_final"))
        stored = sem("stored")
        with nc.Block() as block:
            @block.vector
            def _(dve):
                n_dve(dve)

            @block.sync
            def _(sp):
                for k in range(KT):
                    sp.wait_ge(norm_sems["xn"], y_before + k + 1)
                    sp.dma_start(out_t[:, k, :], y[:, k, :]).then_inc(stored, 16)
                sp.wait_ge(stored, 16 * KT)
    whole.close()


def _unit(w, cols, k0=0):
    n = min(UK, w.shape[0] // P - k0)
    u = np.zeros((P, UK, UM * P), np.float32)
    u[:, :n] = w[k0 * P:(k0 + n) * P, cols:cols + UM * P].reshape(n, P, UM * P).transpose(1, 0, 2)
    return u.reshape(P, -1)


def _blocks(bs):
    u = np.zeros((P, UK * UM * P), np.float32)
    at = 0
    for b in bs:
        u[:, at:at + b.shape[1]] = b
        at += b.shape[1]
    return u


def _stream(a):
    w = a["ev_w_in"][0]
    zq = Q_RANK + KV_RANK + ROPE
    ba = zq + 4 * GDN_HEADS * GDN_D
    kr = w[:, Q_RANK + KV_RANK:zq]
    small = np.concatenate([w[:, ba:ba + 8], np.zeros((D_MODEL, 56), np.float32), kr,
                            kr[:, ROPE // 2:], kr[:, :ROPE // 2]], axis=1)
    units = [_unit(w, 0), _unit(w, 256), _unit(np.concatenate([w[:, 512:640], small], axis=1), 0)]
    units += [_unit(w, zq + 256 * j) for j in range(8)]
    uq = a["ev_w_uq"][0].reshape(3, P, MLA_HEADS, NOPE + ROPE)
    half = NOPE + ROPE // 2
    uq = np.concatenate([uq, uq[..., half:], uq[..., NOPE:half]], axis=-1)
    for heads in (range(5), range(5, 8)):
        units.append(_blocks([uq[k, :, hd] for hd in heads for k in range(3)]))
    ukv = a["ev_w_ukv"][0].reshape(2, P, MLA_HEADS, NOPE + MLA_V)
    units.append(_blocks([ukv[k, :, 2 * j:2 * j + 2, :NOPE].reshape(P, P) for j in range(4) for k in range(2)]
                         + [ukv[k, :, :, NOPE:].reshape(P, -1) for k in range(2)]))
    units += [_unit(a["ev_w_out"][0], 256 * j) for j in range(4)]

    def ffn(n):
        g, u, d = a["ffn_w_gate"][n], a["ffn_w_up"][n], a["ffn_w_down"][n]
        return [_unit(m, 256 * j) for j in range(FT // 2) for m in (g, u)] + \
               [_unit(d, 256 * j, UK * r) for j in range(KT // 2) for r in range(3)]
    units += ffn(0)
    w = a["od_w_in"][0]
    units += [_unit(w, 256 * j) for j in (0, 1, 2, 3, 4, 5, 6, 8, 7, 9)]
    units += [_unit(a[n][0], 0, UK * r) for n in ("od_w1_k", "od_w1_v") for r in range(2)]
    units += [_unit(a["od_w_out"][0], 256 * j) for j in range(4)]
    units += ffn(1)
    assert len(units) == N_UNITS
    return np.stack(units)


def _consts(a):
    c = np.zeros((P, N_COLS), np.float32)

    def put(name, v):
        s, e = COLS[name]
        c[:, s:e] = v
    i = np.arange(P)
    put("ident", np.eye(P, dtype=np.float32))
    put("utri", (i[:, None] <= i[None, :]).astype(np.float32))
    put("ones", 1.0)
    j_, i_ = i[:, None], i[None, :]
    put("level", np.concatenate([((i_ >> (l + 1) == j_ >> (l + 1)) & ((i_ >> l) % 2 == 1) & ((j_ >> l) % 2 == 0))
                                 for l in range(7)], axis=1).astype(np.float32))
    half = ROPE // 2
    inv = np.float32(10000.0) ** (-np.arange(half, dtype=np.float32) / np.float32(half))
    ang = np.arange(SEQ, dtype=np.float32)[None, :] * inv.astype(np.float32)[:, None]
    rope = np.zeros((P, SEQ), np.float32)
    rope[64:96] = np.concatenate([np.cos(ang)] * 2)
    rope[96:128] = np.concatenate([-np.sin(ang), np.sin(ang)])
    put("rope", rope)
    rel = np.arange(SEQ)[None, :] - (SEQ - P) - i[:, None]
    put("rel", np.where(rel <= 0, rel, NEG).astype(np.float32))
    put("causal", np.where(rel <= 0, 0.0, NEG).astype(np.float32))
    pos = (np.arange(NQT)[None, :] * P + i[:, None]).astype(np.float32)
    put("any_valid", (pos >= CMP_BLOCK - 1).astype(np.float32))
    slopes = (2.0 ** (-8.0 * np.arange(1, NSA_HEADS + 1, dtype=np.float32) / NSA_HEADS)).astype(np.float32)
    scale = np.float32(NSA_DIM ** 0.5)
    put("slope", (slopes * scale)[None, :])
    n = np.arange(NCMP)
    centre = (n * CMP_STRIDE + 0.5 * (CMP_BLOCK - 1)).astype(np.float32)
    valid = (n * CMP_STRIDE + CMP_BLOCK - 1)[None, None, :] <= pos[:, :, None]
    bias = (slopes * scale)[None, None, :, None] * (centre[None, None, None, :] - pos[:, :, None, None])
    bias = np.where(valid[:, :, None, :], bias, NEG).astype(np.float32)
    for name, v in (("g_ev", a["ev_attn_norm"][0]), ("g_od", a["od_attn_norm"][0]), ("g_ffn0", a["ffn_norm"][0]),
                    ("g_ffn1", a["ffn_norm"][1]), ("g_final", a["final_norm"]), ("g_q", a["ev_q_norm"][0]),
                    ("g_kv", a["ev_kv_norm"][0]), ("g_gdn", a["ev_gdn_norm"][0]),
                    ("pe_k", a["od_pe_k"][0].reshape(-1)), ("pe_v", a["od_pe_v"][0].reshape(-1))):
        put(name, v.reshape(-1, P).T)
    put("conv", a["ev_conv_w"][0].reshape(GDN_CONV, 12, P).transpose(2, 1, 0).reshape(P, -1))
    put("a_log", a["ev_a_log"])
    put("dt_bias", a["ev_dt_bias"])
    put("eps", EPS)
    g0 = NSA_HEADS * NSA_DIM + 6 * NSA_GROUPS * NSA_DIM
    put("w_gate", a["od_w_in"][0][:, g0:].reshape(KT, P, 48).transpose(1, 0, 2).reshape(P, -1))
    return c, bias.reshape(P, -1)


def kernel(**inputs):
    import concourse.bacc as bacc
    from concourse.bass_utils import run_bass_kernel_spmd

    a = {k: np.asarray(v) for k, v in inputs.items()}
    consts, cmp_bias = _consts(a)
    arrays = {
        "x_t": np.ascontiguousarray(a["x"][0].T.reshape(KT, P, SEQ).transpose(1, 0, 2)),
        "stream": _stream(a),
        "consts": consts,
        "cmp_bias": cmp_bias,
        "w2": np.ascontiguousarray(np.stack([a["od_w2_k"][0], a["od_w2_v"][0]]).reshape(2, 2, P, NSA_DIM)
                                   .transpose(2, 0, 1, 3).reshape(P, -1)),
    }
    nc = bacc.Bacc("TRN2", target_bir_lowering=False, num_devices=1, dynamic_dma_scratch_size=1024)
    args = [nc.dram_tensor(n, v.shape, mybir.dt.float32, kind="ExternalInput").ap() for n, v in arrays.items()]
    out = nc.dram_tensor("out_t", (P, KT, SEQ), mybir.dt.float32, kind="ExternalOutput").ap()
    build_program(nc, *args, out)
    res = run_bass_kernel_spmd(nc, [arrays], core_ids=[0])
    got = res.results[0]["out_t"]
    return np.ascontiguousarray(got.transpose(1, 0, 2).reshape(D_MODEL, SEQ).T)[None]
```
